# Optimizing a Trainium2 kernel written in Bass

```python
import jax, jax.numpy as jnp
from jax import lax
import numpy as np
import math

D_MODEL = 1024
BATCH = 1
SEQ = 256
DEPTH = 2

N_MIXERS = 2
N_A_LAYERS = (DEPTH + 1) // 2
N_B_LAYERS = DEPTH // 2
EPS = 1e-6

D_FF = ((8 * D_MODEL // 3 + 127) // 128) * 128

A_DK = 128
A_DV = 128
A_HEADS = D_MODEL // A_DK
A_CONV = 4
A_CHUNK = 64

B_HD = 64
B_HEADS = D_MODEL // B_HD
B_KV_HEADS = 4
B_WINDOW = 128
B_BLOCK = 128


def rmsnorm(x, w):
    xf = x.astype(jnp.float32)
    y = xf * lax.rsqrt(jnp.mean(xf * xf, axis=-1, keepdims=True) + EPS) * w.astype(jnp.float32)
    return y.astype(x.dtype)

def l2norm(x):
    xf = x.astype(jnp.float32)
    return xf * lax.rsqrt(jnp.sum(xf * xf, axis=-1, keepdims=True) + EPS)

def swiglu(h, w_gu, w_down):
    gate, up = jnp.split(h @ w_gu, 2, axis=-1)
    return (jax.nn.silu(gate) * up) @ w_down

def causal_depthwise_conv(x, w):
    C = x.shape[-1]
    return lax.conv_general_dilated(
        x, w[:, None, :].astype(x.dtype), window_strides=(1,), padding=[(A_CONV - 1, 0)],
        dimension_numbers=("NWC", "WIO", "NWC"), feature_group_count=C)

def gated_delta_rule_chunked(q, k, v, g, beta):
    Bsz, T, H, DK = q.shape
    DV = v.shape[-1]
    C = A_CHUNK
    N = T // C
    f32 = jnp.float32

    def chunk(t):
        return t.astype(f32).reshape(Bsz, N, C, H, -1).transpose(0, 3, 1, 2, 4)

    q, k, v = chunk(q), chunk(k), chunk(v)
    g = g.astype(f32).reshape(Bsz, N, C, H).transpose(0, 3, 1, 2)
    beta = beta.astype(f32).reshape(Bsz, N, C, H).transpose(0, 3, 1, 2)
    g = jnp.cumsum(g, axis=-1)

    idx = jnp.arange(C)
    lower_incl = idx[:, None] >= idx[None, :]
    strict = idx[:, None] > idx[None, :]
    decay = jnp.exp(jnp.where(lower_incl, g[..., :, None] - g[..., None, :], -jnp.inf))

    kb = k * beta[..., None]
    L = jnp.where(strict, jnp.einsum("bhnid,bhnjd->bhnij", kb, k) * decay, 0.0)
    rhs = jnp.concatenate([v * beta[..., None], kb * jnp.exp(g)[..., None]], axis=-1)
    sol = lax.linalg.triangular_solve(L, rhs, left_side=True, lower=True,
                                      transpose_a=False, conjugate_a=False, unit_diagonal=True)
    u, w = sol[..., :DV], sol[..., DV:]

    a_qk = jnp.einsum("bhnid,bhnjd->bhnij", q, k) * decay
    q_dec = q * jnp.exp(g)[..., None]
    k_dec = k * jnp.exp(g[..., -1:] - g)[..., None]
    g_last = jnp.exp(g[..., -1])

    xs = (jnp.moveaxis(q_dec, 2, 0), jnp.moveaxis(k_dec, 2, 0), jnp.moveaxis(u, 2, 0),
          jnp.moveaxis(w, 2, 0), jnp.moveaxis(a_qk, 2, 0), jnp.moveaxis(g_last, 2, 0))

    def step(S, inp):
        qd, kd, u_c, w_c, a_c, gl = inp
        v_new = u_c - jnp.einsum("bhck,bhkv->bhcv", w_c, S)
        o = jnp.einsum("bhck,bhkv->bhcv", qd, S) + jnp.einsum("bhij,bhjv->bhiv", a_c, v_new)
        S = S * gl[..., None, None] + jnp.einsum("bhck,bhcv->bhkv", kd, v_new)
        return S, o

    S0 = jnp.zeros((Bsz, H, DK, DV), f32)
    _, o = lax.scan(step, S0, xs)
    return o.transpose(1, 0, 3, 2, 4).reshape(Bsz, T, H, DV)

def mixer_gated_deltanet(h, w_in, w_conv, A_log, dt_bias, out_norm, w_out):
    Bsz, T, _ = h.shape
    HK = A_HEADS * A_DK
    HV = A_HEADS * A_DV
    proj = h @ w_in
    qkv = proj[..., :2 * HK + HV]
    z = proj[..., 2 * HK + HV:2 * HK + 2 * HV]
    b = proj[..., 2 * HK + 2 * HV:2 * HK + 2 * HV + A_HEADS]
    a = proj[..., 2 * HK + 2 * HV + A_HEADS:]
    qkv = jax.nn.silu(causal_depthwise_conv(qkv, w_conv))
    q = l2norm(qkv[..., :HK].reshape(Bsz, T, A_HEADS, A_DK)) * (A_DK ** -0.5)
    k = l2norm(qkv[..., HK:2 * HK].reshape(Bsz, T, A_HEADS, A_DK))
    v = qkv[..., 2 * HK:].reshape(Bsz, T, A_HEADS, A_DV)
    beta = jax.nn.sigmoid(b.astype(jnp.float32))
    g = -jnp.exp(A_log.astype(jnp.float32)) * jax.nn.softplus(a.astype(jnp.float32) + dt_bias.astype(jnp.float32))
    o = gated_delta_rule_chunked(q, k, v, g, beta)
    zf = z.reshape(Bsz, T, A_HEADS, A_DV).astype(jnp.float32)
    o = rmsnorm(o, out_norm) * jax.nn.silu(zf)
    return o.reshape(Bsz, T, HV).astype(h.dtype) @ w_out

def mixer_sliding_window_sinks(h, w_in, b_in, sinks, w_out, b_out):
    Bsz, T, _ = h.shape
    G = B_HEADS // B_KV_HEADS
    NB = T // B_BLOCK
    HQ = B_HEADS * B_HD
    HKV = B_KV_HEADS * B_HD
    proj = h @ w_in + b_in
    q = proj[..., :HQ].reshape(Bsz, NB, B_BLOCK, B_KV_HEADS, G, B_HD)
    k = proj[..., HQ:HQ + HKV].reshape(Bsz, NB, B_BLOCK, B_KV_HEADS, B_HD)
    v = proj[..., HQ + HKV:].reshape(Bsz, NB, B_BLOCK, B_KV_HEADS, B_HD)

    def with_prev(t):
        prev = jnp.concatenate([jnp.zeros_like(t[:, :1]), t[:, :-1]], axis=1)
        return jnp.concatenate([prev, t], axis=2)

    kk, vv = with_prev(k), with_prev(v)
    s = jnp.einsum("bnqhgd,bnkhd->bnhgqk", q, kk).astype(jnp.float32) * (B_HD ** -0.5)
    qi = jnp.arange(B_BLOCK)[:, None]
    kj = jnp.arange(2 * B_BLOCK)[None, :]
    rel = qi + B_BLOCK - kj
    band = (rel >= 0) & (rel < B_WINDOW)
    blk = jnp.arange(NB)[:, None, None]
    valid = band[None] & ((blk > 0) | (kj >= B_BLOCK)[None])
    s = jnp.where(valid[None, :, None, None], s, -jnp.inf)
    sink = jnp.broadcast_to(sinks.astype(jnp.float32).reshape(B_KV_HEADS, G)[None, None, :, :, None, None],
                            s.shape[:-1] + (1,))
    p = jax.nn.softmax(jnp.concatenate([s, sink], axis=-1), axis=-1)[..., :-1]
    o = jnp.einsum("bnhgqk,bnkhd->bnqhgd", p.astype(vv.dtype), vv)
    return o.reshape(Bsz, T, HQ) @ w_out + b_out

def first_inputs(seed: int = 0) -> dict:
    key = jax.random.key(seed)
    ks = iter(jax.random.split(key, 32))
    f32 = jnp.float32
    nrm = lambda shape, scale: jax.random.normal(next(ks), shape, f32) * scale
    gain = lambda shape: 1.0 + 0.02 * jax.random.normal(next(ks), shape, f32)
    D = D_MODEL
    a_in_cols = 2 * A_HEADS * A_DK + 2 * A_HEADS * A_DV + 2 * A_HEADS
    b_in_cols = (B_HEADS + 2 * B_KV_HEADS) * B_HD
    dt = jnp.exp(jax.random.uniform(next(ks), (N_A_LAYERS, A_HEADS), f32, np.log(1e-3), np.log(1e-1)))
    return {
        "x": jax.random.normal(next(ks), (BATCH, SEQ, D), f32),
        "ffn1_norm": gain((DEPTH, D)),
        "ffn1_w_gu": nrm((DEPTH, D, 2 * D_FF), D ** -0.5),
        "ffn1_w_down": nrm((DEPTH, D_FF, D), D_FF ** -0.5),
        "mix_norm": gain((DEPTH, D)),
        "ffn2_norm": gain((DEPTH, D)),
        "ffn2_w_gu": nrm((DEPTH, D, 2 * D_FF), D ** -0.5),
        "ffn2_w_down": nrm((DEPTH, D_FF, D), D_FF ** -0.5),
        "a_w_in": nrm((N_A_LAYERS, D, a_in_cols), D ** -0.5),
        "a_w_conv": nrm((N_A_LAYERS, A_CONV, 2 * A_HEADS * A_DK + A_HEADS * A_DV), A_CONV ** -0.5),
        "a_A_log": jnp.log(jax.random.uniform(next(ks), (N_A_LAYERS, A_HEADS), f32, 1.0, 16.0)),
        "a_dt_bias": dt + jnp.log(-jnp.expm1(-dt)),
        "a_out_norm": gain((N_A_LAYERS, A_DV)),
        "a_w_out": nrm((N_A_LAYERS, A_HEADS * A_DV, D), (A_HEADS * A_DV) ** -0.5),
        "b_w_in": nrm((N_B_LAYERS, D, b_in_cols), D ** -0.5),
        "b_b_in": nrm((N_B_LAYERS, b_in_cols), 0.02),
        "b_sinks": nrm((N_B_LAYERS, B_HEADS), 1.0),
        "b_w_out": nrm((N_B_LAYERS, B_HEADS * B_HD, D), (B_HEADS * B_HD) ** -0.5),
        "b_b_out": nrm((N_B_LAYERS, D), 0.02),
        "final_norm": gain((D,)),
    }

def first_block(x, ffn1_norm, ffn1_w_gu, ffn1_w_down, mix_norm, ffn2_norm, ffn2_w_gu, ffn2_w_down,
              a_w_in, a_w_conv, a_A_log, a_dt_bias, a_out_norm, a_w_out,
              b_w_in, b_b_in, b_sinks, b_w_out, b_b_out, final_norm):
    for layer in range(DEPTH):
        x = x + 0.5 * swiglu(rmsnorm(x, ffn1_norm[layer]), ffn1_w_gu[layer], ffn1_w_down[layer])
        h = rmsnorm(x, mix_norm[layer])
        j = layer // N_MIXERS
        if layer % N_MIXERS == 0:
            y = mixer_gated_deltanet(h, a_w_in[j], a_w_conv[j], a_A_log[j], a_dt_bias[j],
                                     a_out_norm[j], a_w_out[j])
        else:
            y = mixer_sliding_window_sinks(h, b_w_in[j], b_b_in[j], b_sinks[j], b_w_out[j], b_b_out[j])
        x = x + y
        x = x + 0.5 * swiglu(rmsnorm(x, ffn2_norm[layer]), ffn2_w_gu[layer], ffn2_w_down[layer])
    return rmsnorm(x, final_norm)


N_NSA_LAYERS = (DEPTH + N_MIXERS - 1) // N_MIXERS
N_SSD_LAYERS = DEPTH // N_MIXERS

NSA_HEADS = 16
NSA_HEAD_DIM = 64
NSA_KV_GROUPS = 4
NSA_HEADS_PER_GROUP = NSA_HEADS // NSA_KV_GROUPS
COMP_BLOCK = 32
COMP_STRIDE = 16
COMP_HIDDEN = 256
SEL_BLOCK = 64
N_SELECT = 16
N_LOCAL_BLOCKS = 2
WINDOW = 512
N_BRANCHES = 3
WIN_Q_BLOCK = 128
SEL_Q_BLOCK = 16
NSA_Q_DIM = NSA_HEADS * NSA_HEAD_DIM
NSA_KV_DIM = NSA_KV_GROUPS * NSA_HEAD_DIM
NSA_PROJ_DIM = NSA_Q_DIM + 2 * N_BRANCHES * NSA_KV_DIM + NSA_HEADS * N_BRANCHES

SSD_EXPAND = 2
SSD_D_INNER = SSD_EXPAND * D_MODEL
SSD_HEAD_DIM = 64
SSD_HEADS = SSD_D_INNER // SSD_HEAD_DIM
SSD_GROUPS = 4
SSD_STATE = 128
SSD_CONV = 4
SSD_CHUNK = 128
SSD_CONV_DIM = SSD_D_INNER + 2 * SSD_GROUPS * SSD_STATE
SSD_PROJ_DIM = SSD_D_INNER + SSD_CONV_DIM + SSD_HEADS

FFN_HIDDEN = 2816
FFN_CONV = 3

RMS_EPS = 1e-6
NEG_INF = -1e30
SEL_FORCE = 1e9


def rms_norm(x, gain):
    xf = x.astype(jnp.float32)
    y = xf * lax.rsqrt(jnp.mean(xf * xf, axis=-1, keepdims=True) + RMS_EPS)
    return (y * gain.astype(jnp.float32)).astype(x.dtype)

def causal_dwconv(x, w, b):
    width, ch = w.shape
    y = lax.conv_general_dilated(
        x, w.astype(x.dtype)[:, None, :], window_strides=(1,),
        padding=[(width - 1, 0)], dimension_numbers=("NWC", "WIO", "NWC"),
        feature_group_count=ch)
    return y + b.astype(x.dtype)

def masked_softmax(scores, mask):
    return jax.nn.softmax(jnp.where(mask, scores, NEG_INF), axis=-1)

def compress_tokens(t, pos, w1, w2):
    b, s, g, d = t.shape
    nc = (s - COMP_BLOCK) // COMP_STRIDE + 1
    idx = np.arange(nc)[:, None] * COMP_STRIDE + np.arange(COMP_BLOCK)[None, :]
    blocks = t[:, idx] + pos.astype(t.dtype)[None, None, :, None, :]
    flat = blocks.transpose(0, 1, 3, 2, 4).reshape(b, nc, g, COMP_BLOCK * d)
    return jax.nn.gelu(flat @ w1) @ w2

def cmp_to_sel_overlap(nc, nsb):
    cs = np.arange(nc) * COMP_STRIDE
    ss = np.arange(nsb) * SEL_BLOCK
    ov = (np.minimum(cs[:, None] + COMP_BLOCK, ss[None, :] + SEL_BLOCK)
          - np.maximum(cs[:, None], ss[None, :]))
    return np.clip(ov, 0, None).astype(np.float32) / COMP_BLOCK

def nsa_mixer(h, w_in, cmp_pos, cmp_w1, cmp_w2, w_out):
    b, s, _ = h.shape
    g, hpg, hd = NSA_KV_GROUPS, NSA_HEADS_PER_GROUP, NSA_HEAD_DIM
    scale = hd ** -0.5
    kv_end = NSA_Q_DIM + 2 * N_BRANCHES * NSA_KV_DIM
    proj = h @ w_in
    q = proj[..., :NSA_Q_DIM].reshape(b, s, g, hpg, hd)
    kv = proj[..., NSA_Q_DIM:kv_end].reshape(b, s, 2 * N_BRANCHES, g, hd)
    gates = jax.nn.sigmoid(proj[..., kv_end:].astype(jnp.float32)).reshape(b, s, g, hpg, N_BRANCHES)
    k_cmp, v_cmp = kv[:, :, 0], kv[:, :, 1]
    k_sel, v_sel = kv[:, :, 2], kv[:, :, 3]
    k_win, v_win = kv[:, :, 4], kv[:, :, 5]
    pos = np.arange(s)

    kc = compress_tokens(k_cmp, cmp_pos[0], cmp_w1[0], cmp_w2[0])
    vc = compress_tokens(v_cmp, cmp_pos[1], cmp_w1[1], cmp_w2[1])
    nc = kc.shape[1]
    cmp_mask = (np.arange(nc)[None, :] * COMP_STRIDE + COMP_BLOCK - 1) <= pos[:, None]
    sc = jnp.einsum("bsghd,bcgd->bghsc", q, kc).astype(jnp.float32) * scale
    p_cmp = jnp.where(cmp_mask, masked_softmax(sc, cmp_mask), 0.0)
    o_cmp = jnp.einsum("bghsc,bcgd->bsghd", p_cmp.astype(vc.dtype), vc)

    nsb = s // SEL_BLOCK
    p_slc = jnp.einsum("bgsc,cj->bgsj", p_cmp.sum(axis=2),
                       jnp.asarray(cmp_to_sel_overlap(nc, nsb)))
    blk = np.arange(nsb)[None, :]
    cur = (pos // SEL_BLOCK)[:, None]
    allowed = blk * SEL_BLOCK <= pos[:, None]
    forced = (blk == 0) | ((blk <= cur) & (blk > cur - N_LOCAL_BLOCKS))
    sel_score = jnp.where(forced, SEL_FORCE, jnp.where(allowed, p_slc, NEG_INF))
    n_sel = min(N_SELECT, nsb)
    _, sel_idx = lax.top_k(sel_score, n_sel)
    ks_blocks = k_sel.reshape(b, nsb, SEL_BLOCK, g, hd).transpose(0, 3, 1, 2, 4).reshape(b, g, nsb, SEL_BLOCK * hd)
    vs_blocks = v_sel.reshape(b, nsb, SEL_BLOCK, g, hd).transpose(0, 3, 1, 2, 4).reshape(b, g, nsb, SEL_BLOCK * hd)
    n_qc = s // SEL_Q_BLOCK
    q_ch = q.reshape(b, n_qc, SEL_Q_BLOCK, g, hpg, hd).transpose(1, 0, 3, 4, 2, 5)
    idx_ch = sel_idx.reshape(b, g, n_qc, SEL_Q_BLOCK, n_sel).transpose(2, 0, 1, 3, 4)
    pos_ch = jnp.arange(s).reshape(n_qc, SEL_Q_BLOCK)
    n_keys = n_sel * SEL_BLOCK

    def sel_chunk(args):
        qc, ic, pc = args
        flat_idx = ic.reshape(b, g, SEL_Q_BLOCK * n_sel)[..., None]
        kg = jnp.take_along_axis(ks_blocks, flat_idx, axis=2).reshape(b, g, SEL_Q_BLOCK, n_keys, hd)
        vg = jnp.take_along_axis(vs_blocks, flat_idx, axis=2).reshape(b, g, SEL_Q_BLOCK, n_keys, hd)
        kpos = (ic[..., None] * SEL_BLOCK + jnp.arange(SEL_BLOCK)).reshape(b, g, SEL_Q_BLOCK, n_keys)
        mask = (kpos <= pc[None, None, :, None])[:, :, None]
        scs = jnp.einsum("bghqd,bgqkd->bghqk", qc, kg).astype(jnp.float32) * scale
        p = masked_softmax(scs, mask)
        return jnp.einsum("bghqk,bgqkd->bghqd", p.astype(vg.dtype), vg)

    o_sel = lax.map(sel_chunk, (q_ch, idx_ch, pos_ch)).transpose(1, 0, 4, 2, 3, 5).reshape(b, s, g, hpg, hd)

    n_wb = s // WIN_Q_BLOCK
    span = WIN_Q_BLOCK + WINDOW
    kp = jnp.pad(k_win, ((0, 0), (WINDOW, 0), (0, 0), (0, 0)))
    vp = jnp.pad(v_win, ((0, 0), (WINDOW, 0), (0, 0), (0, 0)))
    q_wb = q.reshape(b, n_wb, WIN_Q_BLOCK, g, hpg, hd).transpose(1, 0, 3, 4, 2, 5)

    def win_block(args):
        qb, i = args
        start = i * WIN_Q_BLOCK
        kb = lax.dynamic_slice_in_dim(kp, start, span, axis=1)
        vb = lax.dynamic_slice_in_dim(vp, start, span, axis=1)
        qpos = start + jnp.arange(WIN_Q_BLOCK)
        kpos = start - WINDOW + jnp.arange(span)
        mask = ((kpos[None, :] >= 0) & (kpos[None, :] <= qpos[:, None])
                & (kpos[None, :] > qpos[:, None] - WINDOW))
        scs = jnp.einsum("bghqd,bkgd->bghqk", qb, kb).astype(jnp.float32) * scale
        p = masked_softmax(scs, mask)
        return jnp.einsum("bghqk,bkgd->bghqd", p.astype(vb.dtype), vb)

    o_win = lax.map(win_block, (q_wb, jnp.arange(n_wb))).transpose(1, 0, 4, 2, 3, 5).reshape(b, s, g, hpg, hd)

    o = (gates[..., 0:1] * o_cmp + gates[..., 1:2] * o_sel + gates[..., 2:3] * o_win).astype(h.dtype)
    return o.reshape(b, s, NSA_Q_DIM) @ w_out

def ssd_scan(x, dt, a, bm, cm):
    b, s, nh, p = x.shape
    g, n = bm.shape[2], bm.shape[3]
    hg = nh // g
    L = SSD_CHUNK
    nc = s // L
    xc = x.reshape(b, nc, L, g, hg, p).transpose(1, 0, 2, 3, 4, 5)
    dtc = dt.reshape(b, nc, L, g, hg).transpose(1, 0, 2, 3, 4)
    bc = bm.reshape(b, nc, L, g, n).transpose(1, 0, 2, 3, 4)
    cc = cm.reshape(b, nc, L, g, n).transpose(1, 0, 2, 3, 4)
    a_g = a.reshape(g, hg)
    causal = np.tril(np.ones((L, L), dtype=bool))[None, :, :, None, None]

    def step(state, inp):
        x_k, dt_k, b_k, c_k = inp
        acs = jnp.cumsum(dt_k * a_g, axis=1)
        seg = acs[:, :, None] - acs[:, None, :]
        lmat = jnp.exp(jnp.where(causal, seg, -jnp.inf))
        cb = jnp.einsum("blgn,bsgn->blsg", c_k, b_k)
        w = cb[..., None] * lmat * dt_k[:, None]
        y = jnp.einsum("blsgh,bsghp->blghp", w, x_k)
        y = y + jnp.einsum("blgn,bghpn->blghp", c_k, state) * jnp.exp(acs)[..., None]
        decay = jnp.exp(acs[:, -1:] - acs) * dt_k
        state = (state * jnp.exp(acs[:, -1])[..., None, None]
                 + jnp.einsum("bsgn,bsgh,bsghp->bghpn", b_k, decay, x_k))
        return state, y

    state0 = jnp.zeros((b, g, hg, p, n), jnp.float32)
    _, ys = lax.scan(step, state0, (xc, dtc, bc, cc))
    return ys.transpose(1, 0, 2, 3, 4, 5).reshape(b, s, nh, p)

def ssd_mixer(h, w_in, conv_w, conv_b, dt_bias, a_log, d_skip, norm_w, w_out):
    b, s, _ = h.shape
    f32 = jnp.float32
    gn = SSD_GROUPS * SSD_STATE
    proj = h @ w_in
    z = proj[..., :SSD_D_INNER]
    xbc = jax.nn.silu(causal_dwconv(proj[..., SSD_D_INNER:SSD_D_INNER + SSD_CONV_DIM], conv_w, conv_b))
    dt_raw = proj[..., SSD_D_INNER + SSD_CONV_DIM:]
    x_ssm = xbc[..., :SSD_D_INNER].astype(f32).reshape(b, s, SSD_HEADS, SSD_HEAD_DIM)
    bm = xbc[..., SSD_D_INNER:SSD_D_INNER + gn].astype(f32).reshape(b, s, SSD_GROUPS, SSD_STATE)
    cm = xbc[..., SSD_D_INNER + gn:].astype(f32).reshape(b, s, SSD_GROUPS, SSD_STATE)
    dt = jax.nn.softplus(dt_raw.astype(f32) + dt_bias.astype(f32))
    a = -jnp.exp(a_log.astype(f32))
    y = ssd_scan(x_ssm, dt, a, bm, cm) + d_skip.astype(f32)[:, None] * x_ssm
    y = y.reshape(b, s, SSD_D_INNER) * jax.nn.silu(z.astype(f32))
    yg = y.reshape(b, s, SSD_GROUPS, SSD_D_INNER // SSD_GROUPS)
    yg = yg * lax.rsqrt(jnp.mean(yg * yg, axis=-1, keepdims=True) + RMS_EPS)
    y = (yg.reshape(b, s, SSD_D_INNER) * norm_w.astype(f32)).astype(h.dtype)
    return y @ w_out

def conv_ffn(h, w_up, conv_w, conv_b, w_down):
    u = causal_dwconv(h @ w_up, conv_w, conv_b)
    val, gate = u[..., :FFN_HIDDEN], u[..., FFN_HIDDEN:]
    return (jax.nn.silu(gate) * val) @ w_down

def second_inputs(seed: int = 0) -> dict:
    key = jax.random.key(seed)
    ks = jax.random.split(key, 19)
    f32 = jnp.float32

    def dense(k, shape, fan_in):
        return jax.random.normal(k, shape, f32) * fan_in ** -0.5

    x = jax.random.normal(ks[0], (BATCH, SEQ, D_MODEL), f32)
    norm_gains = 1.0 + 0.05 * jax.random.normal(ks[1], (DEPTH, 4, D_MODEL), f32)
    nsa_w_in = dense(ks[2], (N_NSA_LAYERS, D_MODEL, NSA_PROJ_DIM), D_MODEL)
    nsa_cmp_pos = 0.1 * jax.random.normal(ks[3], (N_NSA_LAYERS, 2, COMP_BLOCK, NSA_HEAD_DIM), f32)
    nsa_cmp_w1 = dense(ks[4], (N_NSA_LAYERS, 2, COMP_BLOCK * NSA_HEAD_DIM, COMP_HIDDEN), COMP_BLOCK * NSA_HEAD_DIM)
    nsa_cmp_w2 = dense(ks[5], (N_NSA_LAYERS, 2, COMP_HIDDEN, NSA_HEAD_DIM), COMP_HIDDEN)
    nsa_w_out = dense(ks[6], (N_NSA_LAYERS, NSA_Q_DIM, D_MODEL), NSA_Q_DIM)
    ssd_w_in = dense(ks[7], (N_SSD_LAYERS, D_MODEL, SSD_PROJ_DIM), D_MODEL)
    ssd_conv_w = dense(ks[8], (N_SSD_LAYERS, SSD_CONV, SSD_CONV_DIM), SSD_CONV)
    ssd_conv_b = 0.02 * jax.random.normal(ks[9], (N_SSD_LAYERS, SSD_CONV_DIM), f32)
    dt0 = jnp.exp(jax.random.uniform(ks[10], (N_SSD_LAYERS, SSD_HEADS), f32,
                                     minval=math.log(1e-3), maxval=math.log(1e-1)))
    ssd_dt_bias = dt0 + jnp.log(-jnp.expm1(-dt0))
    ssd_a_log = jnp.log(jax.random.uniform(ks[11], (N_SSD_LAYERS, SSD_HEADS), f32, minval=1.0, maxval=16.0))
    ssd_d = 1.0 + 0.05 * jax.random.normal(ks[12], (N_SSD_LAYERS, SSD_HEADS), f32)
    ssd_norm_w = 1.0 + 0.05 * jax.random.normal(ks[13], (N_SSD_LAYERS, SSD_D_INNER), f32)
    ssd_w_out = dense(ks[14], (N_SSD_LAYERS, SSD_D_INNER, D_MODEL), SSD_D_INNER)
    ffn_w_up = dense(ks[15], (DEPTH, D_MODEL, 2 * FFN_HIDDEN), D_MODEL)
    ffn_conv_w = dense(ks[16], (DEPTH, FFN_CONV, 2 * FFN_HIDDEN), FFN_CONV)
    ffn_conv_b = 0.02 * jax.random.normal(ks[17], (DEPTH, 2 * FFN_HIDDEN), f32)
    ffn_w_down = dense(ks[18], (DEPTH, FFN_HIDDEN, D_MODEL), FFN_HIDDEN)
    return {
        "x": x, "norm_gains": norm_gains,
        "nsa_w_in": nsa_w_in, "nsa_cmp_pos": nsa_cmp_pos, "nsa_cmp_w1": nsa_cmp_w1,
        "nsa_cmp_w2": nsa_cmp_w2, "nsa_w_out": nsa_w_out,
        "ssd_w_in": ssd_w_in, "ssd_conv_w": ssd_conv_w, "ssd_conv_b": ssd_conv_b,
        "ssd_dt_bias": ssd_dt_bias, "ssd_a_log": ssd_a_log, "ssd_d": ssd_d,
        "ssd_norm_w": ssd_norm_w, "ssd_w_out": ssd_w_out,
        "ffn_w_up": ffn_w_up, "ffn_conv_w": ffn_conv_w, "ffn_conv_b": ffn_conv_b,
        "ffn_w_down": ffn_w_down,
    }

def second_block(x, norm_gains, nsa_w_in, nsa_cmp_pos, nsa_cmp_w1, nsa_cmp_w2, nsa_w_out,
              ssd_w_in, ssd_conv_w, ssd_conv_b, ssd_dt_bias, ssd_a_log, ssd_d, ssd_norm_w,
              ssd_w_out, ffn_w_up, ffn_conv_w, ffn_conv_b, ffn_w_down):
    h = x
    for i in range(DEPTH):
        gains = norm_gains[i]
        slot = i // N_MIXERS
        hn = rms_norm(h, gains[0])
        if i % N_MIXERS == 0:
            m = nsa_mixer(hn, nsa_w_in[slot], nsa_cmp_pos[slot], nsa_cmp_w1[slot],
                          nsa_cmp_w2[slot], nsa_w_out[slot])
        else:
            m = ssd_mixer(hn, ssd_w_in[slot], ssd_conv_w[slot], ssd_conv_b[slot],
                          ssd_dt_bias[slot], ssd_a_log[slot], ssd_d[slot],
                          ssd_norm_w[slot], ssd_w_out[slot])
        h = h + rms_norm(m, gains[1])
        f = conv_ffn(rms_norm(h, gains[2]), ffn_w_up[i], ffn_conv_w[i], ffn_conv_b[i], ffn_w_down[i])
        h = h + rms_norm(f, gains[3])
    return h


def setup_inputs(seed=0):
    out = dict(first_inputs(seed))
    for name, value in second_inputs(seed + 1).items():
        if name != "x":
            out[name + "_2"] = value
    return out


def reference(
    x, ffn1_norm, ffn1_w_gu, ffn1_w_down, mix_norm, ffn2_norm, ffn2_w_gu, ffn2_w_down, a_w_in,
    a_w_conv, a_A_log, a_dt_bias, a_out_norm, a_w_out, b_w_in, b_b_in, b_sinks, b_w_out,
    b_b_out, final_norm, norm_gains_2, nsa_w_in_2, nsa_cmp_pos_2, nsa_cmp_w1_2, nsa_cmp_w2_2,
    nsa_w_out_2, ssd_w_in_2, ssd_conv_w_2, ssd_conv_b_2, ssd_dt_bias_2, ssd_a_log_2, ssd_d_2,
    ssd_norm_w_2, ssd_w_out_2, ffn_w_up_2, ffn_conv_w_2, ffn_conv_b_2, ffn_w_down_2,
):
    x = first_block(
        x, ffn1_norm, ffn1_w_gu, ffn1_w_down, mix_norm, ffn2_norm, ffn2_w_gu, ffn2_w_down,
        a_w_in, a_w_conv, a_A_log, a_dt_bias, a_out_norm, a_w_out, b_w_in, b_b_in, b_sinks,
        b_w_out, b_b_out, final_norm,
    )
    return second_block(
        x, norm_gains_2, nsa_w_in_2, nsa_cmp_pos_2, nsa_cmp_w1_2, nsa_cmp_w2_2, nsa_w_out_2,
        ssd_w_in_2, ssd_conv_w_2, ssd_conv_b_2, ssd_dt_bias_2, ssd_a_log_2, ssd_d_2,
        ssd_norm_w_2, ssd_w_out_2, ffn_w_up_2, ffn_conv_w_2, ffn_conv_b_2, ffn_w_down_2,
    )


_drawn_inputs = setup_inputs


def setup_inputs(seed=0):
    import zlib

    import numpy as np

    out = dict(_drawn_inputs(seed))
    spreads = {}
    factors = {'ffn2_norm': 3.561,
     'a_out_norm': 3.319,
     'ssd_conv_b_2': 4.279,
     'ssd_d_2': 3.173,
     'b_b_in': 4.246,
     'b_sinks': 3.164,
     'b_b_out': 4.367}
    for name, (base, spread) in spreads.items():
        noise = np.random.default_rng([zlib.crc32(name.encode()), seed]).standard_normal(out[name].shape)
        drawn = base * np.exp(spread * noise) if base else spread * noise
        out[name] = __import__('jax').numpy.asarray(drawn.astype(out[name].dtype))
    for name, factor in factors.items():
        out[name] = (out[name] * factor).astype(out[name].dtype)
    return out
```

```python
from contextlib import ExitStack, contextmanager

import numpy as np

import concourse.bass as bass
from concourse import mybir

ACT = mybir.ActivationFunctionType
ALU = mybir.AluOpType
AX = mybir.AxisListType
F32 = mybir.dt.float32
F32R = mybir.dt.float32r

P = 128
T = 256
NT = T // P
D = 1024
KD = D // P
FF = 2816
FK = FF // P
UNIT = 4096
SLOTS = 3
QUARTER = UNIT // 4
ROUNDED = 6
BANK = 512
ARENA = 19968
EPS = 1e-6
MASKED = -1e30

HEADS_A = 8
GROUPS = 4
HD = 64
NC = 15
SSD_HEADS = 32
LEVELS = 7

CHUNKS = {"swiglu": 11, "gdn": 8, "swa": 3, "nsa": 5, "cffn": 11, "ssd": 10}
EXTRA = {"nsa": 2}
DOWN = {"swiglu": 22, "gdn": 8, "swa": 8, "nsa": 8, "cffn": 22, "ssd": 16}
PLAN = [("swiglu", 0), ("gdn", 0), ("swiglu", 1), ("swiglu", 2), ("swa", 0), ("swiglu", 3),
        ("nsa", 0), ("cffn", 0), ("ssd", 0), ("cffn", 1)]
FINAL_AFTER = 5

CONST = [("ident", P), ("norms", 10 * KD), ("ones", P), ("upper", P), ("heads", 96),
         ("gdn_conv", 24 * 5), ("gdn_gain", 1), ("w_ba", KD * 16), ("levels", LEVELS * P),
         ("swa_bias", 12), ("window", 2 * P), ("causal", 2 * P), ("cmp_keep", NT * 16),
         ("w_gates", KD * 48), ("pos", 2 * 16), ("w_cmp2", 2 * 2 * P),
         ("conv0", 44 * 4), ("conv1", 44 * 4), ("ssd_conv", 24 * 5), ("w_dt", KD * 32),
         ("ssd_gain", 16), ("ssd_skip", 16)]
CONST_AT, CONST_N = {}, 0
for _name, _width in CONST:
    CONST_AT[_name] = CONST_N
    CONST_N += _width
HEAD_AT = {"a_log": 0, "a_dt": 8, "sinks": 16, "ssd_dt": 32, "ssd_a": 64}
ROWS = {("swa", 0): 0, "final": 1, ("nsa", 0): 2, ("cffn", 0): 3, ("ssd", 0): 4, ("cffn", 1): 5}


class Tally:

    def __init__(self, sem):
        self.sem, self.at, self.turns = sem, 0, 0

    def up(self, instruction, n=1):
        instruction.then_inc(self.sem, n)
        self.at += n
        return instruction

    def value(self):
        return self.at + self.turns

    def wait(self, engine):
        engine.wait_ge(self.sem, self.value())


@contextmanager
def rounds(engine, n, *raised):
    began = [t.at for t, _ in raised]
    with engine.Fori(0, n) as i:
        for t, per in raised:
            t.turns = i * per
        yield i
        for (t, per), at in zip(raised, began):
            assert t.at - at == per, (t.at - at, per)
    for (t, per), at in zip(raised, began):
        t.turns, t.at = 0, at + n * per


class Stage:
    pass


class Quarter:

    def __init__(self, unit, q, place, early, count):
        self.unit, self.q, self.place, self.early, self.count = unit, q, place, early, count


def lay_out_quarters(stages):
    quarters = {}
    for g in stages:
        for unit, place, n, early in ((g.unit, g.split, 4 * g.chunks, g.own_ring),
                                      (g.down, g.split_down, g.k_tiles, False)):
            for q in range(n):
                quarters[place + q] = Quarter(unit + q // 4, q % 4, place + q, early, len(quarters) + 1)
    return quarters


def lay_out(plan):
    stages, unit, chunk, gated, hidden, split, rest = [], 0, 0, 0, 0, 0, 0
    for s, (kind, nth) in enumerate(plan):
        g = Stage()
        g.kind, g.nth, g.s = kind, nth, s
        g.chunks, g.k_tiles = CHUNKS[kind], DOWN[kind]
        g.norm = PLAN.index((kind, nth))
        g.unit, g.chunk, g.gated, g.hidden = unit, chunk, gated, hidden
        g.extra = g.unit + g.chunks
        g.down = g.extra + EXTRA.get(kind, 0)
        g.down_units = -(-g.k_tiles // 4)
        g.split = split
        g.split_down = split + 4 * g.chunks
        split = g.split_down + 4 * g.down_units
        g.rest = rest
        rest += g.k_tiles // 2
        g.own_ring = kind not in ("swiglu", "cffn")
        unit = g.down + g.down_units
        chunk += g.chunks
        gated += g.chunks if kind in ("swiglu", "cffn") else 0
        hidden += g.chunks if kind == "cffn" else 0
        stages.append(g)
    return stages, unit


def build_program(nc, units, consts, rows, x_in, out, plan):
    stages, n_units = lay_out(plan)
    quarters = lay_out_quarters(stages)
    last_stage = len(stages) - 1

    events, changes = [], []
    for g in stages:
        mine = [("residual", g.s)] + [("final", g.s)] * (g.norm == FINAL_AFTER)
        events += mine
        changes += [(event, t) for t in range(NT) for event in mine]
    x_after = {change: n + 1 for n, change in enumerate(changes)}
    deviations = [("norm", 0, t) for t in range(NT)]
    for g in stages:
        for t in range(NT):
            if g.kind in ("nsa", "cffn", "ssd"):
                deviations.append(("post", g.s, t))
            if g.norm == FINAL_AFTER:
                deviations.append(("final", g.s, t))
            if g.s < last_stage:
                deviations.append(("norm", g.s + 1, t))
    deviation_at = {key: n + 1 for n, key in enumerate(deviations)}

    def x_event_before_norm(s, t):
        if s == 0:
            return 0
        event = ("final", s - 1) if stages[s - 1].norm == FINAL_AFTER else ("residual", s - 1)
        return x_after[event, t]

    row_uses = []
    for g in stages:
        if (g.kind, g.nth) in ROWS:
            row_uses.append((ROWS[g.kind, g.nth], ("residual", g.s)))
        if g.norm == FINAL_AFTER:
            row_uses.append((ROWS["final"], ("final", g.s)))
    row_at = {event: n for n, (_, event) in enumerate(row_uses)}

    with ExitStack() as ctx:
        def place(name, at, *shape):
            with ExitStack() as below:
                if at:
                    below.enter_context(nc.sbuf_tensor("below_" + name, [P, at], F32))
                return below.enter_context(nc.sbuf_tensor(name, [P, *shape], F32))

        def sem(name):
            return ctx.enter_context(nc.semaphore(name))

        at = {}
        end = 0
        for name, size in (("ring", SLOTS * UNIT), ("x", NT * D), ("xn", NT * D), ("xT", KD * T),
                           ("xT_rest", KD * T), ("hT", ROUNDED * QUARTER), ("cst", CONST_N), ("row", 2 * D),
                           ("stats", 64), ("arena", ARENA)):
            at[name] = end
            end += size
        ring = place("ring", at["ring"], SLOTS, UNIT)
        ring_rest = place("ring_rest", at["ring"], SLOTS, UNIT)
        x = place("x", at["x"], NT, D)
        xn = place("xn", at["xn"], NT, D)
        xT = place("xT", at["xT"], KD, T)
        xT_rest = place("xT_rest", at["xT_rest"], KD, T)
        spare = place("spare", at["xT"], KD, T)
        junk = place("junk", at["xT_rest"], D)
        hT = place("hT", at["hT"], ROUNDED * QUARTER // T, T)
        hT_rest = place("hT_rest", at["hT"], FK, T)
        early_ring = place("early_ring", at["hT"], ROUNDED, QUARTER)
        mixed_rounded = place("mixed_rounded", at["hT"] + 16 * T, 8, T)
        hT_flat = hT[:, :, :].rearrange("p k t -> p (k t)")
        hT_rest_flat = hT_rest[:, :, :].rearrange("p k t -> p (k t)")
        cst = place("cst", at["cst"], CONST_N)
        row = place("row", at["row"], 2, D)
        stats = place("stats", at["stats"], 64)
        arena = place("arena", at["arena"], ARENA)
        hT_rounded_buf = place("hT_rounded_buf", at["arena"] + 6 * T, FK, T)
        hT_rounded_flat = hT_rounded_buf[:, :, :].rearrange("p k t -> p (k t)")
        weight_ring = place("weight_ring", at["arena"] + (6 + FK) * T, ROUNDED, QUARTER)
        ps = ctx.enter_context(nc.psum_tensor("ps", [P, 8, BANK], F32))
        ps_flat = ps[:, :, :].rearrange("p b n -> p (b n)")

        def const(name, a=0, b=None):
            at = CONST_AT[name]
            return cst[:, at + a:at + (dict(CONST)[name] if b is None else b)]

        def heads(name, n):
            return const("heads", HEAD_AT[name], HEAD_AT[name] + n)

        ident = const("ident")
        ones = const("ones")

        def area(at, *shape):
            n = int(np.prod(shape))
            assert at + n <= ARENA
            v = arena[:, at:at + n]
            if len(shape) == 2:
                v = v.rearrange("p (a b) -> p a b", a=shape[0])
            elif len(shape) == 3:
                v = v.rearrange("p (a b c) -> p a b c", a=shape[0], b=shape[1])
            return v

        gate_buf = area(0, 3, 2 * T)
        raw_buf = area(ARENA - 6 * 4 * T, 3, 4 * T)
        conv_buf = area(ARENA - 3 * 4 * T, 3, 4 * T)

        landed = [sem(f"unit_landed_{j}") for j in range(SLOTS)]
        unit_done = sem("unit_done")
        x_loaded = sem("x_loaded")
        early_loaded = sem("early_loaded")
        cst_loaded = sem("cst_loaded")
        row_landed = [sem(f"row_landed_{j}") for j in range(2)]
        x_ready = sem("x_ready")
        deviation = sem("deviation")
        xn_ready = sem("xn_ready")
        xn_turned = sem("xn_turned")
        xT_ready = sem("xT_ready")
        evacuated = sem("evacuated")
        gated = sem("gated")
        hidden = sem("hidden")
        w_rounded = sem("weights_rounded")
        w_split = sem("weights_split")
        xT_rounded = sem("xT_rounded")
        hT_rounded = sem("hT_rounded")
        hT_split = sem("hT_split")
        conv_tail = sem("conv_tail")
        conv_silu = sem("conv_silu")
        first_rows_done = sem("first_rows_done")
        mixed = sem("mixed")
        act_step = Tally(sem("act_step"))
        dve_step = Tally(sem("dve_step"))
        stored = sem("stored")

        def units_until(u):
            return u + 1

        def chunk_read(g, c):
            return 3 + g.chunk + c + 1

        def pair(j):
            return ps_flat[:, 2 * j * BANK:(2 * j + 2) * BANK]

        def quarter(c):
            return ring[:, c.unit % SLOTS, c.q * QUARTER:(c.q + 1) * QUARTER]

        def rest(c):
            return ring_rest[:, c.unit % SLOTS, c.q * QUARTER:(c.q + 1) * QUARTER]

        def rounded(c):
            at = c.place % ROUNDED
            return (early_ring if c.early else weight_ring)[:, at, :]

        def r32(v):
            return v.bitcast(F32R)

        def split_next(place):
            mine = quarters[place]
            found = [quarters.get(place + ROUNDED + n) for n in range(4)]
            return [c for c in found if c and c.early == mine.early]

        def split_first(place):
            return [quarters[place + n] for n in range(ROUNDED)]

        def hT_parts(g):
            return (mixed_rounded if g.kind in ("gdn", "swa", "nsa") else hT_rounded_buf), hT_rest

        def hT_pair(v, n):
            return v[:, 2 * n:2 * n + 2, :].rearrange("p k t -> p (k t)")

        def first_down_steps(g):
            steps = []
            first = split_first(g.split_down)
            for n in range(g.k_tiles // 2):
                steps.append((n, None))
                steps += [(None, c) for c in first[2 * n:2 * n + 2]]
            return steps

        mixed_raises = {"gdn": 4, "swa": 8, "nsa": 8, "ssd": 16}
        mixed_before, at = {}, 0
        for g in stages:
            mixed_before[g.s] = at
            at += mixed_raises.get(g.kind, 0)
        convolved = [g for g in stages if g.kind in ("gdn", "ssd")]

        G_Q, G_K, G_V = 0, 8, 16
        gd_in = area(0, 24, T)
        gd_z = area(6144, 8, T)
        gd_inv = area(8192, 4, 4 * P)
        gd_invT = area(10240, 4, 4 * P)
        gd_LT = area(12288, 4, 4 * P)
        gd_off = area(14336, 4, 4 * P)
        gd_mid = area(16384, 4, 4 * P)
        gd_square = area(16384, 2, 2 * T)
        gd_root = area(17408, 2, 2 * T)
        gd_small = area(18432, 16, 16)
        gd_ba, gd_u, gd_arg, gd_g, gd_gc, gd_beta = (gd_small[:, 2 * n:2 * n + 2, :] for n in range(6))
        gd_rate, gd_kdec = gd_small[:, 12, 0:8], gd_small[:, 13, 0:8]
        gd_grow = area(18688, 8, P)
        gd_attT = xn
        gd_kb = spare
        gd_vb = hT[:, 8:16, :].rearrange("p k (e n) -> p (k e) n", e=2)
        gd_kd = hT[:, 16:20, :].rearrange("p k (e n) -> p (k e) n", e=2)
        gd_new0, gd_state = area(16384, 8, P), area(17408, 8, P)
        gd_rhs, gd_new1 = area(14336, 8, P), area(15360, 8, P)
        gd_osquare, gd_oroot = area(12288, 2, 2 * T), area(13312, 2, 2 * T)
        ba_done = sem("gdn_ba_done")
        q_squared = sem("gdn_q_squared")
        q_square_sum = sem("gdn_q_square_sum")
        q_root = sem("gdn_q_root")
        q_normed = sem("gdn_q_normed")
        g_arg = sem("gdn_g_arg")
        g_log = sem("gdn_g_log")
        g_ready = sem("gdn_g_ready")
        g_cums_done = sem("gdn_g_cums_done")
        g_cums_ready = sem("gdn_g_cums_ready")
        kdec_ready = sem("gdn_kdec_ready")
        g_rows_done = sem("gdn_g_rows_done")
        g_diff = sem("gdn_g_diff")
        g_decay = sem("gdn_g_decay")
        kb_ready = sem("gdn_kb_ready")
        kq_done = sem("gdn_kq_done")
        att_ready = sem("gdn_att_ready")
        v_turned = sem("gdn_v_turned")
        v_ready = sem("gdn_v_ready")
        grown_ready = sem("gdn_grown_ready")
        off_ready = sem("gdn_off_ready")
        off_used = sem("gdn_off_used")
        mid_ready = sem("gdn_mid_ready")
        inv_terms = sem("gdn_inv_terms")
        inv_ready = sem("gdn_inv_ready")
        invT_ready = sem("gdn_invT_ready")
        new0_done, new0_ready = sem("gdn_new0_done"), sem("gdn_new0_ready")
        state_sum, state_copied = sem("gdn_state_sum"), sem("gdn_state_copied")
        carried_done, rhs_ready = sem("gdn_carried_done"), sem("gdn_rhs_ready")
        new1_done, new1_ready = sem("gdn_new1_done"), sem("gdn_new1_ready")
        o_done = sem("gdn_o_done")
        o_squared = sem("gdn_o_squared")
        o_square_sum = sem("gdn_o_square_sum")
        o_root = sem("gdn_o_root")
        class Attention:

            def __init__(self, kind, key_tiles, value_tiles):
                self.kind, self.key_tiles, self.value_tiles = kind, key_tiles, value_tiles
                self.branches = len(key_tiles)
                self.mask = "window" if kind == "swa" else "causal"
                self.scored = sem(kind + "_scored")
                self.masked = sem(kind + "_masked")
                self.maxed = sem(kind + "_maxed")
                self.exped = sem(kind + "_exped")
                self.probs = sem(kind + "_probs")
                self.turned = sem(kind + "_turned")
                self.turned_out = sem(kind + "_turned_out")
                self.summed = sem(kind + "_summed")
                self.values = sem(kind + "_values")
                self.values_turned = sem(kind + "_values_turned")
                self.quads = [(group, qb) for group in range(GROUPS) for qb in range(NT)]
                self.jobs = [(n, b) for n in range(len(self.quads)) for b in range(self.branches)]
                first = -1 if kind == "nsa" else 0
                self.turns = [(n, b) for n in range(len(self.quads)) for b in range(first, self.branches)]

            def scores(self, j):
                keys = (self.quads[self.jobs[j][0]][1] + 1) * P
                v = ps_flat[:, 2 * (j % 2) * BANK:2 * (j % 2) * BANK + 4 * keys]
                return v.rearrange("p (r k) -> p r k", r=4)

            def prob(self, j):
                keys = (self.quads[self.jobs[j][0]][1] + 1) * P
                v = prob_buf[:, j % 2, 0:4 * keys]
                return v.rearrange("p (r k) -> p r k", r=4)

        mix_tiles = area(0, 20, T)
        value_buf = area(5120, 2, NT, T)
        prob_buf = area(6144, 2, 4 * T)
        probT_buf = area(8192, 4, 4 * T)
        max_buf = area(12288, 16, 4)
        sum_buf = area(12352, 16, 4)
        sink_buf = area(12416, 16, 4)
        inv_buf = area(12480, 16, 4)
        attention = {"swa": Attention("swa", [8], [10]), "nsa": Attention("nsa", [12, 16], [14, 18])}
        SCALE = HD ** -0.5
        cmp_probT_buf = area(17024, 2, 4 * P)
        cmp_prob = area(18048, NT, 16, 16)
        gates_buf = area(18560, NT, 48)
        cmp_value = area(16768, 4 * HD)
        NG = GROUPS * NC
        token_pairs = area(12800, 2, GROUPS, P)
        cmp_in = area(13824, 2, 16, NG)
        cmp_hidden = area(15744, 4, 4 * NG)
        cmp_key = area(16704, NG)
        cmp_drop = area(18656, NT, 16)
        cmp_max = area(18688, NT, 16)
        cmp_sum = area(18720, NT, 16)
        pairs_landed = sem("nsa_pairs_landed")
        cmp_in_ready = sem("nsa_cmp_in_ready")
        hidden_done = sem("nsa_hidden_done")
        tanh_in = sem("nsa_tanh_in")
        tanh_done = sem("nsa_tanh_done")
        gelu_done = sem("nsa_gelu_done")
        cmp_done = sem("nsa_cmp_done")
        cmp_out = sem("nsa_cmp_out")
        cmp_scored = sem("nsa_cmp_scored")
        cmp_centered = sem("nsa_cmp_centered")
        cmp_exped = sem("nsa_cmp_exped")
        cmp_ready = sem("nsa_cmp_ready")
        gates_done = sem("nsa_gates_done")
        gates_ready = sem("nsa_gates_ready")
        S_X, S_B, S_C = 0, 16, 20
        ssd_in = area(0, 24, T)
        ssd_z = area(6144, 16, T)
        ssd_xdec = area(10240, 2048)
        ssd_cb = area(12288, 8, P)
        ssd_B = area(13312, 4, P)
        ssd_w = area(13824, 4, 4 * P)
        ssd_state = area(15872, 4, 8 * HD)
        ssd_y = area(17920, 2, 8 * HD)
        ssd_small = area(18944, 12, 64)
        ssd_u, ssd_e, ssd_dt, ssd_dta, ssd_acs, ssd_misc = (ssd_small[:, n, :] for n in range(6))
        ssd_ea, ssd_dec = ssd_small[:, 6, 0:32], ssd_small[:, 7, 0:32]
        xdt_parts = [[spare[:, 2 * gg:2 * gg + 2, :].rearrange("p k t -> p (k t)") for gg in range(4)],
                     [xn[:, gg // 2, (gg % 2) * 512:(gg % 2 + 1) * 512] for gg in range(4)]]
        ssd_square = area(10240, 2, 4 * T)
        ssd_root = area(12288, 4, T)
        dt_done = sem("ssd_dt_done")
        dt_arg = sem("ssd_dt_arg")
        dt_log = sem("ssd_dt_log")
        dta_ready = sem("ssd_dta_ready")
        cums_done = sem("ssd_cums_done")
        cums_ready = sem("ssd_cums_ready")
        cums_exp = sem("ssd_cums_exp")
        b_turned = sem("ssd_b_turned")
        b_ready = sem("ssd_b_ready")
        cb_done = sem("ssd_cb_done")
        cb_ready = sem("ssd_cb_ready")
        x_turned = sem("ssd_x_turned")
        xdt_ready = sem("ssd_xdt_ready")
        xdec_ready = sem("ssd_xdec_ready")
        state_done = sem("ssd_state_done")
        state_ready = sem("ssd_state_ready")
        rows_done = sem("ssd_rows_done")
        diff_ready = sem("ssd_diff_ready")
        decay_ready = sem("ssd_decay_ready")
        w_ready = sem("ssd_w_ready")
        y_half = sem("ssd_y_half")
        y_done = sem("ssd_y_done")
        y_out = sem("ssd_y_out")
        y_turned = sem("ssd_y_turned")
        y_turned_out = sem("ssd_y_turned_out")
        y_gated = sem("ssd_y_gated")
        y_squared = sem("ssd_y_squared")
        y_square_sum = sem("ssd_y_square_sum")
        y_root = sem("ssd_y_root")
        block = ctx.enter_context(nc.Block())

        @block.sync
        def _(sp):
            early = CONST_AT["ones"]
            x_tiles = x_in.rearrange("(t p) d -> p t d", p=P)
            for t in range(NT):
                sp.dma_start(x[:, t, :], x_tiles[:, t, :]).then_inc(x_loaded, 16)
            sp.dma_start(cst[:, 0:early], consts[:, 0:early]).then_inc(early_loaded, 16)
            for j in range(SLOTS):
                sp.dma_start(ring[:, j, :], units[j]).then_inc(landed[j], 16)
                if j == 0:
                    sp.dma_start(cst[:, early:CONST_N], consts[:, early:CONST_N]).then_inc(cst_loaded, 16)
            n_rounds = n_units // SLOTS
            with sp.Fori(1, n_rounds) as i:
                for j in range(SLOTS):
                    sp.wait_ge(unit_done, (i - 1) * SLOTS + j + 1)
                    sp.dma_start(ring[:, j, :], units[i * SLOTS + j]).then_inc(landed[j], 16)
            for u in range(n_rounds * SLOTS, n_units):
                sp.wait_ge(unit_done, u - SLOTS + 1)
                sp.dma_start(ring[:, u % SLOTS, :], units[u]).then_inc(landed[u % SLOTS], 16)
            out_tiles = out.rearrange("(t p) d -> p t d", p=P)
            for t in range(NT):
                sp.wait_ge(x_ready, x_after[events[-1], t])
                sp.dma_start(out_tiles[:, t, :], x[:, t, :]).then_inc(stored, 16)
            sp.wait_ge(stored, 16 * NT)

        @block.tensor
        def _(pe):
            mm = nc.tensor.matmul

            def norm_turned(g):
                for t in range(NT):
                    pe.wait_ge(xn_ready, 2 * g.s + t + 1)
                    for kt in range(KD):
                        o = (kt % 2) * T + t * P
                        last = nc.tensor.transpose(ps[:, kt // 2, o:o + P], xn[:, t, kt * P:(kt + 1) * P], ident)
                        if t == NT - 1 and kt % 2 == 1:
                            last.then_inc(xn_turned, 1)

            def up(g):
                def chunk(j, i=0):
                    pe.wait_ge(evacuated, chunk_read(g, j - 3) + 3 * i)
                    for f in range(4):
                        c = quarters[g.split + 4 * j + f]
                        pe.wait_ge(w_split, c.count + 12 * i)
                        o = ps[:, 2 * (j % 3) + f // 2, (f % 2) * T:(f % 2 + 1) * T]
                        for kt in range(KD):
                            w, w_rest = (r32(v[:, kt * P:(kt + 1) * P]) for v in (rounded(c), rest(c)))
                            x_k, x_rest = r32(xT[:, kt, :]), r32(xT_rest[:, kt, :])
                            if j == 0 and f == 0 and kt % 2 == 0:
                                pe.wait_ge(xT_ready, KD * g.s + kt + 2)
                            mm(o, w, x_k, start=(kt == 0), stop=False)
                            mm(o, w, x_rest, start=False, stop=False)
                            last = mm(o, w_rest, x_k, start=False, stop=(kt == KD - 1))
                    last.then_inc(unit_done, 1)

                turns = g.chunks // 3
                with pe.Fori(0, turns) as i:
                    for j in range(3):
                        chunk(j, i)
                for j in range(3 * turns, g.chunks):
                    chunk(j)

            def down(g):
                h, h_rest = hT_parts(g)
                if not g.own_ring:
                    pe.wait_ge(evacuated, chunk_read(g, 8))

                def products(kt, t):
                    c = quarters[g.split_down + kt]
                    tokens = slice(t * P, (t + 1) * P)
                    for n in range(2):
                        o = ps[:, 4 + 2 * t + n, :]
                        w, w_rest = (r32(v[:, n * BANK:(n + 1) * BANK]) for v in (rounded(c), rest(c)))
                        mm(o, r32(h[:, kt, tokens]), w, start=(kt == 0), stop=False)
                        mm(o, r32(h[:, kt, tokens]), w_rest, start=False, stop=False)
                        last = mm(o, r32(h_rest[:, kt, tokens]), w, start=False, stop=(kt == g.k_tiles - 1))
                    return last

                for v in range(g.down_units):
                    kts = range(4 * v, min(4 * v + 4, g.k_tiles))
                    last_unit = v == g.down_units - 1
                    for kt in kts:
                        pe.wait_ge(w_split, quarters[g.split_down + kt].count)
                        pe.wait_ge(hT_split, g.rest + kt // 2 + 1)
                        if not last_unit:
                            for t in range(NT):
                                last = products(kt, t)
                    if last_unit:
                        for t in range(NT):
                            for kt in kts:
                                last = products(kt, t)
                            if t == 0:
                                last.then_inc(first_rows_done, 1)
                    last.then_inc(unit_done, 1)

            def gdn(g):
                w = const("w_ba").rearrange("p (k n) -> p k n", k=KD)
                pe.wait_ge(evacuated, chunk_read(g, g.chunks - 1))
                for t in range(NT):
                    for kt in range(KD):
                        tokens = slice(t * P, (t + 1) * P)
                        mm(ps[:, 6, t * 16:(t + 1) * 16], xT[:, kt, tokens], w[:, kt, :], start=(kt == 0), stop=False)
                        last = mm(ps[:, 6, t * 16:(t + 1) * 16], xT_rest[:, kt, tokens], w[:, kt, :],
                                  start=False, stop=(kt == KD - 1))
                last.then_inc(ba_done, 1)
                for n in range(8):
                    pe.wait_ge(q_squared, n + 1)
                    if n >= 2:
                        pe.wait_ge(q_root, n - 1)
                    mm(ps[:, n % 2, :], ones, gd_square[:, n % 2, :], start=True, stop=True)\
                        .then_inc(q_square_sum, 1)
                pe.wait_ge(g_ready, 1)
                mm(ps[:, 7, 0:16], const("upper"), gd_g[:, :, 0:8], start=True, stop=True)
                mm(ps[:, 7, 16:24], ones, gd_g[:, 0, 0:8], start=True, stop=True).then_inc(g_cums_done, 1)
                pe.wait_ge(q_root, 8)

                def rows(i):
                    if i >= 2:
                        pe.wait_ge(g_decay, i - 1)
                        pe.wait_ge(kb_ready, i - 1)
                    t, h = i // 2, i % 2 * 4
                    for r in range(4):
                        mm(ps[:, i % 2, r * P:(r + 1) * P], gd_g[:, t, h + r:h + r + 1].to_broadcast([P, P]),
                           const("upper"), start=True, stop=True)
                        last = mm(ps[:, 2 + i % 2, r * P:(r + 1) * P],
                                  gd_beta[:, t, h + r:h + r + 1].to_broadcast([P, P]), ident, start=True, stop=True)
                    last.then_inc(g_rows_done, 1)

                def keys_queries(i):
                    t, h = i // 2, i % 2 * 4
                    tokens = slice(t * P, (t + 1) * P)
                    pe.wait_ge(kb_ready, i + 1)
                    if i >= 1:
                        pe.wait_ge(att_ready, i)
                    for r in range(4):
                        key = gd_in[:, G_K + h + r, tokens]
                        mm(ps[:, 4, r * P:(r + 1) * P], key, gd_kb[:, h + r, tokens], start=True, stop=True)
                        last = mm(ps[:, 5, r * P:(r + 1) * P], key, gd_in[:, G_Q + h + r, tokens],
                                  start=True, stop=True)
                    last.then_inc(kq_done, 1)

                def by_token(i):
                    if i >= 1:
                        pe.wait_ge(v_ready, i)
                    tile, t, h = (G_V, i // 2, i % 2 * 4) if i < 4 else (G_K, 0, (i - 4) * 4)
                    for r in range(4):
                        last = nc.tensor.transpose(ps[:, 6, r * P:(r + 1) * P],
                                                   gd_in[:, tile + h + r, t * P:(t + 1) * P], ident)
                    last.then_inc(v_turned, 1)

                pe.wait_ge(q_normed, 8)
                rows(0)
                rows(1)
                for i in range(4):
                    by_token(i)
                    keys_queries(i)
                    if i < 2:
                        rows(i + 2)
                by_token(4)
                by_token(5)
                for i in range(4):
                    pe.wait_ge(off_ready, i + 1)
                    if i >= 2:
                        pe.wait_ge(inv_ready, i - 1)
                    for r in range(4):
                        last = nc.tensor.transpose(ps[:, i % 2, r * P:(r + 1) * P], gd_off[:, i, r * P:(r + 1) * P],
                                                   ident)
                    last.then_inc(off_used, 1)
                pe.wait_ge(inv_ready, 4)
                with pe.Fori(1, LEVELS) as level:
                    def middle(i):
                        pe.wait_ge(off_ready, level * 4 + i + 1)
                        pe.wait_ge(inv_ready, (level - 1) * 4 + i + 1)
                        if i >= 2:
                            pe.wait_ge(mid_ready, (level - 1) * 4 + i - 1)
                        for r in range(4):
                            problem = slice(r * P, (r + 1) * P)
                            last = mm(ps[:, i % 2, problem], gd_off[:, i, problem], gd_inv[:, i, problem],
                                      start=True, stop=True)
                        last.then_inc(off_used, 1)

                    def corrections(i):
                        pe.wait_ge(mid_ready, (level - 1) * 4 + i + 1)
                        pe.wait_ge(inv_ready, level * 4 + i - 1)
                        pe.wait_ge(invT_ready, level * 4 + i - 1)
                        for r in range(4):
                            problem = slice(r * P, (r + 1) * P)
                            mm(ps[:, 2 + i % 2, problem], gd_invT[:, i, problem], gd_mid[:, i, problem],
                               start=True, stop=True)
                            last = mm(ps[:, 4 + i % 2, problem], gd_mid[:, i, problem], gd_invT[:, i, problem],
                                      start=True, stop=True)
                        last.then_inc(inv_terms, 1)

                    middle(0)
                    middle(1)
                    corrections(0)
                    middle(2)
                    corrections(1)
                    middle(3)
                    corrections(2)
                    corrections(3)

                def per_head(bank, lhsT, rhs, done):
                    for half in range(2):
                        for r in range(4):
                            h = half * 4 + r
                            last = mm(ps[:, bank + half, r * P:(r + 1) * P], lhsT(h), rhs(h), start=True, stop=True)
                        last.then_inc(done, 1)

                def inverse(problem):
                    return gd_invT[:, problem // 4, problem % 4 * P:(problem % 4 + 1) * P]

                pe.wait_ge(inv_ready, 4 * LEVELS)
                pe.wait_ge(invT_ready, 4 * LEVELS)
                pe.wait_ge(v_ready, 6)
                per_head(0, lambda h: inverse(h), lambda h: gd_vb[:, h, :], new0_done)
                pe.wait_ge(new0_ready, 2)
                per_head(2, lambda h: gd_kd[:, h, :], lambda h: gd_new0[:, h, :], state_sum)
                pe.wait_ge(state_copied, 2)
                pe.wait_ge(grown_ready, 2)
                per_head(4, lambda h: gd_kb[:, h, P:T], lambda h: gd_state[:, h, :], carried_done)
                pe.wait_ge(rhs_ready, 2)
                per_head(0, lambda h: inverse(8 + h), lambda h: gd_rhs[:, h, :], new1_done)
                o_banks = (6, 7, 2, 3)

                def o_sum(n):
                    pe.wait_ge(o_squared, n + 1)
                    if n >= 2:
                        pe.wait_ge(o_root, n - 1)
                    mm(ps[:, 4 + n % 2, :], ones, gd_osquare[:, n % 2, :], start=True, stop=True)\
                        .then_inc(o_square_sum, 1)

                for n in range(4):
                    for e in range(2):
                        h = 2 * n + e
                        o = ps[:, o_banks[n], e * T:(e + 1) * T]
                        mm(o[:, 0:P], gd_new0[:, h, :], gd_attT[:, 0, h * P:(h + 1) * P], start=True, stop=True)
                        mm(o[:, P:T], gd_state[:, h, :], gd_in[:, G_Q + h, P:T], start=True, stop=False)
                        if h % 4 == 0:
                            pe.wait_ge(new1_ready, h // 4 + 1)
                        last = mm(o[:, P:T], gd_new1[:, h, :], gd_attT[:, 1, h * P:(h + 1) * P],
                                  start=False, stop=True)
                    last.then_inc(o_done, 1)
                    if n >= 1:
                        o_sum(n - 1)
                o_sum(3)

            def attend(a, g, compressed=None):
                def value_turns(b):
                    for t in range(NT):
                        for f in range(2):
                            last = nc.tensor.transpose(ps[:, 6 + b, (2 * t + f) * P:(2 * t + f + 1) * P],
                                                       mix_tiles[:, a.value_tiles[b] + f, t * P:(t + 1) * P], ident)
                    last.then_inc(a.values_turned, 1)

                def score(j):
                    n, b = a.jobs[j]
                    group, qb = a.quads[n]
                    h0 = HD * (group % 2)
                    if j >= 2:
                        pe.wait_ge(a.masked, j - 1)
                    for r in range(4):
                        last = mm(a.scores(j)[:, r, :],
                                  mix_tiles[h0:h0 + HD, group // 2 * 4 + r, qb * P:(qb + 1) * P],
                                  mix_tiles[h0:h0 + HD, a.key_tiles[b] + group // 2, 0:(qb + 1) * P],
                                  start=True, stop=True)
                    last.then_inc(a.scored, 1)

                def turn(k):
                    n, b = a.turns[k]
                    group, qb = a.quads[n]
                    if k >= 1:
                        pe.wait_ge(a.turned_out, k)
                    if b < 0:
                        for r in range(4):
                            last = nc.tensor.transpose(ps[0:NC, 4, r * P:(r + 1) * P],
                                                       cmp_prob[:, qb, group * 4 + r, 0:NC], ident)
                    else:
                        j = a.jobs.index((n, b))
                        pe.wait_ge(a.probs, j + 1)
                        for kb in range(qb + 1):
                            for r in range(4):
                                last = nc.tensor.transpose(ps[:, 4 + kb, r * P:(r + 1) * P],
                                                           a.prob(j)[:, r, kb * P:(kb + 1) * P], ident)
                    last.then_inc(a.turned, 1)

                def outputs(n):
                    group, qb = a.quads[n]
                    h0 = HD * (group % 2)
                    pe.wait_ge(a.turned_out, len([k for k in a.turns if k[0] <= n]))
                    if n >= 2:
                        pe.wait_ge(mixed, mixed_before[g.s] + n - 1)
                    for r in range(4):
                        o = ps[h0:h0 + HD, 6 + n % 2, r * P:(r + 1) * P]
                        terms = []
                        if compressed:
                            terms.append((cmp_value[0:NC, group * HD:(group + 1) * HD],
                                          cmp_probT_buf[0:NC, n % 2, r * P:(r + 1) * P]))
                        for b in range(a.branches):
                            probT = probT_buf[:, (n * a.branches + b) % 4, :]
                            for kb in range(qb + 1):
                                terms.append((value_buf[:, b, kb, group * HD:(group + 1) * HD],
                                              probT[:, (kb * 4 + r) * P:(kb * 4 + r + 1) * P]))
                        for m, (lhsT, rhs) in enumerate(terms):
                            last = mm(o, lhsT, rhs, start=(m == 0), stop=(m == len(terms) - 1))
                    last.then_inc(a.summed, 1)

                for b in range(a.branches):
                    value_turns(b)
                score(0)
                score(1)
                if compressed:
                    compressed()
                pe.wait_ge(a.values, a.branches)
                for k, (n, b) in enumerate(a.turns):
                    turn(k)
                    if b >= 0:
                        j = a.jobs.index((n, b))
                        if j + 2 < len(a.jobs):
                            score(j + 2)
                    if b == a.branches - 1:
                        outputs(n)

            def swa(g):
                pe.wait_ge(evacuated, chunk_read(g, g.chunks - 1))
                attend(attention["swa"], g)

            def nsa(g):
                pe.wait_ge(evacuated, chunk_read(g, g.chunks - 1))
                w = const("w_gates").rearrange("p (k n) -> p k n", k=KD)
                for t in range(NT):
                    for kt in range(KD):
                        tokens = slice(t * P, (t + 1) * P)
                        mm(ps[:, 5, t * 48:(t + 1) * 48], xT[:, kt, tokens], w[:, kt, :], start=(kt == 0), stop=False)
                        last = mm(ps[:, 5, t * 48:(t + 1) * 48], xT_rest[:, kt, tokens], w[:, kt, :],
                                  start=False, stop=(kt == KD - 1))
                last.then_inc(gates_done, 1)

                def compressed():
                    pe.wait_ge(gates_ready, 1)
                    for kv in range(2):
                        u = g.extra + kv
                        pe.wait_ge(landed[u % SLOTS], 16 * (u // SLOTS + 1))
                        pe.wait_ge(cmp_in_ready, kv + 1)
                        for hid in range(2):
                            for m in range(16):
                                last = mm(ps[:, 4 + kv, hid * NG:(hid + 1) * NG],
                                          ring[:, u % SLOTS, m * 256 + hid * P:m * 256 + (hid + 1) * P],
                                          cmp_in[:, kv, m, :], start=(m == 0), stop=(m == 15))
                        last.then_inc(unit_done, 1)
                    w2 = const("w_cmp2").rearrange("p (v h n) -> p v h n", v=2, h=2)
                    pe.wait_ge(gelu_done, 1)
                    for hid in range(2):
                        mm(ps[:, 4, 0:NG], w2[:, 0, hid, :], cmp_hidden[:, 0, hid * NG:(hid + 1) * NG],
                           start=(hid == 0), stop=(hid == 1))
                    for group in range(GROUPS):
                        for hid in range(2):
                            at = (2 + hid) * NG + group * NC
                            last = mm(ps[0:NC, 5, group * HD:(group + 1) * HD], cmp_hidden[:, 0, at:at + NC],
                                      w2[:, 1, hid, 0:HD], start=(hid == 0), stop=(hid == 1))
                    last.then_inc(cmp_done, 1)
                    pe.wait_ge(cmp_out, 2)
                    for qb in range(NT):
                        for h in range(16):
                            group, r = h // 4, h % 4
                            h0 = HD * (group % 2)
                            at = (qb * 8 + group // 2 * 4 + r) * 16
                            last = mm(ps[:, 4 + group % 2, at:at + NC],
                                      mix_tiles[h0:h0 + HD, group // 2 * 4 + r, qb * P:(qb + 1) * P],
                                      cmp_key[h0:h0 + HD, group * NC:(group + 1) * NC], start=True, stop=True)
                    last.then_inc(cmp_scored, 1)
                    pe.wait_ge(cmp_ready, NT)

                attend(attention["nsa"], g, compressed)

            def ssd(g):
                w = const("w_dt").rearrange("p (k n) -> p k n", k=KD)
                pe.wait_ge(evacuated, chunk_read(g, g.chunks - 1))
                for t in range(NT):
                    for kt in range(KD):
                        tokens = slice(t * P, (t + 1) * P)
                        mm(ps[:, 6, t * 32:(t + 1) * 32], xT[:, kt, tokens], w[:, kt, :], start=(kt == 0), stop=False)
                        last = mm(ps[:, 6, t * 32:(t + 1) * 32], xT_rest[:, kt, tokens], w[:, kt, :],
                                  start=False, stop=(kt == KD - 1))
                last.then_inc(dt_done, 1)
                pe.wait_ge(conv_silu, 6 * (1 + sum(q.s < g.s for q in convolved)))
                for gg in range(4):
                    last = nc.tensor.transpose(ps[:, 4, gg * P:(gg + 1) * P], ssd_in[:, S_B + gg, 0:P], ident)
                last.then_inc(b_turned, 1)
                for t in range(NT):
                    for gg in range(4):
                        tokens = slice(t * P, (t + 1) * P)
                        last = mm(ps[:, t, gg * P:(gg + 1) * P], ssd_in[:, S_B + gg, tokens],
                                  ssd_in[:, S_C + gg, tokens], start=True, stop=True)
                    last.then_inc(cb_done, 1)

                def x_by_token(m):
                    t, gg = m // 4, m % 4
                    if m >= 2:
                        pe.wait_ge(xdt_ready, m - 1)
                    for f in range(4):
                        last = nc.tensor.transpose(ps[:, 2 + m % 2, f * P:(f + 1) * P],
                                                   ssd_in[:, S_X + 4 * gg + f, t * P:(t + 1) * P], ident)
                    last.then_inc(x_turned, 1)

                x_by_token(0)
                x_by_token(1)
                pe.wait_ge(dta_ready, 1)
                mm(ps[:, 7, 0:64], const("upper"), ssd_dta, start=True, stop=True)
                mm(ps[:, 7, 64:96], ones, ssd_dta[:, 0:32], start=True, stop=True).then_inc(cums_done, 1)
                for m in range(2, 8):
                    x_by_token(m)
                pe.wait_ge(b_ready, 1)
                for gg in range(4):
                    pe.wait_ge(xdec_ready, gg + 1)
                    if gg >= 2:
                        pe.wait_ge(state_ready, gg - 1)
                    mm(ps[:, 4 + gg % 2, :], ssd_B[:, gg, :], ssd_xdec[:, gg * 512:(gg + 1) * 512],
                       start=True, stop=True).then_inc(state_done, 1)

                def rows(k):
                    t, h = k // 8, k % 8 * 4
                    if k >= 2:
                        pe.wait_ge(diff_ready, k - 1)
                    for r in range(4):
                        column = ssd_dta[:, t * 32 + h + r:t * 32 + h + r + 1]
                        last = mm(ps[:, k % 2, r * P:(r + 1) * P], column.to_broadcast([P, P]), const("upper"),
                                  start=True, stop=True)
                    last.then_inc(rows_done, 1)

                def quadratic(k):
                    m = k // 2
                    t, gg = m // 4, m % 4
                    pe.wait_ge(w_ready, k + 1)
                    if k % 2 == 0 and m >= 2:
                        pe.wait_ge(y_out, m - 1)
                    for r in range(4):
                        o = (k % 2 * 4 + r) * HD
                        last = mm(ps[:, 2 + m % 2, o:o + HD], ssd_w[:, k % 4, r * P:(r + 1) * P],
                                  xdt_parts[t][gg][:, o:o + HD], start=True, stop=True)
                    last.then_inc(y_half, 1)

                def from_state(m):
                    gg = m % 4
                    if m >= 5:
                        pe.wait_ge(y_out, m)
                    mm(ps[:, 4, :], ssd_in[:, S_C + gg, P:2 * P], ssd_state[:, gg, :],
                       start=True, stop=True).then_inc(y_done, 1)

                def turn(m):
                    pe.wait_ge(y_out, m + 1)
                    if m >= 1:
                        pe.wait_ge(y_turned_out, m)
                    for f in range(4):
                        last = nc.tensor.transpose(ps[:, 5, f * P:(f + 1) * P], ssd_y[:, m % 2, f * P:(f + 1) * P],
                                                   ident)
                    last.then_inc(y_turned, 1)

                pe.wait_ge(cb_ready, 2)
                pe.wait_ge(xdt_ready, 8)
                pe.wait_ge(state_ready, 4)
                rows(0)
                for m in range(8):
                    rows(2 * m + 1)
                    quadratic(2 * m)
                    if m < 7:
                        rows(2 * m + 2)
                    quadratic(2 * m + 1)
                    if m >= 4:
                        from_state(m)
                    if m >= 1:
                        turn(m - 1)
                turn(7)
                for gg in range(4):
                    pe.wait_ge(y_squared, gg + 1)
                    if gg >= 2:
                        pe.wait_ge(y_root, gg - 1)
                    for f in range(4):
                        last = mm(ps[:, gg % 2, 0:T], ones, ssd_square[:, gg % 2, f * T:(f + 1) * T],
                                  start=(f == 0), stop=(f == 3))
                    last.then_inc(y_square_sum, 1)

            pe_mixer = {"gdn": gdn, "swa": swa, "nsa": nsa, "ssd": ssd}

            pe.wait_ge(early_loaded, 16)
            pe.sem_inc(evacuated, 3)
            for g in stages:
                norm_turned(g)
                up(g)
                if g.s == 0:
                    pe.wait_ge(cst_loaded, 16)
                if g.kind in pe_mixer:
                    pe_mixer[g.kind](g)
                down(g)

        @block.scalar
        def _(act):
            activation = nc.scalar.activation

            def deviation_of(in_, key):
                n = deviation_at[key] - 1
                square = stats[:, 4 + n % 4:5 + n % 4]
                act_step.up(activation(junk[:, :], in_, ACT.Square, accum_out=square))
                act_step.wait(act)
                activation(stats[:, n % 4:n % 4 + 1], square, ACT.Sqrt, scale=1.0 / D,
                           bias=EPS).then_inc(deviation, 1)

            def turned_out(g):
                for b in range(4):
                    act.wait_ge(xn_turned, 4 * g.s + b + 1)
                    for kt in (2 * b, 2 * b + 1):
                        gain = const("norms", g.norm * KD + kt, g.norm * KD + kt + 1)
                        activation(r32(xT[:, kt, :]), ps[:, b, (kt % 2) * T:(kt % 2 + 1) * T], ACT.Identity,
                                   scale=gain).then_inc(xT_rounded, 1)

            def split(found, i=0):
                for c in found:
                    if c.q == 0:
                        act.wait_ge(landed[c.unit % SLOTS], 16 * (c.unit // SLOTS + 1) + 16 * i)
                    activation(r32(rounded(c)), quarter(c), ACT.Copy).then_inc(w_rounded, 1)

            def split_hidden(c):
                at = bass.ds(c * 2 * T, 2 * T)
                activation(r32(hT_rounded_flat[:, at]), hT_flat[:, at], ACT.Copy).then_inc(hT_rounded, 1)

            def split_mixed(g):
                act.wait_ge(mixed, mixed_before[g.s] + mixed_raises[g.kind])
                for n, c in first_down_steps(g):
                    if c:
                        split([c])
                    else:
                        activation(r32(hT_pair(hT_parts(g)[0], n)), hT_pair(hT, n), ACT.Copy).then_inc(hT_rounded, 1)

            def swiglu(g):
                def chunk(j, i=0, c=0):
                    act.wait_ge(unit_done, units_until(g.unit + j) + 3 * i)
                    activation(gate_buf[:, j % 3, :], ps[:, 2 * (j % 3), :], ACT.Silu).then_inc(gated, 1)
                    split(split_next(g.split + 4 * j), i)
                    act.wait_ge(evacuated, chunk_read(g, j) + 3 * i)
                    split_hidden(c)

                turns = g.chunks // 3
                with act.Fori(0, turns) as i:
                    for j in range(3):
                        chunk(j, i, 3 * i + j)
                for j in range(3 * turns, g.chunks):
                    chunk(j, 0, j)

            taps_done = [0]

            def raw_out(g, j, i):
                act.wait_ge(unit_done, units_until(g.unit + j) + 3 * i)
                activation(raw_buf[:, j % 3, :], pair(j % 3), ACT.Copy).then_inc(evacuated, 1)

            def cffn(g):
                began = taps_done[0]

                def chunk(j, i=0, c=0):
                    raw_out(g, j, i)
                    split(split_next(g.split + 4 * j), i)
                    act.wait_ge(conv_tail, began + 4 * j + 2 + 12 * i)
                    gates = conv_buf[:, j % 3, 2 * T:4 * T]
                    activation(gates, gates, ACT.Silu).then_inc(gated, 1)
                    act.wait_ge(hidden, g.hidden + j + 1 + 3 * i)
                    split_hidden(c)

                turns = g.chunks // 3
                with act.Fori(0, turns) as i:
                    for j in range(3):
                        chunk(j, i, 3 * i + j)
                for j in range(3 * turns, g.chunks):
                    chunk(j, 0, j)
                taps_done[0] += 4 * g.chunks

            def conv_chunks(g):
                began = taps_done[0]
                with act.Fori(0, 2) as i:
                    for j in range(3):
                        raw_out(g, j, i)
                        split(split_next(g.split + 4 * j), i)
                        act.wait_ge(conv_tail, began + 4 * j + 4 + 12 * i)
                        activation(arena[:, bass.ds((3 * i + j) * 4 * T, 4 * T)], conv_buf[:, j, :],
                                   ACT.Silu).then_inc(conv_silu, 1)
                taps_done[0] += 24

            def gdn(g):
                conv_chunks(g)
                for c in range(6, g.chunks):
                    act.wait_ge(unit_done, units_until(g.unit + c))
                    activation(gd_z[:, 4 * (c - 6):4 * (c - 5), :].rearrange("p f t -> p (f t)"), pair(c % 3),
                               ACT.Silu).then_inc(evacuated, 1)
                    split(split_next(g.split + 4 * c))

                def root(n):
                    act.wait_ge(q_square_sum, n + 1)
                    if n >= 2:
                        act.wait_ge(q_normed, n - 1)
                    activation(gd_root[:, n % 2, :], ps[:, n % 2, :], ACT.Sqrt, bias=EPS).then_inc(q_root, 1)

                act.wait_ge(conv_silu, 6 * (1 + sum(q.s < g.s for q in convolved)))
                for n in range(8):
                    if n >= 2:
                        act.wait_ge(q_square_sum, n - 1)
                    activation(gd_square[:, n % 2, :], gd_in[:, 2 * n:2 * n + 2, :].rearrange("p f t -> p (f t)"),
                               ACT.Square).then_inc(q_squared, 1)
                    if n >= 1:
                        root(n - 1)
                root(7)
                act.wait_ge(g_arg, 1)
                e, b = gd_arg[:, :, 0:8], gd_ba[:, :, 0:8]
                act_step.up(activation(e, e, ACT.Exp))
                act_step.wait(act)
                activation(b, b, ACT.Exp, scale=-1.0)
                activation(gd_rate, heads("a_log", 8), ACT.Exp)
                activation(e, e, ACT.Ln, bias=1.0).then_inc(g_log, 1)
                act.wait_ge(g_cums_ready, 1)
                activation(gd_kdec, gd_kdec, ACT.Exp).then_inc(kdec_ready, 1)
                for i in range(4):
                    act.wait_ge(g_diff, i + 1)
                    last = activation(gd_off[:, i, :], gd_off[:, i, :], ACT.Exp)
                    if i >= 2:
                        half = gd_grow[:, (i - 2) * 4:(i - 1) * 4, :].rearrange("p h n -> p (h n)")
                        last = activation(half, ps[:, i % 2, :], ACT.Exp)
                    last.then_inc(g_decay, 1)
                with act.Fori(1, LEVELS) as level:
                    for i in range(4):
                        act.wait_ge(off_used, level * 4 + i + 1)
                        activation(gd_mid[:, i, :], ps[:, i % 2, :], ACT.Copy).then_inc(mid_ready, 1)

                def copied(to, bank, done, ready):
                    for half in range(2):
                        act.wait_ge(done, half + 1)
                        activation(to[:, half * 4:half * 4 + 4, :].rearrange("p h n -> p (h n)"),
                                   ps[:, bank + half, :], ACT.Copy).then_inc(ready, 1)

                copied(gd_new0, 0, new0_done, new0_ready)
                copied(gd_state, 2, state_sum, state_copied)
                copied(gd_new1, 0, new1_done, new1_ready)

                def o_rooted(n):
                    act.wait_ge(o_square_sum, n + 1)
                    if n >= 2:
                        act.wait_ge(mixed, mixed_before[g.s] + n - 1)
                    activation(gd_oroot[:, n % 2, :], ps[:, 4 + n % 2, :], ACT.Sqrt, scale=1.0 / P,
                               bias=EPS).then_inc(o_root, 1)

                for n in range(4):
                    act.wait_ge(o_done, n + 1)
                    if n >= 2:
                        act.wait_ge(o_square_sum, n - 1)
                    activation(gd_osquare[:, n % 2, :], ps[:, (6, 7, 2, 3)[n], :], ACT.Square).then_inc(o_squared, 1)
                    if n >= 1:
                        o_rooted(n - 1)
                o_rooted(3)

            def attend(a, g):
                def exps(j):
                    act.wait_ge(a.maxed, j + 1)
                    for r in range(4):
                        last = activation(a.prob(j)[:, r, :], a.prob(j)[:, r, :], ACT.Exp, scale=SCALE,
                                          bias=max_buf[:, j, r:r + 1], accum_out=sum_buf[:, j, r:r + 1])
                        if a.kind == "swa" and r == 3:
                            last = activation(sink_buf[:, j, :], sink_buf[:, j, :], ACT.Exp)
                    last.then_inc(a.exped, 1)

                def turned_out(k):
                    n, b = a.turns[k]
                    qb = a.quads[n][1]
                    act.wait_ge(a.turned, k + 1)
                    if n >= 2:
                        act.wait_ge(a.summed, n - 1)
                    if b < 0:
                        last = activation(cmp_probT_buf[0:NC, n % 2, :], ps[0:NC, 4, :], ACT.Copy)
                    else:
                        last = activation(probT_buf[:, (n * a.branches + b) % 4, 0:(qb + 1) * BANK],
                                          ps_flat[:, 4 * BANK:(5 + qb) * BANK], ACT.Copy)
                    last.then_inc(a.turned_out, 1)

                def outputs_out(n):
                    group, qb = a.quads[n]
                    h0 = HD * (group % 2)
                    act.wait_ge(a.summed, n + 1)
                    activation(hT[h0:h0 + HD, group // 2 * 4:group // 2 * 4 + 4, qb * P:(qb + 1) * P],
                               ps[h0:h0 + HD, 6 + n % 2, :].rearrange("p (r q) -> p r q", r=4),
                               ACT.Copy).then_inc(mixed, 1)

                exps(0)
                for k, (n, b) in enumerate(a.turns):
                    if b >= 0:
                        j = a.jobs.index((n, b))
                        if j + 1 < len(a.jobs):
                            exps(j + 1)
                    turned_out(k)
                    if b == a.branches - 1:
                        outputs_out(n)

            def values_out(a):
                for b in range(a.branches):
                    act.wait_ge(a.values_turned, b + 1)
                    activation(value_buf[:, b, :, :].rearrange("p t f -> p (t f)"), ps[:, 6 + b, :],
                               ACT.Copy).then_inc(a.values, 1)

            def swa(g):
                for c in range(g.chunks):
                    act.wait_ge(unit_done, units_until(g.unit + c))
                    for f in range(4):
                        bias = const("swa_bias", 4 * c + f, 4 * c + f + 1)
                        last = activation(mix_tiles[:, 4 * c + f, :], pair(c)[:, f * T:(f + 1) * T],
                                          ACT.Identity, bias=bias)
                    last.then_inc(evacuated, 1)
                    split(split_next(g.split + 4 * c))
                values_out(attention["swa"])
                attend(attention["swa"], g)

            def nsa(g):
                for c in (0, 1, 2, 3, 4):
                    act.wait_ge(unit_done, units_until(g.unit + c))
                    if c == 2:
                        source = pair(c % 3).rearrange("p (f s e) -> p f e s", f=4, e=2)
                        for e in range(2):
                            last = activation(mix_tiles[:, 8:12, e * P:(e + 1) * P], source[:, :, e, :], ACT.Copy)
                    else:
                        last = activation(mix_tiles[:, 4 * c:4 * c + 4, :].rearrange("p f t -> p (f t)"),
                                          pair(c % 3), ACT.Copy)
                    last.then_inc(evacuated, 1)
                    split(split_next(g.split + 4 * c))
                act.wait_ge(gates_done, 1)
                activation(gates_buf[:, :, :].rearrange("p t n -> p (t n)"), ps[:, 5, 0:NT * 48],
                           ACT.Sigmoid).then_inc(gates_ready, 1)
                a = attention["nsa"]
                values_out(a)
                act.wait_ge(tanh_in, 1)
                activation(cmp_hidden[:, 2, :], cmp_hidden[:, 2, :], ACT.Tanh,
                           scale=0.7978845608028654).then_inc(tanh_done, 1)
                act.wait_ge(cmp_done, 1)
                activation(cmp_key[:, :], ps[:, 4, 0:NG], ACT.Copy).then_inc(cmp_out, 1)
                activation(cmp_value[0:NC, :], ps[0:NC, 5, 0:4 * HD], ACT.Copy).then_inc(cmp_out, 1)
                for t in range(NT):
                    act.wait_ge(cmp_centered, t + 1)
                    activation(cmp_prob[:, t, :, 0:NC], cmp_prob[:, t, :, 0:NC], ACT.Exp,
                               scale=SCALE).then_inc(cmp_exped, 1)
                attend(a, g)

            def ssd(g):
                conv_chunks(g)
                for c in range(6, g.chunks):
                    act.wait_ge(unit_done, units_until(g.unit + c))
                    activation(ssd_z[:, 4 * (c - 6):4 * (c - 5), :].rearrange("p f t -> p (f t)"), pair(c % 3),
                               ACT.Silu).then_inc(evacuated, 1)
                    split(split_next(g.split + 4 * c))
                act.wait_ge(dt_arg, 1)
                act_step.up(activation(ssd_e, ssd_e, ACT.Exp))
                act_step.wait(act)
                activation(ssd_ea, heads("ssd_a", 32), ACT.Exp)
                activation(ssd_e, ssd_e, ACT.Ln, bias=1.0).then_inc(dt_log, 1)
                act.wait_ge(b_turned, 1)
                activation(ssd_B[:, :, :].rearrange("p g n -> p (g n)"), ps[:, 4, :], ACT.Copy).then_inc(b_ready, 1)
                act.wait_ge(cums_ready, 1)
                activation(ssd_dec, ssd_dec, ACT.Exp)
                activation(ssd_misc[:, 0:32], ssd_acs[:, 32:64], ACT.Exp).then_inc(cums_exp, 1)
                for gg in range(4):
                    act.wait_ge(state_done, gg + 1)
                    activation(ssd_state[:, gg, :], ps[:, 4 + gg % 2, :], ACT.Copy).then_inc(state_ready, 1)
                for k in range(16):
                    act.wait_ge(diff_ready, k + 1)
                    activation(ssd_w[:, k % 4, :], ssd_w[:, k % 4, :], ACT.Exp).then_inc(decay_ready, 1)
                act.wait_ge(y_gated, 8)
                for gg in range(4):
                    if gg >= 2:
                        act.wait_ge(y_square_sum, gg - 1)
                    activation(ssd_square[:, gg % 2, :], hT[:, 4 * gg:4 * gg + 4, :].rearrange("p f t -> p (f t)"),
                               ACT.Square).then_inc(y_squared, 1)
                    if gg >= 1:
                        root(gg - 1)
                root(3)

            def root(gg):
                act.wait_ge(y_square_sum, gg + 1)
                activation(ssd_root[:, gg, :], ps[:, gg % 2, 0:T], ACT.Sqrt, scale=1.0 / (4 * P),
                           bias=EPS).then_inc(y_root, 1)

            act_mixer = {"gdn": gdn, "swa": swa, "nsa": nsa, "ssd": ssd}

            act.wait_ge(early_loaded, 16)
            for t in range(NT):
                act.wait_ge(x_loaded, 16 * NT)
                deviation_of(x[:, t, :], ("norm", 0, t))
            for g in stages:
                first = split_first(g.split) if g.s == 0 or g.own_ring else []
                split(first[:1])
                turned_out(g)
                split(first[1:] if first else split_next(g.split - 4))
                if g.s == 0:
                    act.wait_ge(cst_loaded, 16)
                if g.kind == "swiglu":
                    swiglu(g)
                elif g.kind == "cffn":
                    cffn(g)
                else:
                    act_mixer[g.kind](g)
                    split_mixed(g)
                for v in range(g.down_units - 1):
                    act.wait_ge(unit_done, units_until(g.down + v))
                    split(split_next(g.split_down + 4 * v))
                for t in range(NT):
                    if g.kind in ("nsa", "cffn", "ssd"):
                        if t == 0:
                            act.wait_ge(first_rows_done, g.s + 1)
                        else:
                            act.wait_ge(unit_done, units_until(g.down + g.down_units - 1))
                        deviation_of(ps_flat[:, (4 + 2 * t) * BANK:(6 + 2 * t) * BANK], ("post", g.s, t))
                    if g.norm == FINAL_AFTER:
                        act.wait_ge(x_ready, x_after[("residual", g.s), t])
                        deviation_of(x[:, t, :], ("final", g.s, t))
                    if g.s < last_stage:
                        act.wait_ge(x_ready, x_event_before_norm(g.s + 1, t))
                        deviation_of(x[:, t, :], ("norm", g.s + 1, t))

        @block.vector
        def _(dve):
            tt, stt, ts = nc.vector.tensor_tensor, nc.vector.scalar_tensor_tensor, nc.vector.tensor_scalar

            def rstd(key):
                n = deviation_at[key]
                dve.wait_ge(deviation, n)
                column = stats[:, 8 + (n - 1) % 4:9 + (n - 1) % 4]
                dve_step.up(nc.vector.reciprocal(column, stats[:, (n - 1) % 4:(n - 1) % 4 + 1]))
                dve_step.wait(dve)
                return column

            def norm(s, t):
                column = rstd(("norm", s, t))
                ts(xn[:, t, :], x[:, t, :], column, None, ALU.mult).then_inc(xn_ready, 1)

            def turned_out(g):
                for b in range(4):
                    dve.wait_ge(xT_rounded, KD * g.s + 2 * b + 2)
                    for kt in (2 * b, 2 * b + 1):
                        gain = const("norms", g.norm * KD + kt, g.norm * KD + kt + 1)
                        stt(r32(xT_rest[:, kt, :]), ps[:, b, (kt % 2) * T:(kt % 2 + 1) * T], gain, xT[:, kt, :],
                            ALU.mult, ALU.subtract).then_inc(xT_ready, 1)

            def split(found, i=0):
                for c in found:
                    dve.wait_ge(w_rounded, c.count + 12 * i)
                    tt(r32(rest(c)), quarter(c), rounded(c), ALU.subtract).then_inc(w_split, 1)

            def split_hidden(g, j, i, c):
                at = bass.ds(c * 2 * T, 2 * T)
                dve.wait_ge(hT_rounded, g.rest + j + 1 + 3 * i)
                tt(r32(hT_rest_flat[:, at]), hT_flat[:, at], hT_rounded_flat[:, at], ALU.subtract).then_inc(hT_split, 1)

            def split_mixed(g):
                for n, c in first_down_steps(g):
                    if c:
                        split([c])
                    else:
                        dve.wait_ge(hT_rounded, g.rest + n + 1)
                        rounded_pair, rest_pair = (hT_pair(v, n) for v in hT_parts(g))
                        tt(r32(rest_pair), hT_pair(hT, n), rounded_pair, ALU.subtract).then_inc(hT_split, 1)

            def swiglu(g):
                def chunk(j, i=0, c=0):
                    dve.wait_ge(gated, g.gated + j + 1 + 3 * i)
                    tt(hT_flat[:, bass.ds(c * 2 * T, 2 * T)], gate_buf[:, j % 3, :],
                       ps[:, 2 * (j % 3) + 1, :], ALU.mult).then_inc(evacuated, 1)
                    split(split_next(g.split + 4 * j), i)
                    split_hidden(g, j, i, c)

                turns = g.chunks // 3
                with dve.Fori(0, turns) as i:
                    for j in range(3):
                        chunk(j, i, 3 * i + j)
                for j in range(3 * turns, g.chunks):
                    chunk(j, 0, j)

            tails = [0]

            def taps(j, weights, c, tiles, width):
                done = {}
                for back in range(width):
                    for f in tiles:
                        k = CONST_AT[weights] + (c * 4 + f) * (width + 1)
                        raw = raw_buf[:, j % 3, f * T:(f + 1) * T - back]
                        acc = conv_buf[:, j % 3, f * T + back:(f + 1) * T]
                        tap = cst[:, bass.ds(k + width - 1 - back, 1)]
                        if back == 0:
                            dve_step.up(ts(acc, raw, tap, cst[:, bass.ds(k + width, 1)], ALU.mult, ALU.add))
                            done[f] = dve_step.value()
                            continue
                        dve.wait_ge(dve_step.sem, done[f])
                        last = stt(acc, raw, tap, acc, ALU.mult, ALU.add)
                        if back == width - 1:
                            last.then_inc(conv_tail, 1)
                        else:
                            dve_step.up(last)
                            done[f] = dve_step.value()

            def cffn(g):
                began = tails[0]

                def chunk(j, i=0, c=0):
                    dve.wait_ge(evacuated, chunk_read(g, j) + 3 * i)
                    ahead = split_next(g.split + 4 * j)
                    taps(j, f"conv{g.nth}", c, (2, 3), 3)
                    split(ahead[:2], i)
                    taps(j, f"conv{g.nth}", c, (0, 1), 3)
                    split(ahead[2:], i)
                    dve.wait_ge(gated, g.gated + j + 1 + 3 * i)
                    dve.wait_ge(conv_tail, began + 4 * j + 4 + 12 * i)
                    tt(hT_flat[:, bass.ds(c * 2 * T, 2 * T)], conv_buf[:, j % 3, 0:2 * T],
                       conv_buf[:, j % 3, 2 * T:4 * T], ALU.mult).then_inc(hidden, 1)
                    split_hidden(g, j, i, c)

                turns = g.chunks // 3
                with rounds(dve, turns, (dve_step, 24)) as i:
                    for j in range(3):
                        chunk(j, i, 3 * i + j)
                for j in range(3 * turns, g.chunks):
                    chunk(j, 0, j)
                tails[0] += 4 * g.chunks

            def conv_chunks(g, weights):
                with rounds(dve, 2, (dve_step, 36)) as i:
                    for j in range(3):
                        dve.wait_ge(evacuated, chunk_read(g, j) + 3 * i)
                        ahead = split_next(g.split + 4 * j)
                        taps(j, weights, 3 * i + j, (0, 1), 4)
                        split(ahead[:2], i)
                        taps(j, weights, 3 * i + j, (2, 3), 4)
                        split(ahead[2:], i)
                tails[0] += 24

            def gdn(g):
                conv_chunks(g, "gdn_conv")
                for c in range(6, g.chunks):
                    split(split_next(g.split + 4 * c))
                dve.wait_ge(ba_done, 1)
                a_dt = heads("a_dt", 8).unsqueeze(1).to_broadcast([P, NT, 8])
                u, arg = gd_u[:, :, 0:8], gd_arg[:, :, 0:8]
                chain(nc.vector.tensor_copy(gd_ba[:, :, :].rearrange("p t n -> p (t n)"), ps[:, 6, 0:32]))
                chain(tt(u, gd_ba[:, :, 8:16], a_dt, ALU.add))
                chain(ts(arg, u, -1.0, None, ALU.mult))
                tt(arg, arg, u, ALU.min).then_inc(g_arg, 1)
                for n in range(8):
                    dve.wait_ge(q_root, n + 1)
                    root = gd_root[:, n % 2, :]
                    chain(nc.vector.reciprocal(root, root))
                    v = gd_in[:, 2 * n:2 * n + 2, :].rearrange("p f t -> p (f t)")
                    stt(v, v, P ** -0.5 if n < 4 else 1.0, root, ALU.mult, ALU.mult).then_inc(q_normed, 1)
                dve.wait_ge(g_log, 1)
                chain(stt(u, u, 0.0, arg, ALU.max, ALU.add))
                chain(ts(gd_beta[:, :, 0:8], gd_ba[:, :, 0:8], 1.0, None, ALU.add))
                chain(nc.vector.reciprocal(gd_beta[:, :, 0:8], gd_beta[:, :, 0:8]))
                rate = gd_rate.unsqueeze(1).to_broadcast([P, NT, 8])
                stt(gd_g[:, :, 0:8], u, -1.0, rate, ALU.mult, ALU.mult).then_inc(g_ready, 1)
                dve.wait_ge(g_cums_done, 1)
                chain(nc.vector.tensor_copy(gd_gc[:, :, 0:8], ps[:, 7, 0:16].rearrange("p (t h) -> p t h", t=NT)))
                tt(gd_kdec, ps[:, 7, 16:24], gd_gc[:, 0, 0:8], ALU.subtract).then_inc(g_cums_ready, 1)

                def exponents(i):
                    t, h = i // 2, i % 2 * 4
                    dve.wait_ge(g_rows_done, i + 1)
                    for r in range(4):
                        last = ts(gd_off[:, i, r * P:(r + 1) * P], ps[:, i % 2, r * P:(r + 1) * P],
                                  gd_gc[:, t, h + r:h + r + 1], 0.0, ALU.subtract, ALU.min)
                    last.then_inc(g_diff, 1)
                    tokens = slice(t * P, (t + 1) * P)
                    tt(gd_kb[:, h:h + 4, tokens], gd_in[:, G_K + h:G_K + h + 4, tokens],
                       ps[:, 2 + i % 2, :].rearrange("p (r n) -> p r n", r=4), ALU.mult).then_inc(kb_ready, 1)

                def attention_of(i):
                    t, h = i // 2, i % 2 * 4
                    dve.wait_ge(g_decay, i + 1)
                    decay = gd_off[:, i, :].rearrange("p (r n) -> p r n", r=4)
                    chain(tt(decay, decay, const("upper").unsqueeze(1).to_broadcast([P, 4, P]), ALU.mult))
                    dve.wait_ge(kq_done, i + 1)
                    dve_step.up(tt(gd_LT[:, i, :], ps[:, 4, :], gd_off[:, i, :], ALU.mult))
                    tt(gd_attT[:, t, h * P:(h + 4) * P], ps[:, 5, :], gd_off[:, i, :], ALU.mult)\
                        .then_inc(att_ready, 1)

                def by_token(i):
                    dve.wait_ge(v_turned, i + 1)
                    t, h = i // 2, i % 2 * 4
                    if i < 4:
                        to, factor = gd_vb[:, 8 * t + h:8 * t + h + 4, :], gd_beta[:, t, h:h + 4]
                    else:
                        if i == 4:
                            dve.wait_ge(kdec_ready, 1)
                        h = (i - 4) * 4
                        to, factor = gd_kd[:, h:h + 4, :], gd_kdec[:, h:h + 4]
                    tt(to, ps[:, 6, :].rearrange("p (r n) -> p r n", r=4),
                       factor.unsqueeze(2).to_broadcast([P, 4, P]), ALU.mult).then_inc(v_ready, 1)

                exponents(0)
                exponents(1)
                for i in range(4):
                    by_token(i)
                    attention_of(i)
                    if i < 2:
                        exponents(i + 2)
                by_token(4)
                by_token(5)
                eye = ident.unsqueeze(1).to_broadcast([P, 4, P])
                for i in range(4):
                    off, inv, invT = (v[:, i, :].rearrange("p (r n) -> p r n", r=4)
                                      for v in (gd_off, gd_inv, gd_invT))
                    dve.wait_ge(off_ready, i + 1)
                    tt(invT, eye, off, ALU.subtract).then_inc(invT_ready, 1)
                    dve.wait_ge(off_used, i + 1)
                    tt(inv, eye, ps[:, i % 2, :].rearrange("p (r n) -> p r n", r=4),
                       ALU.subtract).then_inc(inv_ready, 1)
                for half in range(2):
                    h = half * 4
                    growth = gd_grow[:, h:h + 4, :]
                    query, key = gd_in[:, G_Q + h:G_Q + h + 4, P:T], gd_kb[:, h:h + 4, P:T]
                    dve_step.up(tt(query, query, growth, ALU.mult))
                    tt(key, key, growth, ALU.mult).then_inc(grown_ready, 1)
                with dve.Fori(1, LEVELS) as level:
                    for i in range(4):
                        dve.wait_ge(inv_terms, (level - 1) * 4 + i + 1)
                        tt(gd_inv[:, i, :], gd_inv[:, i, :], ps[:, 2 + i % 2, :], ALU.subtract).then_inc(inv_ready, 1)
                        tt(gd_invT[:, i, :], gd_invT[:, i, :], ps[:, 4 + i % 2, :],
                           ALU.subtract).then_inc(invT_ready, 1)
                for half in range(2):
                    dve.wait_ge(carried_done, half + 1)
                    tt(gd_rhs[:, half * 4:half * 4 + 4, :], gd_vb[:, 8 + half * 4:12 + half * 4, :],
                       ps[:, 4 + half, :].rearrange("p (r n) -> p r n", r=4), ALU.subtract).then_inc(rhs_ready, 1)
                for n in range(4):
                    dve.wait_ge(o_root, n + 1)
                    root, o = gd_oroot[:, n % 2, :], hT_flat[:, 2 * n * T:(2 * n + 2) * T]
                    dve_step.up(stt(o, ps[:, (6, 7, 2, 3)[n], :], const("gdn_gain"),
                                    gd_z[:, 2 * n:2 * n + 2, :].rearrange("p f t -> p (f t)"), ALU.mult, ALU.mult))
                    chain(nc.vector.reciprocal(root, root))
                    tt(o, o, root, ALU.mult).then_inc(mixed, 1)

            def chain(instruction):
                dve_step.up(instruction)
                dve_step.wait(dve)

            def attend(a, g):
                def maxima(j):
                    n, b = a.jobs[j]
                    group, qb = a.quads[n]
                    keys = (qb + 1) * P
                    if j >= 2:
                        dve.wait_ge(a.turned, a.turns.index(a.jobs[j - 2]) + 1)
                    dve.wait_ge(a.scored, j + 1)
                    mask = const(a.mask, 2 * P - keys, 2 * P).unsqueeze(1).to_broadcast([P, 4, keys])
                    tt(a.prob(j), a.scores(j), mask, ALU.add).then_inc(a.masked, 1)
                    dve.wait_ge(a.masked, j + 1)
                    m = max_buf[:, j, :]
                    chain(nc.vector.tensor_reduce(m, a.prob(j), AX.X, ALU.max))
                    if a.kind == "swa":
                        sinks = heads("sinks", 16)[:, 4 * group:4 * group + 4]
                        chain(stt(m, m, SCALE, sinks, ALU.mult, ALU.max))
                        chain(ts(m, m, -1.0, None, ALU.mult))
                        tt(sink_buf[:, j, :], sinks, m, ALU.add).then_inc(a.maxed, 1)
                    else:
                        ts(m, m, -SCALE, None, ALU.mult).then_inc(a.maxed, 1)

                def normalise(j):
                    n, b = a.jobs[j]
                    group, qb = a.quads[n]
                    keys = (qb + 1) * P
                    dve.wait_ge(a.exped, j + 1)
                    inv = inv_buf[:, j, :]
                    if a.kind == "swa":
                        chain(tt(sum_buf[:, j, :], sum_buf[:, j, :], sink_buf[:, j, :], ALU.add))
                    chain(nc.vector.reciprocal(inv, sum_buf[:, j, :]))
                    if a.kind == "nsa":
                        at = group * 4 * 3 + 1 + b
                        chain(tt(inv, inv, gates_buf[:, qb, at:at + 10:3], ALU.mult))
                    tt(a.prob(j), a.prob(j), inv.unsqueeze(2).to_broadcast([P, 4, keys]),
                       ALU.mult).then_inc(a.probs, 1)

                maxima(0)
                for j in range(len(a.jobs)):
                    if j + 1 < len(a.jobs):
                        maxima(j + 1)
                    normalise(j)

            def swa(g):
                for c in range(g.chunks):
                    split(split_next(g.split + 4 * c))
                attend(attention["swa"], g)

            def nsa(g):
                for c in range(g.chunks):
                    split(split_next(g.split + 4 * c))
                dve.wait_ge(pairs_landed, 16 * 8)
                for kv in range(2):
                    for m in range(16):
                        last = ts(cmp_in[:, kv, m, :].rearrange("p (v c) -> p v c", v=GROUPS),
                                  token_pairs[:, kv, :, m:m + 8 * (NC - 1) + 1:8],
                                  const("pos", kv * 16 + m, kv * 16 + m + 1), None, ALU.add)
                    last.then_inc(cmp_in_ready, 1)
                keep = const("cmp_keep").rearrange("p (t c) -> p t c", t=NT)
                chain(ts(cmp_drop, keep, 1.0, -MASKED, ALU.subtract, ALU.mult))
                dve.wait_ge(unit_done, units_until(g.extra + 1))
                h, s, u = (cmp_hidden[:, n, :] for n in (1, 3, 2))
                chain(nc.vector.tensor_copy(h.rearrange("p (v n) -> p v n", v=2), ps[:, 4:6, 0:2 * NG]))
                chain(tt(s, h, h, ALU.mult))
                chain(ts(s, s, 0.044715, 1.0, ALU.mult, ALU.add))
                tt(u, s, h, ALU.mult).then_inc(tanh_in, 1)
                dve.wait_ge(tanh_done, 1)
                chain(ts(u, u, 1.0, 0.5, ALU.add, ALU.mult))
                tt(cmp_hidden[:, 0, :], u, h, ALU.mult).then_inc(gelu_done, 1)
                dve.wait_ge(cmp_scored, 1)
                for t in range(NT):
                    p = cmp_prob[:, t, :, 0:NC]
                    drop = cmp_drop[:, t, 0:NC].unsqueeze(1).to_broadcast([P, 16, NC])
                    m = cmp_max[:, t, :]
                    mask = keep[:, t, 0:NC].unsqueeze(1).unsqueeze(1).to_broadcast([P, 2, 4, NC])
                    by_half = cmp_prob[:, t, :, :].rearrange("p (a e r) c -> p e a r c", a=2, e=2)
                    for e in range(2):
                        scored = ps[:, 4 + e, t * 128:(t + 1) * 128].rearrange("p (a r c) -> p a r c", a=2, r=4)
                        dve_step.up(tt(by_half[:, e, :, :, 0:NC], scored[:, :, :, 0:NC], mask, ALU.mult))
                    dve_step.wait(dve)
                    chain(tt(p, p, drop, ALU.add))
                    chain(nc.vector.tensor_reduce(m, p, AX.X, ALU.max))
                    tt(p, p, m.unsqueeze(2).to_broadcast([P, 16, NC]), ALU.subtract).then_inc(cmp_centered, 1)
                dve.wait_ge(gates_ready, 1)
                for t in range(NT):
                    p = cmp_prob[:, t, :, 0:NC]
                    mask = keep[:, t, 0:NC].unsqueeze(1).to_broadcast([P, 16, NC])
                    total = cmp_sum[:, t, :]
                    dve.wait_ge(cmp_exped, t + 1)
                    chain(nc.vector.tensor_reduce(total, p, AX.X, ALU.add))
                    chain(nc.vector.reciprocal(total, total))
                    chain(tt(total, total, gates_buf[:, t, 0:46:3], ALU.mult))
                    chain(tt(p, p, mask, ALU.mult))
                    tt(p, p, total.unsqueeze(2).to_broadcast([P, 16, NC]), ALU.mult).then_inc(cmp_ready, 1)
                attend(attention["nsa"], g)

            def ssd(g):
                conv_chunks(g, "ssd_conv")
                for c in range(6, g.chunks):
                    split(split_next(g.split + 4 * c))
                dve.wait_ge(dt_done, 1)
                bias = heads("ssd_dt", 32).unsqueeze(1).to_broadcast([P, NT, 32])
                u, e, dt, dta = (v.rearrange("p (t h) -> p t h", t=NT) for v in (ssd_u, ssd_e, ssd_dt, ssd_dta))
                chain(tt(u, ps[:, 6, 0:64].rearrange("p (t h) -> p t h", t=NT), bias, ALU.add))
                chain(ts(ssd_misc, ssd_u, -1.0, None, ALU.mult))
                tt(ssd_e, ssd_u, ssd_misc, ALU.min).then_inc(dt_arg, 1)
                dve.wait_ge(dt_log, 1)
                chain(stt(ssd_dt, ssd_u, 0.0, ssd_e, ALU.max, ALU.add))
                rate = ssd_ea.unsqueeze(1).to_broadcast([P, NT, 32])
                stt(dta, dt, -1.0, rate, ALU.mult, ALU.mult).then_inc(dta_ready, 1)

                def times_dt(m):
                    t, gg = m // 4, m % 4
                    dve.wait_ge(x_turned, m + 1)
                    by_head = dt[:, t, 8 * gg:8 * gg + 8].unsqueeze(2).to_broadcast([P, 8, HD])
                    tt(xdt_parts[t][gg].rearrange("p (h d) -> p h d", h=8),
                       ps[:, 2 + m % 2, :].rearrange("p (h d) -> p h d", h=8), by_head,
                       ALU.mult).then_inc(xdt_ready, 1)

                times_dt(0)
                times_dt(1)
                dve.wait_ge(cums_done, 1)
                chain(nc.vector.tensor_copy(ssd_acs, ps[:, 7, 0:64]))
                tt(ssd_dec, ps[:, 7, 64:96], ssd_acs[:, 0:32], ALU.subtract).then_inc(cums_ready, 1)
                times_dt(2)
                times_dt(3)
                for t in range(NT):
                    dve.wait_ge(cb_done, t + 1)
                    tt(ssd_cb[:, 4 * t:4 * t + 4, :], ps[:, t, :].rearrange("p (g n) -> p g n", g=4),
                       const("upper").unsqueeze(1).to_broadcast([P, 4, P]), ALU.mult).then_inc(cb_ready, 1)
                dve.wait_ge(cums_exp, 1)
                dve.wait_ge(xdt_ready, 4)
                for gg in range(4):
                    by_head = ssd_dec[:, 8 * gg:8 * gg + 8].unsqueeze(2).to_broadcast([P, 8, HD])
                    tt(ssd_xdec[:, gg * 512:(gg + 1) * 512].rearrange("p (h d) -> p h d", h=8),
                       xdt_parts[0][gg].rearrange("p (h d) -> p h d", h=8), by_head,
                       ALU.mult).then_inc(xdec_ready, 1)
                for m in range(4, 8):
                    times_dt(m)

                def exponents(k):
                    t, h = k // 8, k % 8 * 4
                    dve.wait_ge(rows_done, k + 1)
                    if k >= 4:
                        dve.wait_ge(y_half, k - 3)
                    for r in range(4):
                        column = ssd_acs[:, t * 32 + h + r:t * 32 + h + r + 1]
                        last = ts(ssd_w[:, k % 4, r * P:(r + 1) * P], ps[:, k % 2, r * P:(r + 1) * P], column, 0.0,
                                  ALU.subtract, ALU.min)
                    last.then_inc(diff_ready, 1)

                def weights(k):
                    t, gg = k // 8, k % 8 // 2
                    dve.wait_ge(decay_ready, k + 1)
                    w = ssd_w[:, k % 4, :].rearrange("p (r n) -> p r n", r=4)
                    tt(w, w, ssd_cb[:, 4 * t + gg, :].unsqueeze(1).to_broadcast([P, 4, P]),
                       ALU.mult).then_inc(w_ready, 1)

                def outputs(m):
                    t, gg = m // 4, m % 4
                    y = ssd_y[:, m % 2, :]
                    if m >= 2:
                        dve.wait_ge(y_turned, m - 1)
                    dve.wait_ge(y_half, 2 * m + 2)
                    if t == 0:
                        nc.vector.tensor_copy(y, ps[:, 2 + m % 2, :]).then_inc(y_out, 1)
                        return
                    dve.wait_ge(y_done, m - 3)
                    grown = ssd_misc[:, 8 * gg:8 * gg + 8].unsqueeze(2).to_broadcast([P, 8, HD])
                    chain(tt(y.rearrange("p (h d) -> p h d", h=8), ps[:, 4, :].rearrange("p (h d) -> p h d", h=8),
                             grown, ALU.mult))
                    tt(y, y, ps[:, 2 + m % 2, :], ALU.add).then_inc(y_out, 1)

                def gate(m):
                    t, gg = m // 4, m % 4
                    tokens = slice(t * P, (t + 1) * P)
                    dve.wait_ge(y_turned, m + 1)
                    for f in range(4):
                        last = stt(hT[:, 4 * gg + f, tokens], ssd_in[:, S_X + 4 * gg + f, tokens],
                                   const("ssd_skip", 4 * gg + f, 4 * gg + f + 1), ps[:, 5, f * P:(f + 1) * P],
                                   ALU.mult, ALU.add)
                    last.then_inc(y_turned_out, 1)
                    dve.wait_ge(y_turned_out, m + 1)
                    y = hT[:, 4 * gg:4 * gg + 4, tokens]
                    tt(y, y, ssd_z[:, 4 * gg:4 * gg + 4, tokens], ALU.mult).then_inc(y_gated, 1)

                dve.wait_ge(evacuated, chunk_read(g, g.chunks - 1))
                exponents(0)
                for k in range(16):
                    if k + 1 < 16:
                        exponents(k + 1)
                    weights(k)
                    if k % 2 == 1:
                        if k >= 3:
                            outputs(k // 2 - 1)
                        if k >= 5:
                            gate(k // 2 - 2)
                gate(6)
                outputs(7)
                gate(7)
                for gg in range(4):
                    dve.wait_ge(y_root, gg + 1)
                    chain(nc.vector.reciprocal(ssd_root[:, gg, :], ssd_root[:, gg, :]))
                    for f in range(4 * gg, 4 * gg + 4):
                        stt(hT[:, f, :], hT[:, f, :], const("ssd_gain", f, f + 1), ssd_root[:, gg, :],
                            ALU.mult, ALU.mult).then_inc(mixed, 1)

            dve_mixer = {"gdn": gdn, "swa": swa, "nsa": nsa, "ssd": ssd}

            def residual(g, t):
                if t == 0:
                    dve.wait_ge(first_rows_done, g.s + 1)
                else:
                    dve.wait_ge(unit_done, units_until(g.down + g.down_units - 1))
                product = ps_flat[:, (4 + 2 * t) * BANK:(6 + 2 * t) * BANK]
                event = ("residual", g.s)
                if g.kind in ("nsa", "cffn", "ssd"):
                    column = rstd(("post", g.s, t))
                    n = row_at[event]
                    dve.wait_ge(row_landed[n % 2], 16 * (n // 2 + 1))
                    dve_step.up(stt(xn[:, t, :], product, column, row[:, n % 2, :], ALU.mult, ALU.mult))
                    dve_step.wait(dve)
                    tt(x[:, t, :], x[:, t, :], xn[:, t, :], ALU.add).then_inc(x_ready, 1)
                elif g.kind == "swiglu":
                    stt(x[:, t, :], product, 0.5, x[:, t, :], ALU.mult, ALU.add).then_inc(x_ready, 1)
                else:
                    tt(x[:, t, :], product, x[:, t, :], ALU.add).then_inc(x_ready, 1)

            def output_bias(g):
                n = row_at[("residual", g.s)]
                dve.wait_ge(row_landed[n % 2], 16 * (n // 2 + 1))
                for t in range(NT):
                    dve_step.up(tt(x[:, t, :], x[:, t, :], row[:, n % 2, :], ALU.add))
                dve_step.wait(dve)

            dve.wait_ge(early_loaded, 16)
            dve.wait_ge(x_loaded, 16 * NT)
            for t in range(NT):
                norm(0, t)
            for g in stages:
                first = split_first(g.split) if g.s == 0 or g.own_ring else []
                split(first[:1])
                turned_out(g)
                split(first[1:] if first else split_next(g.split - 4))
                if g.s == 0:
                    dve.wait_ge(cst_loaded, 16)
                if g.kind == "swiglu":
                    swiglu(g)
                elif g.kind == "cffn":
                    cffn(g)
                else:
                    dve_mixer[g.kind](g)
                    if g.kind == "swa":
                        output_bias(g)
                    split_mixed(g)
                for v in range(g.down_units - 1):
                    split(split_next(g.split_down + 4 * v))
                for t in range(NT):
                    residual(g, t)
                    if g.norm == FINAL_AFTER:
                        column = rstd(("final", g.s, t))
                        n = row_at[("final", g.s)]
                        dve.wait_ge(row_landed[n % 2], 16 * (n // 2 + 1))
                        stt(x[:, t, :], x[:, t, :], column, row[:, n % 2, :],
                            ALU.mult, ALU.mult).then_inc(x_ready, 1)
                    if g.s < last_stage:
                        norm(g.s + 1, t)

        @block.gpsimd
        def _(pool):
            def load_row(n):
                r, _ = row_uses[n]
                if n >= 2:
                    pool.wait_ge(x_ready, x_after[row_uses[n - 2][1], NT - 1])
                pool.dma_start(row[:, n % 2, :], rows[r:r + 1, :].to_broadcast([P, D]))\
                    .then_inc(row_landed[n % 2], 16)

            def gdn(g):
                masks = CONST_AT["levels"]
                for level in range(LEVELS):
                    masks = CONST_AT["levels"] + level * P
                    mask = cst[:, masks:masks + P].unsqueeze(1).to_broadcast([P, 4, P])
                    for i in range(4):
                        if level == 0:
                            pool.wait_ge(att_ready, i + 1)
                        else:
                            pool.wait_ge(off_used, (level - 1) * 4 + i + 1)
                            pool.wait_ge(invT_ready, i + 1)
                        v, off = (b[:, i, :].rearrange("p (r n) -> p r n", r=4) for b in (gd_LT, gd_off))
                        nc.gpsimd.tensor_tensor(off, v, mask, ALU.mult).then_inc(off_ready, 1)

            def nsa(g):
                pool.wait_ge(evacuated, chunk_read(g, 2))
                for kv in range(2):
                    for half in range(2):
                        for parity in range(2):
                            pool.dma_start(token_pairs[parity * HD:(parity + 1) * HD, kv, half:half + 3:2, :],
                                           mix_tiles[half * HD:(half + 1) * HD, 8 + 2 * kv:10 + 2 * kv,
                                                     parity * P:(parity + 1) * P]).then_inc(pairs_landed, 16)

            pool_mixer = {"gdn": gdn, "nsa": nsa}

            for n in range(min(2, len(row_uses))):
                load_row(n)
            loaded = min(2, len(row_uses))
            for g in stages:
                if g.kind in pool_mixer:
                    pool_mixer[g.kind](g)
                while loaded < len(row_uses) and row_uses[loaded - 2][1][1] <= g.s:
                    load_row(loaded)
                    loaded += 1


def column_tiles(v):
    return v.reshape(-1, P).T


def up_units(w, columns):
    w = w[:, columns]
    n = w.shape[1] // 512
    return w.reshape(KD, P, n, 4, P).transpose(2, 1, 3, 0, 4).reshape(n, P, UNIT)


def down_units(w):
    kts = w.shape[0] // P
    n = -(-kts // 4)
    padded = np.zeros((4 * n, P, D), w.dtype)
    padded[:kts] = w.reshape(kts, P, D)
    return padded.reshape(n, 4, P, D).transpose(0, 2, 1, 3).reshape(n, P, UNIT)


def paired(n_tiles=FK):
    return np.arange(2 * FF).reshape(2, FF // 256, 256).transpose(1, 0, 2).ravel()


def head_order():
    return np.arange(16 * HD).reshape(2, 2, 4, HD).transpose(0, 2, 1, 3).ravel()


def weights_of(a, kind, nth):
    if kind == "swiglu":
        which, layer = ("ffn1", "ffn2")[nth % 2], nth // 2
        yield up_units(a[which + "_w_gu"][layer], paired())
        yield down_units(a[which + "_w_down"][layer])
    elif kind == "cffn":
        yield up_units(a["ffn_w_up_2"][nth], paired())
        yield down_units(a["ffn_w_down_2"][nth])
    elif kind == "gdn":
        yield up_units(a["a_w_in"][0], np.arange(4096))
        yield down_units(a["a_w_out"][0])
    elif kind == "swa":
        yield up_units(a["b_w_in"][0], np.concatenate([head_order(), np.arange(1024, 1536)]))
        yield down_units(a["b_w_out"][0][head_order()])
    elif kind == "nsa":
        yield up_units(a["nsa_w_in_2"][0], np.concatenate([head_order(), np.arange(1024, 2560)]))
        yield a["nsa_cmp_w1_2"][0].reshape(2, 16, P, 256).transpose(0, 2, 1, 3).reshape(2, P, UNIT)
        yield down_units(a["nsa_w_out_2"][0][head_order()])
    elif kind == "ssd":
        yield up_units(a["ssd_w_in_2"][0], np.concatenate([np.arange(2048, 5120), np.arange(2048)]))
        yield down_units(a["ssd_w_out_2"][0])


def const_parts(a):
    key, query = np.arange(P)[:, None], np.arange(P)[None, :]
    f = np.float32
    zeros = np.zeros
    c = {"ident": (key == query).astype(f), "ones": np.ones((P, P), f), "upper": (key <= query).astype(f)}
    norms = [a["ffn1_norm"][0], a["mix_norm"][0], a["ffn2_norm"][0], a["ffn1_norm"][1], a["mix_norm"][1],
             a["ffn2_norm"][1]] + [a["norm_gains_2"][i][n] for i in range(2) for n in (0, 2)]
    c["norms"] = np.concatenate([column_tiles(v) for v in norms], 1)
    over_heads = np.concatenate([a["a_A_log"][0], a["a_dt_bias"][0], a["b_sinks"][0], a["ssd_dt_bias_2"][0],
                                 a["ssd_a_log_2"][0]])
    c["heads"] = np.broadcast_to(over_heads, (P, 96))

    def conv(w, b, order):
        wb = np.concatenate([w, b[None]])[:, order]
        return wb.reshape(len(wb), -1, P).transpose(2, 1, 0).reshape(P, -1)

    c["gdn_conv"] = conv(a["a_w_conv"][0], zeros(3072, f), np.arange(3072))
    c["ssd_conv"] = conv(a["ssd_conv_w_2"][0], a["ssd_conv_b_2"][0], np.arange(3072))
    for n in range(2):
        c[f"conv{n}"] = conv(a["ffn_conv_w_2"][n], a["ffn_conv_b_2"][n], paired())
    c["gdn_gain"] = column_tiles(a["a_out_norm"][0])

    def narrow(w):
        return w.reshape(KD, P, -1).transpose(1, 0, 2).reshape(P, -1)

    c["w_ba"] = narrow(a["a_w_in"][0][:, 4096:])
    c["w_gates"] = narrow(a["nsa_w_in_2"][0][:, 2560:])
    c["w_dt"] = narrow(a["ssd_w_in_2"][0][:, 5120:])
    levels = []
    for n in range(LEVELS):
        half = 1 << n
        levels.append((key // (2 * half) == query // (2 * half)) & (key // half % 2 == 0) & (query // half % 2 == 1))
    c["levels"] = np.concatenate(levels, 1).astype(f)
    c["swa_bias"] = column_tiles(a["b_b_in"][0][np.concatenate([head_order(), np.arange(1024, 1536)])])
    q, k = np.arange(P)[:, None], np.arange(P)[None, :]
    c["window"] = np.where(np.concatenate([k > q, k <= q], 1), 0.0, MASKED).astype(f)
    c["causal"] = np.where(np.concatenate([k > -1 + 0 * q, k <= q], 1), 0.0, MASKED).astype(f)
    keep = np.zeros((P, NT, 16), f)
    for t in range(NT):
        keep[:, t, :NC] = np.arange(NC)[None] * 16 + 31 <= t * P + np.arange(P)[:, None]
    c["cmp_keep"] = keep.reshape(P, -1)
    c["pos"] = a["nsa_cmp_pos_2"][0].reshape(2, 16, P).transpose(2, 0, 1).reshape(P, -1)
    w2 = a["nsa_cmp_w2_2"][0].reshape(2, 2, P, HD)
    c["w_cmp2"] = np.concatenate([w2, w2], 3).transpose(2, 0, 1, 3).reshape(P, -1)
    c["ssd_gain"] = column_tiles(a["ssd_norm_w_2"][0])
    c["ssd_skip"] = column_tiles(np.repeat(a["ssd_d_2"][0], HD))
    return c


def prepare(a, plan=PLAN):
    units = np.concatenate([u for kind, nth in plan for u in weights_of(a, kind, nth)])
    parts = const_parts(a)
    consts = np.concatenate([parts[name] for name, _ in CONST], 1)
    rows = np.stack([a["b_b_out"][0], a["final_norm"], a["norm_gains_2"][0][1], a["norm_gains_2"][0][3],
                     a["norm_gains_2"][1][1], a["norm_gains_2"][1][3]])
    return {"units": units, "consts": consts, "rows": rows, "x_in": np.ascontiguousarray(a["x"][0])}


def kernel(**inputs):
    from concourse import bacc
    from concourse.bass_utils import run_bass_kernel_spmd

    arrays = prepare({name: np.asarray(v) for name, v in inputs.items()})
    nc = bacc.Bacc("TRN2", target_bir_lowering=False, num_devices=1)
    drams = {n: nc.dram_tensor(n, v.shape, mybir.dt.from_np(v.dtype), kind="ExternalInput").ap()
             for n, v in arrays.items()}
    out = nc.dram_tensor("out", (T, D), F32, kind="ExternalOutput").ap()
    build_program(nc, drams["units"], drams["consts"], drams["rows"], drams["x_in"], out, PLAN)
    result = run_bass_kernel_spmd(nc, [arrays], core_ids=[0])
    return result.results[0]["out"].reshape(1, T, D)
```

```python
from contextlib import ExitStack, contextmanager

import numpy as np

import concourse.bass as bass
from concourse import mybir

ACT = mybir.ActivationFunctionType
ALU = mybir.AluOpType
AX = mybir.AxisListType
F32 = mybir.dt.float32
F32R = mybir.dt.float32r

P = 128
T = 256
NT = T // P
D = 1024
KD = D // P
FF = 2816
FK = FF // P
UNIT = 4096
SLOTS = 3
QUARTER = UNIT // 4
ROUNDED = 6
BANK = 512
ARENA = 19968
EPS = 1e-6
MASKED = -1e30

HEADS_A = 8
GROUPS = 4
HD = 64
NC = 15
SSD_HEADS = 32
LEVELS = 7

CHUNKS = {"swiglu": 11, "gdn": 8, "swa": 3, "nsa": 5, "cffn": 11, "ssd": 10}
EXTRA = {"nsa": 2}
DOWN = {"swiglu": 22, "gdn": 8, "swa": 8, "nsa": 8, "cffn": 22, "ssd": 16}
PLAN = [("swiglu", 0), ("gdn", 0), ("swiglu", 1), ("swiglu", 2), ("swa", 0), ("swiglu", 3),
        ("nsa", 0), ("cffn", 0), ("ssd", 0), ("cffn", 1)]
FINAL_AFTER = 5

CONST = [("ident", P), ("norms", 10 * KD), ("ones", P), ("upper", P), ("heads", 96),
         ("gdn_conv", 24 * 5), ("gdn_gain", 1), ("w_ba", KD * 16), ("levels", LEVELS * P),
         ("swa_bias", 12), ("window", 2 * P), ("causal", 2 * P), ("cmp_keep", NT * 16),
         ("w_gates", KD * 48), ("pos", 2 * 16), ("w_cmp2", 2 * 2 * P),
         ("conv0", 44 * 4), ("conv1", 44 * 4), ("ssd_conv", 24 * 5), ("w_dt", KD * 32),
         ("ssd_gain", 16), ("ssd_skip", 16)]
CONST_AT, CONST_N = {}, 0
for _name, _width in CONST:
    CONST_AT[_name] = CONST_N
    CONST_N += _width
HEAD_AT = {"a_log": 0, "a_dt": 8, "sinks": 16, "ssd_dt": 32, "ssd_a": 64}
ROWS = {("swa", 0): 0, "final": 1, ("nsa", 0): 2, ("cffn", 0): 3, ("ssd", 0): 4, ("cffn", 1): 5}


class Tally:

    def __init__(self, sem):
        self.sem, self.at, self.turns = sem, 0, 0

    def up(self, instruction, n=1):
        instruction.then_inc(self.sem, n)
        self.at += n
        return instruction

    def value(self):
        return self.at + self.turns

    def wait(self, engine):
        engine.wait_ge(self.sem, self.value())


@contextmanager
def rounds(engine, n, *raised):
    began = [t.at for t, _ in raised]
    with engine.Fori(0, n) as i:
        for t, per in raised:
            t.turns = i * per
        yield i
        for (t, per), at in zip(raised, began):
            assert t.at - at == per, (t.at - at, per)
    for (t, per), at in zip(raised, began):
        t.turns, t.at = 0, at + n * per


class Stage:
    pass


class Quarter:

    def __init__(self, unit, q, place, early, count):
        self.unit, self.q, self.place, self.early, self.count = unit, q, place, early, count


def lay_out_quarters(stages):
    quarters = {}
    for g in stages:
        for unit, place, n, early in ((g.unit, g.split, 4 * g.chunks, g.own_ring),
                                      (g.down, g.split_down, g.k_tiles, False)):
            for q in range(n):
                quarters[place + q] = Quarter(unit + q // 4, q % 4, place + q, early, len(quarters) + 1)
    return quarters


def lay_out(plan):
    stages, unit, chunk, gated, hidden, split, rest = [], 0, 0, 0, 0, 0, 0
    for s, (kind, nth) in enumerate(plan):
        g = Stage()
        g.kind, g.nth, g.s = kind, nth, s
        g.chunks, g.k_tiles = CHUNKS[kind], DOWN[kind]
        g.norm = PLAN.index((kind, nth))
        g.unit, g.chunk, g.gated, g.hidden = unit, chunk, gated, hidden
        g.extra = g.unit + g.chunks
        g.down = g.extra + EXTRA.get(kind, 0)
        g.down_units = -(-g.k_tiles // 4)
        g.split = split
        g.split_down = split + 4 * g.chunks
        split = g.split_down + 4 * g.down_units
        g.rest = rest
        rest += g.k_tiles // 2
        g.own_ring = kind not in ("swiglu", "cffn")
        unit = g.down + g.down_units
        chunk += g.chunks
        gated += g.chunks if kind in ("swiglu", "cffn") else 0
        hidden += g.chunks if kind == "cffn" else 0
        stages.append(g)
    return stages, unit


def build_program(nc, units, consts, rows, x_in, out, plan):
    stages, n_units = lay_out(plan)
    quarters = lay_out_quarters(stages)
    last_stage = len(stages) - 1

    events, changes = [], []
    for g in stages:
        mine = [("residual", g.s)] + [("final", g.s)] * (g.norm == FINAL_AFTER)
        events += mine
        changes += [(event, t) for t in range(NT) for event in mine]
    x_after = {change: n + 1 for n, change in enumerate(changes)}
    deviations = [("norm", 0, t) for t in range(NT)]
    for g in stages:
        for t in range(NT):
            if g.kind in ("nsa", "cffn", "ssd"):
                deviations.append(("post", g.s, t))
            if g.norm == FINAL_AFTER:
                deviations.append(("final", g.s, t))
            if g.s < last_stage:
                deviations.append(("norm", g.s + 1, t))
    deviation_at = {key: n + 1 for n, key in enumerate(deviations)}

    def x_event_before_norm(s, t):
        if s == 0:
            return 0
        event = ("final", s - 1) if stages[s - 1].norm == FINAL_AFTER else ("residual", s - 1)
        return x_after[event, t]

    row_uses = []
    for g in stages:
        if (g.kind, g.nth) in ROWS:
            row_uses.append((ROWS[g.kind, g.nth], ("residual", g.s)))
        if g.norm == FINAL_AFTER:
            row_uses.append((ROWS["final"], ("final", g.s)))
    row_at = {event: n for n, (_, event) in enumerate(row_uses)}

    with ExitStack() as ctx:
        def place(name, at, *shape):
            with ExitStack() as below:
                if at:
                    below.enter_context(nc.sbuf_tensor("below_" + name, [P, at], F32))
                return below.enter_context(nc.sbuf_tensor(name, [P, *shape], F32))

        def sem(name):
            return ctx.enter_context(nc.semaphore(name))

        at = {}
        end = 0
        for name, size in (("ring", SLOTS * UNIT), ("x", NT * D), ("xn", NT * D), ("xT", KD * T),
                           ("xT_rest", KD * T), ("hT", ROUNDED * QUARTER), ("cst", CONST_N), ("row", 2 * D),
                           ("stats", 64), ("arena", ARENA)):
            at[name] = end
            end += size
        ring = place("ring", at["ring"], SLOTS, UNIT)
        ring_rest = place("ring_rest", at["ring"], SLOTS, UNIT)
        x = place("x", at["x"], NT, D)
        xn = place("xn", at["xn"], NT, D)
        xT = place("xT", at["xT"], KD, T)
        xT_rest = place("xT_rest", at["xT_rest"], KD, T)
        spare = place("spare", at["xT"], KD, T)
        narrow_rounded = place("narrow_rounded", at["xn"], KD * 48)
        narrow_rest = place("narrow_rest", at["xn"] + KD * 48, KD * 48)
        junk = place("junk", at["xT_rest"], D)
        hT = place("hT", at["hT"], ROUNDED * QUARTER // T, T)
        hT_rest = place("hT_rest", at["hT"], FK, T)
        early_ring = place("early_ring", at["hT"], ROUNDED, QUARTER)
        mixed_rounded = place("mixed_rounded", at["hT"] + 16 * T, 8, T)
        hT_flat = hT[:, :, :].rearrange("p k t -> p (k t)")
        hT_rest_flat = hT_rest[:, :, :].rearrange("p k t -> p (k t)")
        cst = place("cst", at["cst"], CONST_N)
        row = place("row", at["row"], 2, D)
        stats = place("stats", at["stats"], 64)
        arena = place("arena", at["arena"], ARENA)
        hT_rounded_buf = place("hT_rounded_buf", at["arena"] + 6 * T, FK, T)
        hT_rounded_flat = hT_rounded_buf[:, :, :].rearrange("p k t -> p (k t)")
        weight_ring = place("weight_ring", at["arena"] + (6 + FK) * T, ROUNDED, QUARTER)
        ps = ctx.enter_context(nc.psum_tensor("ps", [P, 8, BANK], F32))
        ps_flat = ps[:, :, :].rearrange("p b n -> p (b n)")

        def const(name, a=0, b=None):
            at = CONST_AT[name]
            return cst[:, at + a:at + (dict(CONST)[name] if b is None else b)]

        def heads(name, n):
            return const("heads", HEAD_AT[name], HEAD_AT[name] + n)

        ident = const("ident")
        ones = const("ones")

        def area(at, *shape):
            n = int(np.prod(shape))
            assert at + n <= ARENA
            v = arena[:, at:at + n]
            if len(shape) == 2:
                v = v.rearrange("p (a b) -> p a b", a=shape[0])
            elif len(shape) == 3:
                v = v.rearrange("p (a b c) -> p a b c", a=shape[0], b=shape[1])
            return v

        gate_buf = area(0, 3, 2 * T)
        raw_buf = area(ARENA - 6 * 4 * T, 3, 4 * T)
        conv_buf = area(ARENA - 3 * 4 * T, 3, 4 * T)

        landed = [sem(f"unit_landed_{j}") for j in range(SLOTS)]
        unit_done = sem("unit_done")
        x_loaded = sem("x_loaded")
        early_loaded = sem("early_loaded")
        cst_loaded = sem("cst_loaded")
        row_landed = [sem(f"row_landed_{j}") for j in range(2)]
        x_ready = sem("x_ready")
        deviation = sem("deviation")
        xn_ready = sem("xn_ready")
        xn_turned = sem("xn_turned")
        xT_ready = sem("xT_ready")
        evacuated = sem("evacuated")
        gated = sem("gated")
        hidden = sem("hidden")
        w_rounded = sem("weights_rounded")
        w_split = sem("weights_split")
        narrow_rounding = sem("narrow_rounding")
        narrow_split = sem("narrow_split")
        xT_rounded = sem("xT_rounded")
        hT_rounded = sem("hT_rounded")
        hT_split = sem("hT_split")
        conv_tail = sem("conv_tail")
        conv_silu = sem("conv_silu")
        first_rows_done = sem("first_rows_done")
        mixed = sem("mixed")
        act_step = Tally(sem("act_step"))
        dve_step = Tally(sem("dve_step"))
        stored = sem("stored")

        def units_until(u):
            return u + 1

        def chunk_read(g, c):
            return 3 + g.chunk + c + 1

        def pair(j):
            return ps_flat[:, 2 * j * BANK:(2 * j + 2) * BANK]

        def quarter(c):
            return ring[:, c.unit % SLOTS, c.q * QUARTER:(c.q + 1) * QUARTER]

        def rest(c):
            return ring_rest[:, c.unit % SLOTS, c.q * QUARTER:(c.q + 1) * QUARTER]

        def rounded(c):
            at = c.place % ROUNDED
            return (early_ring if c.early else weight_ring)[:, at, :]

        def r32(v):
            return v.bitcast(F32R)

        def split_next(place):
            mine = quarters[place]
            found = [quarters.get(place + ROUNDED + n) for n in range(4)]
            return [c for c in found if c and c.early == mine.early]

        def split_first(place):
            return [quarters[place + n] for n in range(ROUNDED)]

        def hT_parts(g):
            return (mixed_rounded if g.kind in ("gdn", "swa", "nsa") else hT_rounded_buf), hT_rest

        def hT_pair(v, n):
            return v[:, 2 * n:2 * n + 2, :].rearrange("p k t -> p (k t)")

        def first_down_steps(g):
            steps = []
            first = split_first(g.split_down)
            for n in range(g.k_tiles // 2):
                steps.append((n, None))
                steps += [(None, c) for c in first[2 * n:2 * n + 2]]
            return steps

        narrow_width = {"gdn": 16, "nsa": 48, "ssd": 32}
        narrow_const = {"gdn": "w_ba", "nsa": "w_gates", "ssd": "w_dt"}
        narrow_counts = {g.s: n + 1 for n, g in enumerate([g for g in stages if g.kind in narrow_width])}

        mixed_raises = {"gdn": 4, "swa": 8, "nsa": 8, "ssd": 16}
        mixed_before, at = {}, 0
        for g in stages:
            mixed_before[g.s] = at
            at += mixed_raises.get(g.kind, 0)

        def mixed_for_pair(g, n):
            return {"gdn": n + 1, "ssd": 2 * n + 2}.get(g.kind, 4 if n < 2 else 8)

        convolved = [g for g in stages if g.kind in ("gdn", "ssd")]

        G_Q, G_K, G_V = 0, 8, 16
        gd_in = area(0, 24, T)
        gd_z = area(6144, 8, T)
        gd_inv = area(8192, 4, 4 * P)
        gd_invT = area(10240, 4, 4 * P)
        gd_LT = area(12288, 4, 4 * P)
        gd_off = area(14336, 4, 4 * P)
        gd_mid = area(16384, 4, 4 * P)
        gd_norm = area(8192, 8, 2 * T)
        gd_small = area(18432, 16, 16)
        gd_ba, gd_u, gd_arg, gd_g, gd_gc, gd_beta = (gd_small[:, 2 * n:2 * n + 2, :] for n in range(6))
        gd_rate, gd_kdec = gd_small[:, 12, 0:8], gd_small[:, 13, 0:8]
        gd_grow = area(18688, 8, P)
        gd_attT = xn
        gd_kb = spare
        gd_vb = hT[:, 8:16, :].rearrange("p k (e n) -> p (k e) n", e=2)
        gd_kd = hT[:, 16:20, :].rearrange("p k (e n) -> p (k e) n", e=2)
        gd_new0, gd_state = area(16384, 8, P), area(17408, 8, P)
        gd_rhs, gd_new1 = area(14336, 8, P), area(15360, 8, P)
        gd_onorm = area(13312, 4, 2 * T)
        ba_done = sem("gdn_ba_done")
        q_squared = sem("gdn_q_squared")
        q_square_sum = sem("gdn_q_square_sum")
        q_log = sem("gdn_q_log")
        q_inverse = sem("gdn_q_inverse")
        q_normed = sem("gdn_q_normed")
        g_arg = sem("gdn_g_arg")
        g_log = sem("gdn_g_log")
        g_ready = sem("gdn_g_ready")
        g_cums_done = sem("gdn_g_cums_done")
        g_cums_ready = sem("gdn_g_cums_ready")
        kdec_ready = sem("gdn_kdec_ready")
        g_rows_done = sem("gdn_g_rows_done")
        g_diff = sem("gdn_g_diff")
        g_decay = sem("gdn_g_decay")
        kb_ready = sem("gdn_kb_ready")
        kq_done = sem("gdn_kq_done")
        att_ready = sem("gdn_att_ready")
        v_turned = sem("gdn_v_turned")
        v_ready = sem("gdn_v_ready")
        grown_ready = sem("gdn_grown_ready")
        off_ready = sem("gdn_off_ready")
        off_used = sem("gdn_off_used")
        mid_ready = sem("gdn_mid_ready")
        inv_terms = sem("gdn_inv_terms")
        inv_ready = sem("gdn_inv_ready")
        invT_ready = sem("gdn_invT_ready")
        new0_done, new0_ready = sem("gdn_new0_done"), sem("gdn_new0_ready")
        state_sum, state_copied = sem("gdn_state_sum"), sem("gdn_state_copied")
        carried_done, rhs_ready = sem("gdn_carried_done"), sem("gdn_rhs_ready")
        new1_done, new1_ready = sem("gdn_new1_done"), sem("gdn_new1_ready")
        o_done = sem("gdn_o_done")
        o_squared = sem("gdn_o_squared")
        o_square_sum = sem("gdn_o_square_sum")
        o_log = sem("gdn_o_log")
        o_inverse = sem("gdn_o_inverse")
        class Attention:

            def __init__(self, kind, key_tiles, value_tiles):
                self.kind, self.key_tiles, self.value_tiles = kind, key_tiles, value_tiles
                self.branches = len(key_tiles)
                self.mask = "window" if kind == "swa" else "causal"
                self.scored = sem(kind + "_scored")
                self.masked = sem(kind + "_masked")
                self.maxed = sem(kind + "_maxed")
                self.exped = sem(kind + "_exped")
                self.probs = sem(kind + "_probs")
                self.turned = sem(kind + "_turned")
                self.turned_out = sem(kind + "_turned_out")
                self.summed = sem(kind + "_summed")
                self.values = sem(kind + "_values")
                self.values_turned = sem(kind + "_values_turned")
                self.quads = [(group, qb) for group in range(GROUPS) for qb in range(NT)]
                self.jobs = [(n, b) for n in range(len(self.quads)) for b in range(self.branches)]
                order = (0, -1, 1) if kind == "nsa" else (0,)
                self.turns = [(n, b) for n in range(len(self.quads)) for b in order]

            def scores(self, j):
                keys = (self.quads[self.jobs[j][0]][1] + 1) * P
                v = ps_flat[:, 2 * (j % 2) * BANK:2 * (j % 2) * BANK + 4 * keys]
                return v.rearrange("p (r k) -> p r k", r=4)

            def prob(self, j):
                keys = (self.quads[self.jobs[j][0]][1] + 1) * P
                v = prob_buf[:, j % 4, 0:4 * keys]
                return v.rearrange("p (r k) -> p r k", r=4)

        mix_tiles = area(0, 20, T)
        value_buf = area(5120, 2, NT, T)
        prob_buf = hT[:, 8:24, :].rearrange("p (n k) t -> p n (k t)", n=4)
        probT_buf = area(8192, 4, 4 * T)
        max_buf = area(12288, 16, 4)
        sum_buf = area(12352, 16, 4)
        sink_buf = area(12416, 16, 4)
        inv_buf = area(12480, 16, 4)
        attention = {"swa": Attention("swa", [8], [10]), "nsa": Attention("nsa", [12, 16], [14, 18])}
        SCALE = HD ** -0.5
        cmp_probT_buf = area(17024, 2, 4 * P)
        cmp_prob = area(18048, NT, 16, 16)
        gates_buf = area(18560, NT, 48)
        cmp_value = area(16768, 4 * HD)
        NG = GROUPS * NC
        token_pairs = area(12800, 2, GROUPS, P)
        cmp_in = area(13824, 2, 16, NG)
        cmp_hidden = area(6144, 4, 4 * P)
        cmp_hiddenT = area(15744, 4 * NG)
        cmp_key = area(16704, NG)
        cmp_drop = area(18656, NT, 16)
        cmp_max = area(18688, NT, 16)
        cmp_sum = area(18720, NT, 16)
        pairs_landed = sem("nsa_pairs_landed")
        cmp_in_ready = sem("nsa_cmp_in_ready")
        hidden_done = sem("nsa_hidden_done")
        tanh_in = sem("nsa_tanh_in")
        tanh_done = sem("nsa_tanh_done")
        gelu_done = sem("nsa_gelu_done")
        gelu_turned = sem("nsa_gelu_turned")
        gelu_turned_out = sem("nsa_gelu_turned_out")
        cmp_done = sem("nsa_cmp_done")
        cmp_out = sem("nsa_cmp_out")
        cmp_scored = sem("nsa_cmp_scored")
        cmp_centered = sem("nsa_cmp_centered")
        cmp_exped = sem("nsa_cmp_exped")
        cmp_ready = sem("nsa_cmp_ready")
        gates_done = sem("nsa_gates_done")
        gates_ready = sem("nsa_gates_ready")
        S_X, S_B, S_C = 0, 16, 20
        ssd_in = area(0, 24, T)
        ssd_z = area(6144, 16, T)
        ssd_xdec = area(10240, 2048)
        ssd_cb = area(12288, 8, P)
        ssd_B = area(13312, 4, P)
        ssd_w = area(13824, 4, 4 * P)
        ssd_state = area(15872, 4, 8 * HD)
        ssd_y = area(17920, 2, 8 * HD)
        ssd_small = area(18944, 12, 64)
        ssd_u, ssd_e, ssd_dt, ssd_dta, ssd_acs, ssd_misc = (ssd_small[:, n, :] for n in range(6))
        ssd_ea, ssd_dec = ssd_small[:, 6, 0:32], ssd_small[:, 7, 0:32]
        xdt_parts = [[spare[:, 2 * gg:2 * gg + 2, :].rearrange("p k t -> p (k t)") for gg in range(4)],
                     [xn[:, gg // 2, (gg % 2) * 512:(gg % 2 + 1) * 512] for gg in range(4)]]
        ssd_square = area(10240, 2, 4 * T)
        ssd_inverse = area(13824, 4, T)
        dt_done = sem("ssd_dt_done")
        dt_arg = sem("ssd_dt_arg")
        dt_log = sem("ssd_dt_log")
        dta_ready = sem("ssd_dta_ready")
        cums_done = sem("ssd_cums_done")
        cums_ready = sem("ssd_cums_ready")
        cums_exp = sem("ssd_cums_exp")
        b_turned = sem("ssd_b_turned")
        b_ready = sem("ssd_b_ready")
        cb_done = sem("ssd_cb_done")
        cb_ready = sem("ssd_cb_ready")
        x_turned = sem("ssd_x_turned")
        xdt_ready = sem("ssd_xdt_ready")
        xdec_ready = sem("ssd_xdec_ready")
        state_done = sem("ssd_state_done")
        state_ready = sem("ssd_state_ready")
        rows_done = sem("ssd_rows_done")
        diff_ready = sem("ssd_diff_ready")
        decay_ready = sem("ssd_decay_ready")
        w_ready = sem("ssd_w_ready")
        y_half = sem("ssd_y_half")
        y_done = sem("ssd_y_done")
        y_out = sem("ssd_y_out")
        y_turned = sem("ssd_y_turned")
        y_turned_out = sem("ssd_y_turned_out")
        y_gated = sem("ssd_y_gated")
        y_squared = sem("ssd_y_squared")
        y_square_sum = sem("ssd_y_square_sum")
        y_log = sem("ssd_y_log")
        y_inverse = sem("ssd_y_inverse")
        block = ctx.enter_context(nc.Block())

        @block.sync
        def _(sp):
            early = CONST_AT["ones"]
            x_tiles = x_in.rearrange("(t p) d -> p t d", p=P)
            for t in range(NT):
                sp.dma_start(x[:, t, :], x_tiles[:, t, :]).then_inc(x_loaded, 16)
            sp.dma_start(cst[:, 0:early], consts[:, 0:early]).then_inc(early_loaded, 16)
            for j in range(SLOTS):
                sp.dma_start(ring[:, j, :], units[j]).then_inc(landed[j], 16)
                if j == 0:
                    sp.dma_start(cst[:, early:CONST_N], consts[:, early:CONST_N]).then_inc(cst_loaded, 16)
            n_rounds = n_units // SLOTS
            with sp.Fori(1, n_rounds) as i:
                for j in range(SLOTS):
                    sp.wait_ge(unit_done, (i - 1) * SLOTS + j + 1)
                    sp.dma_start(ring[:, j, :], units[i * SLOTS + j]).then_inc(landed[j], 16)
            for u in range(n_rounds * SLOTS, n_units):
                sp.wait_ge(unit_done, u - SLOTS + 1)
                sp.dma_start(ring[:, u % SLOTS, :], units[u]).then_inc(landed[u % SLOTS], 16)
            out_tiles = out.rearrange("(t p) d -> p t d", p=P)
            for t in range(NT):
                sp.wait_ge(x_ready, x_after[events[-1], t])
                sp.dma_start(out_tiles[:, t, :], x[:, t, :]).then_inc(stored, 16)
            sp.wait_ge(stored, 16 * NT)

        @block.tensor
        def _(pe):
            mm = nc.tensor.matmul

            def norm_turned(g):
                for t in range(NT):
                    for kt in range(KD):
                        if kt % (KD // 2) == 0:
                            pe.wait_ge(xn_ready, 4 * g.s + 2 * t + kt // (KD // 2) + 1)
                        o = (kt % 2) * T + t * P
                        last = nc.tensor.transpose(ps[:, kt // 2, o:o + P], xn[:, t, kt * P:(kt + 1) * P], ident)
                        if t == NT - 1 and kt % 2 == 1:
                            last.then_inc(xn_turned, 1)

            def up(g):
                def chunk(j, i=0):
                    pe.wait_ge(evacuated, chunk_read(g, j - 3) + 3 * i)
                    for f in range(4):
                        c = quarters[g.split + 4 * j + f]
                        pe.wait_ge(w_split, c.count + 12 * i)
                        o = ps[:, 2 * (j % 3) + f // 2, (f % 2) * T:(f % 2 + 1) * T]
                        for kt in range(KD):
                            w, w_rest = (r32(v[:, kt * P:(kt + 1) * P]) for v in (rounded(c), rest(c)))
                            x_k, x_rest = r32(xT[:, kt, :]), r32(xT_rest[:, kt, :])
                            if j == 0 and f == 0 and kt % 2 == 0:
                                pe.wait_ge(xT_ready, KD * g.s + kt + 2)
                            mm(o, w, x_k, start=(kt == 0), stop=False)
                            mm(o, w, x_rest, start=False, stop=False)
                            last = mm(o, w_rest, x_k, start=False, stop=(kt == KD - 1))
                    last.then_inc(unit_done, 1)

                turns = g.chunks // 3
                with pe.Fori(0, turns) as i:
                    for j in range(3):
                        chunk(j, i)
                for j in range(3 * turns, g.chunks):
                    chunk(j)

            def down(g):
                h, h_rest = hT_parts(g)
                if not g.own_ring:
                    pe.wait_ge(evacuated, chunk_read(g, 8))

                def products(kt, t):
                    c = quarters[g.split_down + kt]
                    tokens = slice(t * P, (t + 1) * P)
                    for n in range(2):
                        o = ps[:, 4 + 2 * t + n, :]
                        w, w_rest = (r32(v[:, n * BANK:(n + 1) * BANK]) for v in (rounded(c), rest(c)))
                        mm(o, r32(h[:, kt, tokens]), w, start=(kt == 0), stop=False)
                        mm(o, r32(h[:, kt, tokens]), w_rest, start=False, stop=False)
                        last = mm(o, r32(h_rest[:, kt, tokens]), w, start=False, stop=(kt == g.k_tiles - 1))
                    return last

                for v in range(g.down_units):
                    kts = range(4 * v, min(4 * v + 4, g.k_tiles))
                    for kt in kts:
                        pe.wait_ge(w_split, quarters[g.split_down + kt].count)
                        pe.wait_ge(hT_split, g.rest + kt // 2 + 1)
                        if kt < g.k_tiles - 2:
                            for t in range(NT):
                                last = products(kt, t)
                    if v == g.down_units - 1:
                        for t in range(NT):
                            for kt in (g.k_tiles - 2, g.k_tiles - 1):
                                last = products(kt, t)
                            if t == 0:
                                last.then_inc(first_rows_done, 1)
                    last.then_inc(unit_done, 1)

            def narrow(g, bank):
                n = narrow_width[g.kind]
                pe.wait_ge(narrow_split, narrow_counts[g.s])
                for t in range(NT):
                    o = ps[:, bank, t * n:(t + 1) * n]
                    for kt in range(KD):
                        x_k, x_rest = (r32(v[:, kt, t * P:(t + 1) * P]) for v in (xT, xT_rest))
                        w, w_rest = (r32(v[:, kt * n:(kt + 1) * n]) for v in (narrow_rounded, narrow_rest))
                        mm(o, x_k, w, start=(kt == 0), stop=False)
                        mm(o, x_k, w_rest, start=False, stop=False)
                        last = mm(o, x_rest, w, start=False, stop=(kt == KD - 1))
                return last

            def gdn(g):
                pe.wait_ge(evacuated, chunk_read(g, g.chunks - 1))
                narrow(g, 6).then_inc(ba_done, 1)
                for n in range(8):
                    pe.wait_ge(q_squared, n + 1)
                    if n >= 2:
                        pe.wait_ge(q_log, n - 1)
                    mm(ps[:, n % 2, :], ones, gd_norm[:, n, :], start=True, stop=True)\
                        .then_inc(q_square_sum, 1)
                pe.wait_ge(g_ready, 1)
                mm(ps[:, 7, 0:16], const("upper"), gd_g[:, :, 0:8], start=True, stop=True)
                mm(ps[:, 7, 16:24], ones, gd_g[:, 0, 0:8], start=True, stop=True).then_inc(g_cums_done, 1)
                pe.wait_ge(q_log, 8)

                def rows(i):
                    if i >= 2:
                        pe.wait_ge(g_decay, i - 1)
                        pe.wait_ge(kb_ready, i - 1)
                    t, h = i // 2, i % 2 * 4
                    for r in range(4):
                        mm(ps[:, i % 2, r * P:(r + 1) * P], gd_g[:, t, h + r:h + r + 1].to_broadcast([P, P]),
                           const("upper"), start=True, stop=True)
                        last = mm(ps[:, 2 + i % 2, r * P:(r + 1) * P],
                                  gd_beta[:, t, h + r:h + r + 1].to_broadcast([P, P]), ident, start=True, stop=True)
                    last.then_inc(g_rows_done, 1)

                def keys_queries(i):
                    t, h = i // 2, i % 2 * 4
                    tokens = slice(t * P, (t + 1) * P)
                    pe.wait_ge(kb_ready, i + 1)
                    if i >= 1:
                        pe.wait_ge(att_ready, i)
                    for r in range(4):
                        key = gd_in[:, G_K + h + r, tokens]
                        mm(ps[:, 4, r * P:(r + 1) * P], key, gd_kb[:, h + r, tokens], start=True, stop=True)
                        last = mm(ps[:, 5, r * P:(r + 1) * P], key, gd_in[:, G_Q + h + r, tokens],
                                  start=True, stop=True)
                    last.then_inc(kq_done, 1)

                def by_token(i):
                    if i >= 1:
                        pe.wait_ge(v_ready, i)
                    tile, t, h = (G_V, i // 2, i % 2 * 4) if i < 4 else (G_K, 0, (i - 4) * 4)
                    for r in range(4):
                        last = nc.tensor.transpose(ps[:, 6, r * P:(r + 1) * P],
                                                   gd_in[:, tile + h + r, t * P:(t + 1) * P], ident)
                    last.then_inc(v_turned, 1)

                rows(0)
                rows(1)
                pe.wait_ge(q_normed, 8)
                for i in range(4):
                    by_token(i)
                    keys_queries(i)
                    if i < 2:
                        rows(i + 2)
                by_token(4)
                by_token(5)
                for i in range(4):
                    pe.wait_ge(off_ready, i + 1)
                    if i >= 2:
                        pe.wait_ge(inv_ready, i - 1)
                    for r in range(4):
                        last = nc.tensor.transpose(ps[:, i % 2, r * P:(r + 1) * P], gd_off[:, i, r * P:(r + 1) * P],
                                                   ident)
                    last.then_inc(off_used, 1)
                pe.wait_ge(inv_ready, 4)
                def join(level, last_level=False):
                    def middle(i):
                        pe.wait_ge(off_ready, level * 4 + i + 1)
                        pe.wait_ge(inv_ready, (level - 1) * 4 + i + 1)
                        if i >= 2:
                            pe.wait_ge(mid_ready, (level - 1) * 4 + i - 1)
                        for r in range(4):
                            problem = slice(r * P, (r + 1) * P)
                            last = mm(ps[:, i % 2, problem], gd_off[:, i, problem], gd_inv[:, i, problem],
                                      start=True, stop=True)
                        last.then_inc(off_used, 1)

                    def corrections(i):
                        pe.wait_ge(mid_ready, (level - 1) * 4 + i + 1)
                        if not last_level:
                            pe.wait_ge(inv_ready, level * 4 + i - 1)
                        pe.wait_ge(invT_ready, level * 4 + i - 1)
                        for r in range(4):
                            problem = slice(r * P, (r + 1) * P)
                            if not last_level:
                                mm(ps[:, 2 + i % 2, problem], gd_invT[:, i, problem], gd_mid[:, i, problem],
                                   start=True, stop=True)
                            last = mm(ps[:, 4 + i % 2, problem], gd_mid[:, i, problem], gd_invT[:, i, problem],
                                      start=True, stop=True)
                        last.then_inc(inv_terms, 1)

                    middle(0)
                    middle(1)
                    corrections(0)
                    middle(2)
                    corrections(1)
                    middle(3)
                    corrections(2)
                    corrections(3)

                with pe.Fori(1, LEVELS - 1) as level:
                    join(level)
                join(LEVELS - 1, last_level=True)

                def per_head(bank, lhsT, rhs, done):
                    for half in range(2):
                        for r in range(4):
                            h = half * 4 + r
                            last = mm(ps[:, bank + half, r * P:(r + 1) * P], lhsT(h), rhs(h), start=True, stop=True)
                        last.then_inc(done, 1)

                def inverse(problem):
                    return gd_invT[:, problem // 4, problem % 4 * P:(problem % 4 + 1) * P]

                pe.wait_ge(invT_ready, 4 * LEVELS)
                pe.wait_ge(v_ready, 6)
                per_head(0, lambda h: inverse(h), lambda h: gd_vb[:, h, :], new0_done)
                pe.wait_ge(new0_ready, 2)
                per_head(2, lambda h: gd_kd[:, h, :], lambda h: gd_new0[:, h, :], state_sum)
                pe.wait_ge(state_copied, 2)
                pe.wait_ge(grown_ready, 2)
                per_head(4, lambda h: gd_kb[:, h, P:T], lambda h: gd_state[:, h, :], carried_done)
                pe.wait_ge(rhs_ready, 2)
                per_head(0, lambda h: inverse(8 + h), lambda h: gd_rhs[:, h, :], new1_done)
                o_banks = (6, 7, 2, 3)

                def o_sum(n):
                    pe.wait_ge(o_squared, n + 1)
                    if n >= 2:
                        pe.wait_ge(o_log, n - 1)
                    mm(ps[:, 4 + n % 2, :], ones, gd_onorm[:, n, :], start=True, stop=True)\
                        .then_inc(o_square_sum, 1)

                for n in range(4):
                    for e in range(2):
                        h = 2 * n + e
                        o = ps[:, o_banks[n], e * T:(e + 1) * T]
                        mm(o[:, 0:P], gd_new0[:, h, :], gd_attT[:, 0, h * P:(h + 1) * P], start=True, stop=True)
                        mm(o[:, P:T], gd_state[:, h, :], gd_in[:, G_Q + h, P:T], start=True, stop=False)
                        if h % 4 == 0:
                            pe.wait_ge(new1_ready, h // 4 + 1)
                        last = mm(o[:, P:T], gd_new1[:, h, :], gd_attT[:, 1, h * P:(h + 1) * P],
                                  start=False, stop=True)
                    last.then_inc(o_done, 1)
                    if n >= 1:
                        o_sum(n - 1)
                o_sum(3)

            def attend(a, g, compressed=None):
                def value_turns(b):
                    for t in range(NT):
                        for f in range(2):
                            last = nc.tensor.transpose(ps[:, 6 + b, (2 * t + f) * P:(2 * t + f + 1) * P],
                                                       mix_tiles[:, a.value_tiles[b] + f, t * P:(t + 1) * P], ident)
                    last.then_inc(a.values_turned, 1)

                def score(j):
                    n, b = a.jobs[j]
                    group, qb = a.quads[n]
                    h0 = HD * (group % 2)
                    if j >= 2:
                        pe.wait_ge(a.masked, j - 1)
                    for r in range(4):
                        last = mm(a.scores(j)[:, r, :],
                                  mix_tiles[h0:h0 + HD, group // 2 * 4 + r, qb * P:(qb + 1) * P],
                                  mix_tiles[h0:h0 + HD, a.key_tiles[b] + group // 2, 0:(qb + 1) * P],
                                  start=True, stop=True)
                    last.then_inc(a.scored, 1)

                def turn(k):
                    n, b = a.turns[k]
                    group, qb = a.quads[n]
                    if k >= 1:
                        pe.wait_ge(a.turned_out, k)
                    if b < 0:
                        pe.wait_ge(cmp_ready, NT)
                        for r in range(4):
                            last = nc.tensor.transpose(ps[0:NC, 4, r * P:(r + 1) * P],
                                                       cmp_prob[:, qb, group * 4 + r, 0:NC], ident)
                    else:
                        j = a.jobs.index((n, b))
                        pe.wait_ge(a.probs, j + 1)
                        for kb in range(qb + 1):
                            for r in range(4):
                                last = nc.tensor.transpose(ps[:, 4 + kb, r * P:(r + 1) * P],
                                                           a.prob(j)[:, r, kb * P:(kb + 1) * P], ident)
                    last.then_inc(a.turned, 1)

                def outputs(n):
                    group, qb = a.quads[n]
                    h0 = HD * (group % 2)
                    pe.wait_ge(a.turned_out, len([k for k in a.turns if k[0] <= n]))
                    if n >= 2:
                        pe.wait_ge(mixed, mixed_before[g.s] + n - 1)
                    for r in range(4):
                        o = ps[h0:h0 + HD, 6 + n % 2, r * P:(r + 1) * P]
                        terms = []
                        if compressed:
                            terms.append((cmp_value[0:NC, group * HD:(group + 1) * HD],
                                          cmp_probT_buf[0:NC, n % 2, r * P:(r + 1) * P]))
                        for b in range(a.branches):
                            probT = probT_buf[:, (n * a.branches + b) % 4, :]
                            for kb in range(qb + 1):
                                terms.append((value_buf[:, b, kb, group * HD:(group + 1) * HD],
                                              probT[:, (kb * 4 + r) * P:(kb * 4 + r + 1) * P]))
                        for m, (lhsT, rhs) in enumerate(terms):
                            last = mm(o, lhsT, rhs, start=(m == 0), stop=(m == len(terms) - 1))
                    last.then_inc(a.summed, 1)

                for b in range(a.branches):
                    value_turns(b)
                score(0)
                score(1)
                if compressed:
                    compressed()
                pe.wait_ge(a.values, a.branches)
                for k, (n, b) in enumerate(a.turns):
                    if b >= 0:
                        j = a.jobs.index((n, b))
                        if j + 2 < len(a.jobs):
                            score(j + 2)
                    turn(k)
                    if n >= 1 and a.turns[k - 1][0] == n - 1:
                        outputs(n - 1)
                outputs(len(a.quads) - 1)

            def swa(g):
                pe.wait_ge(evacuated, chunk_read(g, g.chunks - 1))
                attend(attention["swa"], g)

            def nsa(g):
                pe.wait_ge(evacuated, chunk_read(g, g.chunks - 1))
                narrow(g, 5).then_inc(gates_done, 1)

                def compressed():
                    pe.wait_ge(gates_ready, 1)
                    for kv in range(2):
                        u = g.extra + kv
                        pe.wait_ge(landed[u % SLOTS], 16 * (u // SLOTS + 1))
                        pe.wait_ge(cmp_in_ready, kv + 1)
                        for m in range(16):
                            last = mm(ps[0:NG, 4 + kv, 0:2 * P], cmp_in[:, kv, m, :],
                                      ring[:, u % SLOTS, m * 2 * P:(m + 1) * 2 * P], start=(m == 0), stop=(m == 15))
                        last.then_inc(unit_done, 1)
                    w2 = const("w_cmp2").rearrange("p (v h n) -> p v h n", v=2, h=2)
                    pe.wait_ge(gelu_done, 1)
                    for n in range(4):
                        last = nc.tensor.transpose(ps[:, 4, n * NG:(n + 1) * NG], cmp_hidden[0:NG, 0, n * P:(n + 1) * P],
                                                   ident[0:NG, 0:NG])
                    last.then_inc(gelu_turned, 1)
                    pe.wait_ge(gelu_turned_out, 1)
                    for hid in range(2):
                        mm(ps[:, 4, 0:NG], w2[:, 0, hid, :], cmp_hiddenT[:, hid * NG:(hid + 1) * NG],
                           start=(hid == 0), stop=(hid == 1))
                    for group in range(GROUPS):
                        for hid in range(2):
                            at = (2 + hid) * NG + group * NC
                            last = mm(ps[0:NC, 5, group * HD:(group + 1) * HD], cmp_hiddenT[:, at:at + NC],
                                      w2[:, 1, hid, 0:HD], start=(hid == 0), stop=(hid == 1))
                    last.then_inc(cmp_done, 1)
                    pe.wait_ge(cmp_out, 2)
                    pe.wait_ge(attention["nsa"].values, 2)
                    for qb in range(NT):
                        for h in range(16):
                            group, r = h // 4, h % 4
                            h0 = HD * (group % 2)
                            at = (qb * 8 + group // 2 * 4 + r) * 16
                            last = mm(ps[:, 6 + group % 2, at:at + NC],
                                      mix_tiles[h0:h0 + HD, group // 2 * 4 + r, qb * P:(qb + 1) * P],
                                      cmp_key[h0:h0 + HD, group * NC:(group + 1) * NC], start=True, stop=True)
                    last.then_inc(cmp_scored, 1)

                attend(attention["nsa"], g, compressed)

            def ssd(g):
                pe.wait_ge(evacuated, chunk_read(g, g.chunks - 1))
                narrow(g, 6).then_inc(dt_done, 1)
                pe.wait_ge(conv_silu, 6 * (1 + sum(q.s < g.s for q in convolved)))
                for gg in range(4):
                    last = nc.tensor.transpose(ps[:, 4, gg * P:(gg + 1) * P], ssd_in[:, S_B + gg, 0:P], ident)
                last.then_inc(b_turned, 1)
                for t in range(NT):
                    for gg in range(4):
                        tokens = slice(t * P, (t + 1) * P)
                        last = mm(ps[:, t, gg * P:(gg + 1) * P], ssd_in[:, S_B + gg, tokens],
                                  ssd_in[:, S_C + gg, tokens], start=True, stop=True)
                    last.then_inc(cb_done, 1)

                def x_by_token(m):
                    t, gg = m // 4, m % 4
                    if m >= 2:
                        pe.wait_ge(xdt_ready, m - 1)
                    for f in range(4):
                        last = nc.tensor.transpose(ps[:, 2 + m % 2, f * P:(f + 1) * P],
                                                   ssd_in[:, S_X + 4 * gg + f, t * P:(t + 1) * P], ident)
                    last.then_inc(x_turned, 1)

                x_by_token(0)
                x_by_token(1)
                pe.wait_ge(dta_ready, 1)
                mm(ps[:, 7, 0:64], const("upper"), ssd_dta, start=True, stop=True)
                mm(ps[:, 7, 64:96], ones, ssd_dta[:, 0:32], start=True, stop=True).then_inc(cums_done, 1)
                for m in range(2, 8):
                    x_by_token(m)
                pe.wait_ge(b_ready, 1)
                for gg in range(4):
                    pe.wait_ge(xdec_ready, gg + 1)
                    if gg >= 2:
                        pe.wait_ge(state_ready, gg - 1)
                    mm(ps[:, 4 + gg % 2, :], ssd_B[:, gg, :], ssd_xdec[:, gg * 512:(gg + 1) * 512],
                       start=True, stop=True).then_inc(state_done, 1)

                def rows(k):
                    t, h = k // 8, k % 8 * 4
                    if k >= 2:
                        pe.wait_ge(diff_ready, k - 1)
                    for r in range(4):
                        column = ssd_dta[:, t * 32 + h + r:t * 32 + h + r + 1]
                        last = mm(ps[:, k % 2, r * P:(r + 1) * P], column.to_broadcast([P, P]), const("upper"),
                                  start=True, stop=True)
                    last.then_inc(rows_done, 1)

                def quadratic(k):
                    m = k // 2
                    t, gg = m // 4, m % 4
                    pe.wait_ge(w_ready, k + 1)
                    if k % 2 == 0 and m >= 2:
                        pe.wait_ge(y_out, m - 1)
                    for r in range(4):
                        o = (k % 2 * 4 + r) * HD
                        last = mm(ps[:, 2 + m % 2, o:o + HD], ssd_w[:, k % 4, r * P:(r + 1) * P],
                                  xdt_parts[t][gg][:, o:o + HD], start=True, stop=True)
                    last.then_inc(y_half, 1)

                def from_state(m):
                    gg = m % 4
                    if m >= 5:
                        pe.wait_ge(y_out, m)
                    mm(ps[:, 4, :], ssd_in[:, S_C + gg, P:2 * P], ssd_state[:, gg, :],
                       start=True, stop=True).then_inc(y_done, 1)

                def turn(m):
                    pe.wait_ge(y_out, m + 1)
                    if m >= 1:
                        pe.wait_ge(y_turned_out, m)
                    for f in range(4):
                        last = nc.tensor.transpose(ps[:, 5, f * P:(f + 1) * P], ssd_y[:, m % 2, f * P:(f + 1) * P],
                                                   ident)
                    last.then_inc(y_turned, 1)

                pe.wait_ge(cb_ready, 2)
                pe.wait_ge(xdt_ready, 8)
                pe.wait_ge(state_ready, 4)
                rows(0)
                rows(1)
                for m in range(8):
                    for k in (2 * m, 2 * m + 1):
                        if k + 2 < 16:
                            rows(k + 2)
                        quadratic(k)
                    if m >= 4:
                        from_state(m)
                    if m >= 1:
                        turn(m - 1)
                turn(7)
                for gg in range(4):
                    pe.wait_ge(y_squared, gg + 1)
                    if gg >= 2:
                        pe.wait_ge(y_log, gg - 1)
                    for f in range(4):
                        last = mm(ps[:, gg % 2, 0:T], ones, ssd_square[:, gg % 2, f * T:(f + 1) * T],
                                  start=(f == 0), stop=(f == 3))
                    last.then_inc(y_square_sum, 1)

            pe_mixer = {"gdn": gdn, "swa": swa, "nsa": nsa, "ssd": ssd}

            pe.wait_ge(early_loaded, 16)
            pe.sem_inc(evacuated, 3)
            for g in stages:
                norm_turned(g)
                up(g)
                if g.s == 0:
                    pe.wait_ge(cst_loaded, 16)
                if g.kind in pe_mixer:
                    pe_mixer[g.kind](g)
                down(g)

        @block.scalar
        def _(act):
            activation = nc.scalar.activation

            def deviation_of(in_, key):
                n = deviation_at[key] - 1
                square = stats[:, 4 + n % 4:5 + n % 4]
                act_step.up(activation(junk[:, :], in_, ACT.Square, accum_out=square))
                act_step.wait(act)
                activation(stats[:, n % 4:n % 4 + 1], square, ACT.Sqrt, scale=1.0 / D,
                           bias=EPS).then_inc(deviation, 1)

            def turned_out(g):
                for b in range(4):
                    act.wait_ge(xn_turned, 4 * g.s + b + 1)
                    for kt in (2 * b, 2 * b + 1):
                        gain = const("norms", g.norm * KD + kt, g.norm * KD + kt + 1)
                        activation(r32(xT[:, kt, :]), ps[:, b, (kt % 2) * T:(kt % 2 + 1) * T], ACT.Identity,
                                   scale=gain).then_inc(xT_rounded, 1)

            def split(found, i=0):
                for c in found:
                    if c.q == 0:
                        act.wait_ge(landed[c.unit % SLOTS], 16 * (c.unit // SLOTS + 1) + 16 * i)
                    activation(r32(rounded(c)), quarter(c), ACT.Copy).then_inc(w_rounded, 1)

            def split_hidden(c):
                at = bass.ds(c * 2 * T, 2 * T)
                activation(r32(hT_rounded_flat[:, at]), hT_flat[:, at], ACT.Copy).then_inc(hT_rounded, 1)

            def split_mixed(g):
                for n, c in first_down_steps(g):
                    if c:
                        split([c])
                    else:
                        act.wait_ge(mixed, mixed_before[g.s] + mixed_for_pair(g, n))
                        activation(r32(hT_pair(hT_parts(g)[0], n)), hT_pair(hT, n), ACT.Copy).then_inc(hT_rounded, 1)

            def swiglu(g):
                def chunk(j, i=0, c=0):
                    act.wait_ge(unit_done, units_until(g.unit + j) + 3 * i)
                    activation(gate_buf[:, j % 3, :], ps[:, 2 * (j % 3), :], ACT.Silu).then_inc(gated, 1)
                    split(split_next(g.split + 4 * j), i)
                    act.wait_ge(evacuated, chunk_read(g, j) + 3 * i)
                    split_hidden(c)

                turns = g.chunks // 3
                with act.Fori(0, turns) as i:
                    for j in range(3):
                        chunk(j, i, 3 * i + j)
                for j in range(3 * turns, g.chunks):
                    chunk(j, 0, j)

            taps_done = [0]

            def raw_out(g, j, i, c, weights, width):
                for f in range(4):
                    k = CONST_AT[weights] + (c * 4 + f) * (width + 1)
                    activation(conv_buf[:, j % 3, f * T:(f + 1) * T], pair(j % 3)[:, f * T:(f + 1) * T], ACT.Identity,
                               scale=cst[:, bass.ds(k + width - 1, 1)], bias=cst[:, bass.ds(k + width, 1)])
                activation(raw_buf[:, j % 3, :], pair(j % 3), ACT.Copy).then_inc(evacuated, 1)

            def cffn(g):
                began = taps_done[0]

                def chunk(j, i=0, c=0):
                    ahead = split_next(g.split + 4 * j)
                    act.wait_ge(unit_done, units_until(g.unit + j) + 3 * i)
                    split(ahead[:2], i)
                    raw_out(g, j, i, c, f"conv{g.nth}", 3)
                    split(ahead[2:], i)
                    if j > 0:
                        act.wait_ge(hidden, g.hidden + j + 3 * i)
                        split_hidden(c - 1)
                    act.wait_ge(conv_tail, began + 4 * j + 2 + 12 * i)
                    gates = conv_buf[:, j % 3, 2 * T:4 * T]
                    activation(gates, gates, ACT.Silu).then_inc(gated, 1)

                chunk(0)
                turns = (g.chunks - 1) // 3
                with act.Fori(0, turns) as i:
                    for j in range(1, 4):
                        chunk(j, i, 3 * i + j)
                for j in range(1 + 3 * turns, g.chunks):
                    chunk(j, 0, j)
                act.wait_ge(hidden, g.hidden + g.chunks)
                split_hidden(g.chunks - 1)
                taps_done[0] += 4 * g.chunks

            def conv_chunks(g, weights):
                began = taps_done[0]
                with act.Fori(0, 2) as i:
                    def silu(j):
                        act.wait_ge(conv_tail, began + 4 * j + 4 + 12 * i)
                        activation(arena[:, bass.ds((3 * i + j) * 4 * T, 4 * T)], conv_buf[:, j, :],
                                   ACT.Silu).then_inc(conv_silu, 1)

                    for j in range(3):
                        act.wait_ge(unit_done, units_until(g.unit + j) + 3 * i)
                        ahead = split_next(g.split + 4 * j)
                        split(ahead[:2], i)
                        raw_out(g, j, i, 3 * i + j, weights, 4)
                        split(ahead[2:], i)
                        if j > 0:
                            silu(j - 1)
                    silu(2)
                taps_done[0] += 24

            def gdn(g):
                conv_chunks(g, "gdn_conv")
                for c in range(6, g.chunks):
                    act.wait_ge(unit_done, units_until(g.unit + c))
                    activation(gd_z[:, 4 * (c - 6):4 * (c - 5), :].rearrange("p f t -> p (f t)"), pair(c % 3),
                               ACT.Silu).then_inc(evacuated, 1)
                    split(split_next(g.split + 4 * c))
                    if c == 6:
                        act.wait_ge(conv_silu, 6 * (1 + sum(q.s < g.s for q in convolved)))
                        for n in range(8):
                            activation(gd_norm[:, n, :], gd_in[:, 2 * n:2 * n + 2, :].rearrange("p f t -> p (f t)"),
                                       ACT.Square).then_inc(q_squared, 1)
                act.wait_ge(g_arg, 1)
                e, b = gd_arg[:, :, 0:8], gd_ba[:, :, 0:8]
                act_step.up(activation(e, e, ACT.Exp))
                act_step.wait(act)
                activation(b, b, ACT.Exp, scale=-1.0)
                activation(gd_rate, heads("a_log", 8), ACT.Exp)
                activation(e, e, ACT.Ln, bias=1.0).then_inc(g_log, 1)
                for n in range(8):
                    act.wait_ge(q_square_sum, n + 1)
                    activation(gd_norm[:, n, :], ps[:, n % 2, :], ACT.Ln, bias=EPS).then_inc(q_log, 1)
                for n in range(8):
                    act.wait_ge(q_log, n + 1)
                    activation(gd_norm[:, n, :], gd_norm[:, n, :], ACT.Exp, scale=-0.5).then_inc(q_inverse, 1)
                act.wait_ge(g_cums_ready, 1)
                activation(gd_kdec, gd_kdec, ACT.Exp).then_inc(kdec_ready, 1)
                for i in range(4):
                    act.wait_ge(g_diff, i + 1)
                    last = activation(gd_off[:, i, :], gd_off[:, i, :], ACT.Exp)
                    if i >= 2:
                        half = gd_grow[:, (i - 2) * 4:(i - 1) * 4, :].rearrange("p h n -> p (h n)")
                        last = activation(half, ps[:, i % 2, :], ACT.Exp)
                    last.then_inc(g_decay, 1)
                with act.Fori(1, LEVELS) as level:
                    for i in range(4):
                        act.wait_ge(off_used, level * 4 + i + 1)
                        activation(gd_mid[:, i, :], ps[:, i % 2, :], ACT.Copy).then_inc(mid_ready, 1)

                def copied(to, bank, done, ready):
                    for half in range(2):
                        act.wait_ge(done, half + 1)
                        activation(to[:, half * 4:half * 4 + 4, :].rearrange("p h n -> p (h n)"),
                                   ps[:, bank + half, :], ACT.Copy).then_inc(ready, 1)

                copied(gd_new0, 0, new0_done, new0_ready)
                copied(gd_state, 2, state_sum, state_copied)
                copied(gd_new1, 0, new1_done, new1_ready)

                def logs(n):
                    act.wait_ge(o_square_sum, n + 1)
                    activation(gd_onorm[:, n, :], ps[:, 4 + n % 2, :], ACT.Ln, scale=1.0 / P,
                               bias=EPS).then_inc(o_log, 1)

                for n in range(4):
                    act.wait_ge(o_done, n + 1)
                    activation(gd_onorm[:, n, :], ps[:, (6, 7, 2, 3)[n], :], ACT.Square).then_inc(o_squared, 1)
                    if n >= 1:
                        logs(n - 1)
                logs(3)
                for n in range(4):
                    act.wait_ge(o_log, n + 1)
                    activation(gd_onorm[:, n, :], gd_onorm[:, n, :], ACT.Exp, scale=-0.5).then_inc(o_inverse, 1)

            def attend(a, g, compressed=None):
                def exps(j):
                    act.wait_ge(a.maxed, j + 1)
                    for r in range(4):
                        last = activation(a.prob(j)[:, r, :], a.prob(j)[:, r, :], ACT.Exp, scale=SCALE,
                                          bias=max_buf[:, j, r:r + 1], accum_out=sum_buf[:, j, r:r + 1])
                        if a.kind == "swa" and r == 3:
                            last = activation(sink_buf[:, j, :], sink_buf[:, j, :], ACT.Exp)
                    last.then_inc(a.exped, 1)

                def turned_out(k):
                    n, b = a.turns[k]
                    qb = a.quads[n][1]
                    act.wait_ge(a.turned, k + 1)
                    if n >= 2:
                        act.wait_ge(a.summed, n - 1)
                    if b < 0:
                        last = activation(cmp_probT_buf[0:NC, n % 2, :], ps[0:NC, 4, :], ACT.Copy)
                    else:
                        last = activation(probT_buf[:, (n * a.branches + b) % 4, 0:(qb + 1) * BANK],
                                          ps_flat[:, 4 * BANK:(5 + qb) * BANK], ACT.Copy)
                    last.then_inc(a.turned_out, 1)

                def outputs_out(n):
                    group, qb = a.quads[n]
                    h0 = HD * (group % 2)
                    act.wait_ge(a.summed, n + 1)
                    activation(hT[h0:h0 + HD, group // 2 * 4:group // 2 * 4 + 4, qb * P:(qb + 1) * P],
                               ps[h0:h0 + HD, 6 + n % 2, :].rearrange("p (r q) -> p r q", r=4),
                               ACT.Copy).then_inc(mixed, 1)

                exps(0)
                exps(1)
                if compressed:
                    compressed()
                for k, (n, b) in enumerate(a.turns):
                    if b >= 0:
                        j = a.jobs.index((n, b))
                        if 1 <= j < len(a.jobs) - 1:
                            exps(j + 1)
                    turned_out(k)
                    if n >= 1 and a.turns[k - 1][0] == n - 1:
                        outputs_out(n - 1)
                outputs_out(len(a.quads) - 1)

            def values_out(a):
                for b in range(a.branches):
                    act.wait_ge(a.values_turned, b + 1)
                    activation(value_buf[:, b, :, :].rearrange("p t f -> p (t f)"), ps[:, 6 + b, :],
                               ACT.Copy).then_inc(a.values, 1)

            def swa(g):
                for c in range(g.chunks):
                    act.wait_ge(unit_done, units_until(g.unit + c))
                    for f in range(4):
                        bias = const("swa_bias", 4 * c + f, 4 * c + f + 1)
                        last = activation(mix_tiles[:, 4 * c + f, :], pair(c)[:, f * T:(f + 1) * T],
                                          ACT.Identity, bias=bias)
                    last.then_inc(evacuated, 1)
                    split(split_next(g.split + 4 * c))
                values_out(attention["swa"])
                attend(attention["swa"], g)

            def nsa(g):
                for c in (0, 1, 2, 3, 4):
                    act.wait_ge(unit_done, units_until(g.unit + c))
                    if c == 2:
                        source = pair(c % 3).rearrange("p (f s e) -> p f e s", f=4, e=2)
                        for e in range(2):
                            last = activation(mix_tiles[:, 8:12, e * P:(e + 1) * P], source[:, :, e, :], ACT.Copy)
                    else:
                        last = activation(mix_tiles[:, 4 * c:4 * c + 4, :].rearrange("p f t -> p (f t)"),
                                          pair(c % 3), ACT.Copy)
                    last.then_inc(evacuated, 1)
                    split(split_next(g.split + 4 * c))
                act.wait_ge(gates_done, 1)
                activation(gates_buf[:, :, :].rearrange("p t n -> p (t n)"), ps[:, 5, 0:NT * 48],
                           ACT.Sigmoid).then_inc(gates_ready, 1)
                a = attention["nsa"]
                values_out(a)

                def compressed():
                    act.wait_ge(tanh_in, 1)
                    activation(cmp_hidden[0:NG, 2, :], cmp_hidden[0:NG, 2, :], ACT.Tanh,
                               scale=0.7978845608028654).then_inc(tanh_done, 1)
                    act.wait_ge(gelu_turned, 1)
                    activation(cmp_hiddenT[:, :], ps[:, 4, 0:4 * NG], ACT.Copy).then_inc(gelu_turned_out, 1)
                    act.wait_ge(cmp_done, 1)
                    activation(cmp_key[:, :], ps[:, 4, 0:NG], ACT.Copy).then_inc(cmp_out, 1)
                    activation(cmp_value[0:NC, :], ps[0:NC, 5, 0:4 * HD], ACT.Copy).then_inc(cmp_out, 1)
                    for t in range(NT):
                        act.wait_ge(cmp_centered, t + 1)
                        activation(cmp_prob[:, t, :, 0:NC], cmp_prob[:, t, :, 0:NC], ACT.Exp,
                                   scale=SCALE).then_inc(cmp_exped, 1)

                attend(a, g, compressed)

            def ssd(g):
                conv_chunks(g, "ssd_conv")
                for c in range(6, g.chunks):
                    act.wait_ge(unit_done, units_until(g.unit + c))
                    activation(ssd_z[:, 4 * (c - 6):4 * (c - 5), :].rearrange("p f t -> p (f t)"), pair(c % 3),
                               ACT.Silu).then_inc(evacuated, 1)
                    split(split_next(g.split + 4 * c))
                act.wait_ge(dt_arg, 1)
                act_step.up(activation(ssd_e, ssd_e, ACT.Exp))
                act_step.wait(act)
                activation(ssd_ea, heads("ssd_a", 32), ACT.Exp)
                activation(ssd_e, ssd_e, ACT.Ln, bias=1.0).then_inc(dt_log, 1)
                act.wait_ge(b_turned, 1)
                activation(ssd_B[:, :, :].rearrange("p g n -> p (g n)"), ps[:, 4, :], ACT.Copy).then_inc(b_ready, 1)
                act.wait_ge(cums_ready, 1)
                activation(ssd_dec, ssd_dec, ACT.Exp)
                activation(ssd_misc[:, 0:32], ssd_acs[:, 32:64], ACT.Exp).then_inc(cums_exp, 1)
                for gg in range(4):
                    act.wait_ge(state_done, gg + 1)
                    activation(ssd_state[:, gg, :], ps[:, 4 + gg % 2, :], ACT.Copy).then_inc(state_ready, 1)
                for k in range(16):
                    act.wait_ge(diff_ready, k + 1)
                    activation(ssd_w[:, k % 4, :], ssd_w[:, k % 4, :], ACT.Exp).then_inc(decay_ready, 1)
                for gg in range(4):
                    act.wait_ge(y_gated, 4 + gg + 1)
                    if gg >= 2:
                        act.wait_ge(y_square_sum, gg - 1)
                    activation(ssd_square[:, gg % 2, :], hT[:, 4 * gg:4 * gg + 4, :].rearrange("p f t -> p (f t)"),
                               ACT.Square).then_inc(y_squared, 1)
                    if gg >= 1:
                        log_of(gg - 1)
                log_of(3)
                for gg in range(4):
                    act.wait_ge(y_log, gg + 1)
                    activation(ssd_inverse[:, gg, :], ssd_inverse[:, gg, :], ACT.Exp, scale=-0.5).then_inc(y_inverse, 1)

            def log_of(gg):
                act.wait_ge(y_square_sum, gg + 1)
                activation(ssd_inverse[:, gg, :], ps[:, gg % 2, 0:T], ACT.Ln, scale=1.0 / (4 * P),
                           bias=EPS).then_inc(y_log, 1)

            act_mixer = {"gdn": gdn, "swa": swa, "nsa": nsa, "ssd": ssd}

            act.wait_ge(early_loaded, 16)
            for t in range(NT):
                act.wait_ge(x_loaded, 16 * NT)
                deviation_of(x[:, t, :], ("norm", 0, t))
            for g in stages:
                first = split_first(g.split) if g.s == 0 or g.own_ring else []
                split(first[:1])
                turned_out(g)
                split(first[1:] if first else split_next(g.split - 4))
                if g.s == 0:
                    act.wait_ge(cst_loaded, 16)
                if g.kind == "swiglu":
                    swiglu(g)
                elif g.kind == "cffn":
                    cffn(g)
                else:
                    if g.kind in narrow_width:
                        activation(r32(narrow_rounded[:, 0:KD * narrow_width[g.kind]]), const(narrow_const[g.kind]),
                                   ACT.Copy).then_inc(narrow_rounding, 1)
                    act_mixer[g.kind](g)
                    split_mixed(g)
                for v in range(g.down_units - 1):
                    act.wait_ge(unit_done, units_until(g.down + v))
                    split(split_next(g.split_down + 4 * v))
                for t in range(NT):
                    if g.kind in ("nsa", "cffn", "ssd"):
                        if t == 0:
                            act.wait_ge(first_rows_done, g.s + 1)
                        else:
                            act.wait_ge(unit_done, units_until(g.down + g.down_units - 1))
                        deviation_of(ps_flat[:, (4 + 2 * t) * BANK:(6 + 2 * t) * BANK], ("post", g.s, t))
                    if g.norm == FINAL_AFTER:
                        act.wait_ge(x_ready, x_after[("residual", g.s), t])
                        deviation_of(x[:, t, :], ("final", g.s, t))
                    if g.s < last_stage:
                        act.wait_ge(x_ready, x_event_before_norm(g.s + 1, t))
                        deviation_of(x[:, t, :], ("norm", g.s + 1, t))

        @block.vector
        def _(dve):
            tt, stt, ts = nc.vector.tensor_tensor, nc.vector.scalar_tensor_tensor, nc.vector.tensor_scalar

            def rstd(key):
                n = deviation_at[key]
                dve.wait_ge(deviation, n)
                column = stats[:, 8 + (n - 1) % 4:9 + (n - 1) % 4]
                dve_step.up(nc.vector.reciprocal(column, stats[:, (n - 1) % 4:(n - 1) % 4 + 1]))
                dve_step.wait(dve)
                return column

            def norm(s, t):
                column = rstd(("norm", s, t))
                for half in range(2):
                    at = slice(half * D // 2, (half + 1) * D // 2)
                    ts(xn[:, t, at], x[:, t, at], column, None, ALU.mult).then_inc(xn_ready, 1)

            def turned_out(g):
                for b in range(4):
                    dve.wait_ge(xT_rounded, KD * g.s + 2 * b + 2)
                    for kt in (2 * b, 2 * b + 1):
                        gain = const("norms", g.norm * KD + kt, g.norm * KD + kt + 1)
                        stt(r32(xT_rest[:, kt, :]), ps[:, b, (kt % 2) * T:(kt % 2 + 1) * T], gain, xT[:, kt, :],
                            ALU.mult, ALU.subtract).then_inc(xT_ready, 1)

            def split(found, i=0):
                for c in found:
                    dve.wait_ge(w_rounded, c.count + 12 * i)
                    tt(r32(rest(c)), quarter(c), rounded(c), ALU.subtract).then_inc(w_split, 1)

            def split_hidden(g, j, i, c):
                at = bass.ds(c * 2 * T, 2 * T)
                dve.wait_ge(hT_rounded, g.rest + j + 1 + 3 * i)
                tt(r32(hT_rest_flat[:, at]), hT_flat[:, at], hT_rounded_flat[:, at], ALU.subtract).then_inc(hT_split, 1)

            def split_mixed(g, finish):
                if finish:
                    finish(0)
                for n, c in first_down_steps(g):
                    if c:
                        split([c])
                    else:
                        if finish and n + 1 < g.k_tiles // 2:
                            finish(n + 1)
                        dve.wait_ge(hT_rounded, g.rest + n + 1)
                        rounded_pair, rest_pair = (hT_pair(v, n) for v in hT_parts(g))
                        tt(r32(rest_pair), hT_pair(hT, n), rounded_pair, ALU.subtract).then_inc(hT_split, 1)

            def swiglu(g):
                def chunk(j, i=0, c=0):
                    dve.wait_ge(gated, g.gated + j + 1 + 3 * i)
                    tt(hT_flat[:, bass.ds(c * 2 * T, 2 * T)], gate_buf[:, j % 3, :],
                       ps[:, 2 * (j % 3) + 1, :], ALU.mult).then_inc(evacuated, 1)
                    split(split_next(g.split + 4 * j), i)
                    split_hidden(g, j, i, c)

                turns = g.chunks // 3
                with dve.Fori(0, turns) as i:
                    for j in range(3):
                        chunk(j, i, 3 * i + j)
                for j in range(3 * turns, g.chunks):
                    chunk(j, 0, j)

            tails = [0]

            def taps(j, weights, c, tiles, width):
                done = {}
                for back in range(1, width):
                    for f in tiles:
                        k = CONST_AT[weights] + (c * 4 + f) * (width + 1)
                        raw = raw_buf[:, j % 3, f * T:(f + 1) * T - back]
                        acc = conv_buf[:, j % 3, f * T + back:(f + 1) * T]
                        tap = cst[:, bass.ds(k + width - 1 - back, 1)]
                        if back > 1:
                            dve.wait_ge(dve_step.sem, done[f])
                        last = stt(acc, raw, tap, acc, ALU.mult, ALU.add)
                        if back == width - 1:
                            last.then_inc(conv_tail, 1)
                        else:
                            dve_step.up(last)
                            done[f] = dve_step.value()

            def cffn(g):
                began = tails[0]

                def chunk(j, i=0, c=0):
                    ahead = split_next(g.split + 4 * j)
                    split(ahead[:2], i)
                    dve.wait_ge(evacuated, chunk_read(g, j) + 3 * i)
                    taps(j, f"conv{g.nth}", c, (2, 3), 3)
                    taps(j, f"conv{g.nth}", c, (0, 1), 3)
                    split(ahead[2:], i)
                    if j > 0:
                        split_hidden(g, j - 1, i, c - 1)
                    dve.wait_ge(gated, g.gated + j + 1 + 3 * i)
                    dve.wait_ge(conv_tail, began + 4 * j + 4 + 12 * i)
                    tt(hT_flat[:, bass.ds(c * 2 * T, 2 * T)], conv_buf[:, j % 3, 0:2 * T],
                       conv_buf[:, j % 3, 2 * T:4 * T], ALU.mult).then_inc(hidden, 1)

                chunk(0)
                turns = (g.chunks - 1) // 3
                with rounds(dve, turns, (dve_step, 12)) as i:
                    for j in range(1, 4):
                        chunk(j, i, 3 * i + j)
                for j in range(1 + 3 * turns, g.chunks):
                    chunk(j, 0, j)
                split_hidden(g, g.chunks - 1, 0, g.chunks - 1)
                tails[0] += 4 * g.chunks

            def conv_chunks(g, weights):
                with rounds(dve, 2, (dve_step, 24)) as i:
                    for j in range(3):
                        ahead = split_next(g.split + 4 * j)
                        split(ahead[:2], i)
                        dve.wait_ge(evacuated, chunk_read(g, j) + 3 * i)
                        taps(j, weights, 3 * i + j, (0, 1, 2, 3), 4)
                        split(ahead[2:], i)
                tails[0] += 24

            def gdn(g):
                conv_chunks(g, "gdn_conv")
                for c in range(6, g.chunks):
                    split(split_next(g.split + 4 * c))
                dve.wait_ge(ba_done, 1)
                a_dt = heads("a_dt", 8).unsqueeze(1).to_broadcast([P, NT, 8])
                u, arg = gd_u[:, :, 0:8], gd_arg[:, :, 0:8]
                chain(nc.vector.tensor_copy(gd_ba[:, :, :].rearrange("p t n -> p (t n)"), ps[:, 6, 0:32]))
                chain(tt(u, gd_ba[:, :, 8:16], a_dt, ALU.add))
                chain(ts(arg, u, -1.0, None, ALU.mult))
                tt(arg, arg, u, ALU.min).then_inc(g_arg, 1)
                dve.wait_ge(g_log, 1)
                chain(stt(u, u, 0.0, arg, ALU.max, ALU.add))
                chain(ts(gd_beta[:, :, 0:8], gd_ba[:, :, 0:8], 1.0, None, ALU.add))
                chain(nc.vector.reciprocal(gd_beta[:, :, 0:8], gd_beta[:, :, 0:8]))
                rate = gd_rate.unsqueeze(1).to_broadcast([P, NT, 8])
                stt(gd_g[:, :, 0:8], u, -1.0, rate, ALU.mult, ALU.mult).then_inc(g_ready, 1)
                dve.wait_ge(g_cums_done, 1)
                chain(nc.vector.tensor_copy(gd_gc[:, :, 0:8], ps[:, 7, 0:16].rearrange("p (t h) -> p t h", t=NT)))
                tt(gd_kdec, ps[:, 7, 16:24], gd_gc[:, 0, 0:8], ALU.subtract).then_inc(g_cums_ready, 1)
                for n in range(8):
                    dve.wait_ge(q_inverse, n + 1)
                    v = gd_in[:, 2 * n:2 * n + 2, :].rearrange("p f t -> p (f t)")
                    stt(v, v, P ** -0.5 if n < 4 else 1.0, gd_norm[:, n, :], ALU.mult, ALU.mult).then_inc(q_normed, 1)

                def exponents(i):
                    t, h = i // 2, i % 2 * 4
                    dve.wait_ge(g_rows_done, i + 1)
                    for r in range(4):
                        last = ts(gd_off[:, i, r * P:(r + 1) * P], ps[:, i % 2, r * P:(r + 1) * P],
                                  gd_gc[:, t, h + r:h + r + 1], 0.0, ALU.subtract, ALU.min)
                    last.then_inc(g_diff, 1)
                    tokens = slice(t * P, (t + 1) * P)
                    tt(gd_kb[:, h:h + 4, tokens], gd_in[:, G_K + h:G_K + h + 4, tokens],
                       ps[:, 2 + i % 2, :].rearrange("p (r n) -> p r n", r=4), ALU.mult).then_inc(kb_ready, 1)

                def attention_of(i):
                    t, h = i // 2, i % 2 * 4
                    dve.wait_ge(g_decay, i + 1)
                    decay = gd_off[:, i, :].rearrange("p (r n) -> p r n", r=4)
                    chain(tt(decay, decay, const("upper").unsqueeze(1).to_broadcast([P, 4, P]), ALU.mult))
                    dve.wait_ge(kq_done, i + 1)
                    dve_step.up(tt(gd_LT[:, i, :], ps[:, 4, :], gd_off[:, i, :], ALU.mult))
                    tt(gd_attT[:, t, h * P:(h + 4) * P], ps[:, 5, :], gd_off[:, i, :], ALU.mult)\
                        .then_inc(att_ready, 1)

                def by_token(i):
                    dve.wait_ge(v_turned, i + 1)
                    t, h = i // 2, i % 2 * 4
                    if i < 4:
                        to, factor = gd_vb[:, 8 * t + h:8 * t + h + 4, :], gd_beta[:, t, h:h + 4]
                    else:
                        if i == 4:
                            dve.wait_ge(kdec_ready, 1)
                        h = (i - 4) * 4
                        to, factor = gd_kd[:, h:h + 4, :], gd_kdec[:, h:h + 4]
                    tt(to, ps[:, 6, :].rearrange("p (r n) -> p r n", r=4),
                       factor.unsqueeze(2).to_broadcast([P, 4, P]), ALU.mult).then_inc(v_ready, 1)

                dve.wait_ge(q_normed, 8)
                exponents(0)
                exponents(1)
                for i in range(4):
                    by_token(i)
                    attention_of(i)
                    if i < 2:
                        exponents(i + 2)
                by_token(4)
                by_token(5)
                eye = ident.unsqueeze(1).to_broadcast([P, 4, P])
                for i in range(4):
                    off, inv, invT = (v[:, i, :].rearrange("p (r n) -> p r n", r=4)
                                      for v in (gd_off, gd_inv, gd_invT))
                    dve.wait_ge(off_ready, i + 1)
                    tt(invT, eye, off, ALU.subtract).then_inc(invT_ready, 1)
                    dve.wait_ge(off_used, i + 1)
                    tt(inv, eye, ps[:, i % 2, :].rearrange("p (r n) -> p r n", r=4),
                       ALU.subtract).then_inc(inv_ready, 1)
                for half in range(2):
                    h = half * 4
                    growth = gd_grow[:, h:h + 4, :]
                    query, key = gd_in[:, G_Q + h:G_Q + h + 4, P:T], gd_kb[:, h:h + 4, P:T]
                    dve_step.up(tt(query, query, growth, ALU.mult))
                    tt(key, key, growth, ALU.mult).then_inc(grown_ready, 1)
                def joined(level, last_level=False):
                    for i in range(4):
                        dve.wait_ge(inv_terms, (level - 1) * 4 + i + 1)
                        if not last_level:
                            tt(gd_inv[:, i, :], gd_inv[:, i, :], ps[:, 2 + i % 2, :],
                               ALU.subtract).then_inc(inv_ready, 1)
                        tt(gd_invT[:, i, :], gd_invT[:, i, :], ps[:, 4 + i % 2, :],
                           ALU.subtract).then_inc(invT_ready, 1)

                with dve.Fori(1, LEVELS - 1) as level:
                    joined(level)
                joined(LEVELS - 1, last_level=True)
                for half in range(2):
                    dve.wait_ge(carried_done, half + 1)
                    tt(gd_rhs[:, half * 4:half * 4 + 4, :], gd_vb[:, 8 + half * 4:12 + half * 4, :],
                       ps[:, 4 + half, :].rearrange("p (r n) -> p r n", r=4), ALU.subtract).then_inc(rhs_ready, 1)
                for n in range(4):
                    dve.wait_ge(o_squared, n + 1)
                    dve_step.up(stt(hT_flat[:, 2 * n * T:(2 * n + 2) * T], ps[:, (6, 7, 2, 3)[n], :], const("gdn_gain"),
                                    gd_z[:, 2 * n:2 * n + 2, :].rearrange("p f t -> p (f t)"), ALU.mult, ALU.mult))
                dve_step.wait(dve)

                def finish(n):
                    dve.wait_ge(o_inverse, n + 1)
                    o = hT_flat[:, 2 * n * T:(2 * n + 2) * T]
                    tt(o, o, gd_onorm[:, n, :], ALU.mult).then_inc(mixed, 1)

                return finish

            def chain(instruction):
                dve_step.up(instruction)
                dve_step.wait(dve)

            def attend(a, g, compressed=None):
                def maxima(j):
                    n, b = a.jobs[j]
                    group, qb = a.quads[n]
                    keys = (qb + 1) * P
                    if j >= 4:
                        dve.wait_ge(a.turned, a.turns.index(a.jobs[j - 4]) + 1)
                    dve.wait_ge(a.scored, j + 1)
                    mask = const(a.mask, 2 * P - keys, 2 * P).unsqueeze(1).to_broadcast([P, 4, keys])
                    tt(a.prob(j), a.scores(j), mask, ALU.add).then_inc(a.masked, 1)
                    dve.wait_ge(a.masked, j + 1)
                    m = max_buf[:, j, :]
                    chain(nc.vector.tensor_reduce(m, a.prob(j), AX.X, ALU.max))
                    if a.kind == "swa":
                        sinks = heads("sinks", 16)[:, 4 * group:4 * group + 4]
                        chain(stt(m, m, SCALE, sinks, ALU.mult, ALU.max))
                        chain(ts(m, m, -1.0, None, ALU.mult))
                        tt(sink_buf[:, j, :], sinks, m, ALU.add).then_inc(a.maxed, 1)
                    else:
                        ts(m, m, -SCALE, None, ALU.mult).then_inc(a.maxed, 1)

                def normalise(j):
                    n, b = a.jobs[j]
                    group, qb = a.quads[n]
                    keys = (qb + 1) * P
                    dve.wait_ge(a.exped, j + 1)
                    inv = inv_buf[:, j, :]
                    if a.kind == "swa":
                        chain(tt(sum_buf[:, j, :], sum_buf[:, j, :], sink_buf[:, j, :], ALU.add))
                    chain(nc.vector.reciprocal(inv, sum_buf[:, j, :]))
                    if a.kind == "nsa":
                        at = group * 4 * 3 + 1 + b
                        chain(tt(inv, inv, gates_buf[:, qb, at:at + 10:3], ALU.mult))
                    tt(a.prob(j), a.prob(j), inv.unsqueeze(2).to_broadcast([P, 4, keys]),
                       ALU.mult).then_inc(a.probs, 1)

                maxima(0)
                maxima(1)
                if compressed:
                    normalise(0)
                    normalise(1)
                    compressed()
                for j in range(len(a.jobs)):
                    if not (compressed and j < 2):
                        normalise(j)
                    if j + 2 < len(a.jobs):
                        maxima(j + 2)

            def swa(g):
                for c in range(g.chunks):
                    split(split_next(g.split + 4 * c))
                attend(attention["swa"], g)

            def nsa(g):
                for c in range(g.chunks):
                    split(split_next(g.split + 4 * c))
                dve.wait_ge(pairs_landed, 16 * 8)
                for kv in range(2):
                    for m in range(16):
                        last = ts(cmp_in[:, kv, m, :].rearrange("p (v c) -> p v c", v=GROUPS),
                                  token_pairs[:, kv, :, m:m + 8 * (NC - 1) + 1:8],
                                  const("pos", kv * 16 + m, kv * 16 + m + 1), None, ALU.add)
                    last.then_inc(cmp_in_ready, 1)
                keep = const("cmp_keep").rearrange("p (t c) -> p t c", t=NT)
                chain(ts(cmp_drop, keep, 1.0, -MASKED, ALU.subtract, ALU.mult))
                dve.wait_ge(gates_ready, 1)

                def compressed():
                    dve.wait_ge(unit_done, units_until(g.extra + 1))
                    h, s, u = (cmp_hidden[0:NG, n, :] for n in (1, 3, 2))
                    chain(nc.vector.tensor_copy(h.rearrange("p (v n) -> p v n", v=2), ps[0:NG, 4:6, 0:2 * P]))
                    chain(tt(s, h, h, ALU.mult))
                    chain(ts(s, s, 0.044715, 1.0, ALU.mult, ALU.add))
                    tt(u, s, h, ALU.mult).then_inc(tanh_in, 1)
                    dve.wait_ge(tanh_done, 1)
                    chain(ts(u, u, 1.0, 0.5, ALU.add, ALU.mult))
                    tt(cmp_hidden[0:NG, 0, :], u, h, ALU.mult).then_inc(gelu_done, 1)
                    dve.wait_ge(cmp_scored, 1)
                    for t in range(NT):
                        p = cmp_prob[:, t, :, 0:NC]
                        drop = cmp_drop[:, t, 0:NC].unsqueeze(1).to_broadcast([P, 16, NC])
                        m = cmp_max[:, t, :]
                        mask = keep[:, t, 0:NC].unsqueeze(1).unsqueeze(1).to_broadcast([P, 2, 4, NC])
                        by_half = cmp_prob[:, t, :, :].rearrange("p (a e r) c -> p e a r c", a=2, e=2)
                        for e in range(2):
                            scored = ps[:, 6 + e, t * 128:(t + 1) * 128].rearrange("p (a r c) -> p a r c", a=2, r=4)
                            dve_step.up(tt(by_half[:, e, :, :, 0:NC], scored[:, :, :, 0:NC], mask, ALU.mult))
                        dve_step.wait(dve)
                        chain(tt(p, p, drop, ALU.add))
                        chain(nc.vector.tensor_reduce(m, p, AX.X, ALU.max))
                        tt(p, p, m.unsqueeze(2).to_broadcast([P, 16, NC]), ALU.subtract).then_inc(cmp_centered, 1)
                    for t in range(NT):
                        p = cmp_prob[:, t, :, 0:NC]
                        mask = keep[:, t, 0:NC].unsqueeze(1).to_broadcast([P, 16, NC])
                        total = cmp_sum[:, t, :]
                        dve.wait_ge(cmp_exped, t + 1)
                        chain(nc.vector.tensor_reduce(total, p, AX.X, ALU.add))
                        chain(nc.vector.reciprocal(total, total))
                        chain(tt(total, total, gates_buf[:, t, 0:46:3], ALU.mult))
                        chain(tt(p, p, mask, ALU.mult))
                        tt(p, p, total.unsqueeze(2).to_broadcast([P, 16, NC]), ALU.mult).then_inc(cmp_ready, 1)

                attend(attention["nsa"], g, compressed)

            def ssd(g):
                conv_chunks(g, "ssd_conv")
                for c in range(6, g.chunks):
                    split(split_next(g.split + 4 * c))
                dve.wait_ge(dt_done, 1)
                bias = heads("ssd_dt", 32).unsqueeze(1).to_broadcast([P, NT, 32])
                u, e, dt, dta = (v.rearrange("p (t h) -> p t h", t=NT) for v in (ssd_u, ssd_e, ssd_dt, ssd_dta))
                chain(tt(u, ps[:, 6, 0:64].rearrange("p (t h) -> p t h", t=NT), bias, ALU.add))
                chain(ts(ssd_misc, ssd_u, -1.0, None, ALU.mult))
                tt(ssd_e, ssd_u, ssd_misc, ALU.min).then_inc(dt_arg, 1)
                dve.wait_ge(dt_log, 1)
                chain(stt(ssd_dt, ssd_u, 0.0, ssd_e, ALU.max, ALU.add))
                rate = ssd_ea.unsqueeze(1).to_broadcast([P, NT, 32])
                stt(dta, dt, -1.0, rate, ALU.mult, ALU.mult).then_inc(dta_ready, 1)

                def times_dt(m):
                    t, gg = m // 4, m % 4
                    dve.wait_ge(x_turned, m + 1)
                    by_head = dt[:, t, 8 * gg:8 * gg + 8].unsqueeze(2).to_broadcast([P, 8, HD])
                    tt(xdt_parts[t][gg].rearrange("p (h d) -> p h d", h=8),
                       ps[:, 2 + m % 2, :].rearrange("p (h d) -> p h d", h=8), by_head,
                       ALU.mult).then_inc(xdt_ready, 1)

                times_dt(0)
                times_dt(1)
                dve.wait_ge(cums_done, 1)
                chain(nc.vector.tensor_copy(ssd_acs, ps[:, 7, 0:64]))
                tt(ssd_dec, ps[:, 7, 64:96], ssd_acs[:, 0:32], ALU.subtract).then_inc(cums_ready, 1)
                times_dt(2)
                times_dt(3)
                for t in range(NT):
                    dve.wait_ge(cb_done, t + 1)
                    tt(ssd_cb[:, 4 * t:4 * t + 4, :], ps[:, t, :].rearrange("p (g n) -> p g n", g=4),
                       const("upper").unsqueeze(1).to_broadcast([P, 4, P]), ALU.mult).then_inc(cb_ready, 1)
                dve.wait_ge(cums_exp, 1)
                dve.wait_ge(xdt_ready, 4)
                for gg in range(4):
                    by_head = ssd_dec[:, 8 * gg:8 * gg + 8].unsqueeze(2).to_broadcast([P, 8, HD])
                    tt(ssd_xdec[:, gg * 512:(gg + 1) * 512].rearrange("p (h d) -> p h d", h=8),
                       xdt_parts[0][gg].rearrange("p (h d) -> p h d", h=8), by_head,
                       ALU.mult).then_inc(xdec_ready, 1)
                for m in range(4, 8):
                    times_dt(m)

                def exponents(k):
                    t, h = k // 8, k % 8 * 4
                    dve.wait_ge(rows_done, k + 1)
                    if k >= 4:
                        dve.wait_ge(y_half, k - 3)
                    for r in range(4):
                        column = ssd_acs[:, t * 32 + h + r:t * 32 + h + r + 1]
                        last = ts(ssd_w[:, k % 4, r * P:(r + 1) * P], ps[:, k % 2, r * P:(r + 1) * P], column, 0.0,
                                  ALU.subtract, ALU.min)
                    last.then_inc(diff_ready, 1)

                def weights(k):
                    t, gg = k // 8, k % 8 // 2
                    dve.wait_ge(decay_ready, k + 1)
                    w = ssd_w[:, k % 4, :].rearrange("p (r n) -> p r n", r=4)
                    tt(w, w, ssd_cb[:, 4 * t + gg, :].unsqueeze(1).to_broadcast([P, 4, P]),
                       ALU.mult).then_inc(w_ready, 1)

                def outputs(m):
                    t, gg = m // 4, m % 4
                    y = ssd_y[:, m % 2, :]
                    if m >= 2:
                        dve.wait_ge(y_turned, m - 1)
                    dve.wait_ge(y_half, 2 * m + 2)
                    if t == 0:
                        nc.vector.tensor_copy(y, ps[:, 2 + m % 2, :]).then_inc(y_out, 1)
                        return
                    dve.wait_ge(y_done, m - 3)
                    grown = ssd_misc[:, 8 * gg:8 * gg + 8].unsqueeze(2).to_broadcast([P, 8, HD])
                    chain(tt(y.rearrange("p (h d) -> p h d", h=8), ps[:, 4, :].rearrange("p (h d) -> p h d", h=8),
                             grown, ALU.mult))
                    tt(y, y, ps[:, 2 + m % 2, :], ALU.add).then_inc(y_out, 1)

                def gate(m):
                    t, gg = m // 4, m % 4
                    tokens = slice(t * P, (t + 1) * P)
                    dve.wait_ge(y_turned, m + 1)
                    for f in range(4):
                        last = stt(hT[:, 4 * gg + f, tokens], ssd_in[:, S_X + 4 * gg + f, tokens],
                                   const("ssd_skip", 4 * gg + f, 4 * gg + f + 1), ps[:, 5, f * P:(f + 1) * P],
                                   ALU.mult, ALU.add)
                    last.then_inc(y_turned_out, 1)
                    dve.wait_ge(y_turned_out, m + 1)
                    y = hT[:, 4 * gg:4 * gg + 4, tokens]
                    tt(y, y, ssd_z[:, 4 * gg:4 * gg + 4, tokens], ALU.mult).then_inc(y_gated, 1)

                dve.wait_ge(evacuated, chunk_read(g, g.chunks - 1))
                exponents(0)
                exponents(1)
                for k in range(16):
                    weights(k)
                    if k + 2 < 16:
                        exponents(k + 2)
                    if k % 2 == 1:
                        if k >= 3:
                            outputs(k // 2 - 1)
                        if k >= 5:
                            gate(k // 2 - 2)
                gate(6)
                outputs(7)
                gate(7)

                def finish(n):
                    gg = n // 2
                    dve.wait_ge(y_inverse, gg + 1)
                    for f in (2 * n, 2 * n + 1):
                        stt(hT[:, f, :], hT[:, f, :], const("ssd_gain", f, f + 1), ssd_inverse[:, gg, :],
                            ALU.mult, ALU.mult).then_inc(mixed, 1)

                return finish

            dve_mixer = {"gdn": gdn, "swa": swa, "nsa": nsa, "ssd": ssd}

            def residual(g, t):
                if t == 0:
                    dve.wait_ge(first_rows_done, g.s + 1)
                else:
                    dve.wait_ge(unit_done, units_until(g.down + g.down_units - 1))
                product = ps_flat[:, (4 + 2 * t) * BANK:(6 + 2 * t) * BANK]
                event = ("residual", g.s)
                if g.kind in ("nsa", "cffn", "ssd"):
                    column = rstd(("post", g.s, t))
                    n = row_at[event]
                    dve.wait_ge(row_landed[n % 2], 16 * (n // 2 + 1))
                    dve_step.up(stt(xn[:, t, :], product, column, row[:, n % 2, :], ALU.mult, ALU.mult))
                    dve_step.wait(dve)
                    tt(x[:, t, :], x[:, t, :], xn[:, t, :], ALU.add).then_inc(x_ready, 1)
                elif g.kind == "swiglu":
                    stt(x[:, t, :], product, 0.5, x[:, t, :], ALU.mult, ALU.add).then_inc(x_ready, 1)
                else:
                    tt(x[:, t, :], product, x[:, t, :], ALU.add).then_inc(x_ready, 1)

            def output_bias(g):
                n = row_at[("residual", g.s)]
                dve.wait_ge(row_landed[n % 2], 16 * (n // 2 + 1))
                for t in range(NT):
                    dve_step.up(tt(x[:, t, :], x[:, t, :], row[:, n % 2, :], ALU.add))
                dve_step.wait(dve)

            dve.wait_ge(early_loaded, 16)
            dve.wait_ge(x_loaded, 16 * NT)
            for t in range(NT):
                norm(0, t)
            for g in stages:
                first = split_first(g.split) if g.s == 0 or g.own_ring else []
                split(first[:1])
                turned_out(g)
                split(first[1:] if first else split_next(g.split - 4))
                if g.s == 0:
                    dve.wait_ge(cst_loaded, 16)
                if g.kind == "swiglu":
                    swiglu(g)
                elif g.kind == "cffn":
                    cffn(g)
                else:
                    if g.kind in narrow_width:
                        n = KD * narrow_width[g.kind]
                        dve.wait_ge(narrow_rounding, narrow_counts[g.s])
                        tt(r32(narrow_rest[:, 0:n]), const(narrow_const[g.kind]), narrow_rounded[:, 0:n],
                           ALU.subtract).then_inc(narrow_split, 1)
                    finish = dve_mixer[g.kind](g)
                    if g.kind == "swa":
                        output_bias(g)
                    split_mixed(g, finish)
                for v in range(g.down_units - 1):
                    split(split_next(g.split_down + 4 * v))
                for t in range(NT):
                    residual(g, t)
                    if g.norm == FINAL_AFTER:
                        column = rstd(("final", g.s, t))
                        n = row_at[("final", g.s)]
                        dve.wait_ge(row_landed[n % 2], 16 * (n // 2 + 1))
                        stt(x[:, t, :], x[:, t, :], column, row[:, n % 2, :],
                            ALU.mult, ALU.mult).then_inc(x_ready, 1)
                    if g.s < last_stage:
                        norm(g.s + 1, t)

        @block.gpsimd
        def _(pool):
            def load_row(n):
                r, _ = row_uses[n]
                if n >= 2:
                    pool.wait_ge(x_ready, x_after[row_uses[n - 2][1], NT - 1])
                pool.dma_start(row[:, n % 2, :], rows[r:r + 1, :].to_broadcast([P, D]))\
                    .then_inc(row_landed[n % 2], 16)

            def gdn(g):
                masks = CONST_AT["levels"]
                for level in range(LEVELS):
                    masks = CONST_AT["levels"] + level * P
                    mask = cst[:, masks:masks + P].unsqueeze(1).to_broadcast([P, 4, P])
                    for i in range(4):
                        if level == 0:
                            pool.wait_ge(att_ready, i + 1)
                        else:
                            pool.wait_ge(off_used, (level - 1) * 4 + i + 1)
                            pool.wait_ge(invT_ready, i + 1)
                        v, off = (b[:, i, :].rearrange("p (r n) -> p r n", r=4) for b in (gd_LT, gd_off))
                        nc.gpsimd.tensor_tensor(off, v, mask, ALU.mult).then_inc(off_ready, 1)

            def nsa(g):
                pool.wait_ge(evacuated, chunk_read(g, 2))
                for kv in range(2):
                    for half in range(2):
                        for parity in range(2):
                            pool.dma_start(token_pairs[parity * HD:(parity + 1) * HD, kv, half:half + 3:2, :],
                                           mix_tiles[half * HD:(half + 1) * HD, 8 + 2 * kv:10 + 2 * kv,
                                                     parity * P:(parity + 1) * P]).then_inc(pairs_landed, 16)

            pool_mixer = {"gdn": gdn, "nsa": nsa}

            for n in range(min(2, len(row_uses))):
                load_row(n)
            loaded = min(2, len(row_uses))
            for g in stages:
                if g.kind in pool_mixer:
                    pool_mixer[g.kind](g)
                while loaded < len(row_uses) and row_uses[loaded - 2][1][1] <= g.s:
                    load_row(loaded)
                    loaded += 1


def column_tiles(v):
    return v.reshape(-1, P).T


def up_units(w, columns):
    w = w[:, columns]
    n = w.shape[1] // 512
    return w.reshape(KD, P, n, 4, P).transpose(2, 1, 3, 0, 4).reshape(n, P, UNIT)


def down_units(w):
    kts = w.shape[0] // P
    n = -(-kts // 4)
    padded = np.zeros((4 * n, P, D), w.dtype)
    padded[:kts] = w.reshape(kts, P, D)
    return padded.reshape(n, 4, P, D).transpose(0, 2, 1, 3).reshape(n, P, UNIT)


def paired(n_tiles=FK):
    return np.arange(2 * FF).reshape(2, FF // 256, 256).transpose(1, 0, 2).ravel()


def head_order():
    return np.arange(16 * HD).reshape(2, 2, 4, HD).transpose(0, 2, 1, 3).ravel()


def weights_of(a, kind, nth):
    if kind == "swiglu":
        which, layer = ("ffn1", "ffn2")[nth % 2], nth // 2
        yield up_units(a[which + "_w_gu"][layer], paired())
        yield down_units(a[which + "_w_down"][layer])
    elif kind == "cffn":
        yield up_units(a["ffn_w_up_2"][nth], paired())
        yield down_units(a["ffn_w_down_2"][nth])
    elif kind == "gdn":
        yield up_units(a["a_w_in"][0], np.arange(4096))
        yield down_units(a["a_w_out"][0])
    elif kind == "swa":
        yield up_units(a["b_w_in"][0], np.concatenate([head_order(), np.arange(1024, 1536)]))
        yield down_units(a["b_w_out"][0][head_order()])
    elif kind == "nsa":
        yield up_units(a["nsa_w_in_2"][0], np.concatenate([head_order(), np.arange(1024, 2560)]))
        yield a["nsa_cmp_w1_2"][0].reshape(2, 16, P, 256).transpose(0, 2, 1, 3).reshape(2, P, UNIT)
        yield down_units(a["nsa_w_out_2"][0][head_order()])
    elif kind == "ssd":
        yield up_units(a["ssd_w_in_2"][0], np.concatenate([np.arange(2048, 5120), np.arange(2048)]))
        yield down_units(a["ssd_w_out_2"][0])


def const_parts(a):
    key, query = np.arange(P)[:, None], np.arange(P)[None, :]
    f = np.float32
    zeros = np.zeros
    c = {"ident": (key == query).astype(f), "ones": np.ones((P, P), f), "upper": (key <= query).astype(f)}
    norms = [a["ffn1_norm"][0], a["mix_norm"][0], a["ffn2_norm"][0], a["ffn1_norm"][1], a["mix_norm"][1],
             a["ffn2_norm"][1]] + [a["norm_gains_2"][i][n] for i in range(2) for n in (0, 2)]
    c["norms"] = np.concatenate([column_tiles(v) for v in norms], 1)
    over_heads = np.concatenate([a["a_A_log"][0], a["a_dt_bias"][0], a["b_sinks"][0], a["ssd_dt_bias_2"][0],
                                 a["ssd_a_log_2"][0]])
    c["heads"] = np.broadcast_to(over_heads, (P, 96))

    def conv(w, b, order):
        wb = np.concatenate([w, b[None]])[:, order]
        return wb.reshape(len(wb), -1, P).transpose(2, 1, 0).reshape(P, -1)

    c["gdn_conv"] = conv(a["a_w_conv"][0], zeros(3072, f), np.arange(3072))
    c["ssd_conv"] = conv(a["ssd_conv_w_2"][0], a["ssd_conv_b_2"][0], np.arange(3072))
    for n in range(2):
        c[f"conv{n}"] = conv(a["ffn_conv_w_2"][n], a["ffn_conv_b_2"][n], paired())
    c["gdn_gain"] = column_tiles(a["a_out_norm"][0])

    def narrow(w):
        return w.reshape(KD, P, -1).transpose(1, 0, 2).reshape(P, -1)

    c["w_ba"] = narrow(a["a_w_in"][0][:, 4096:])
    c["w_gates"] = narrow(a["nsa_w_in_2"][0][:, 2560:])
    c["w_dt"] = narrow(a["ssd_w_in_2"][0][:, 5120:])
    levels = []
    for n in range(LEVELS):
        half = 1 << n
        levels.append((key // (2 * half) == query // (2 * half)) & (key // half % 2 == 0) & (query // half % 2 == 1))
    c["levels"] = np.concatenate(levels, 1).astype(f)
    c["swa_bias"] = column_tiles(a["b_b_in"][0][np.concatenate([head_order(), np.arange(1024, 1536)])])
    q, k = np.arange(P)[:, None], np.arange(P)[None, :]
    c["window"] = np.where(np.concatenate([k > q, k <= q], 1), 0.0, MASKED).astype(f)
    c["causal"] = np.where(np.concatenate([k > -1 + 0 * q, k <= q], 1), 0.0, MASKED).astype(f)
    keep = np.zeros((P, NT, 16), f)
    for t in range(NT):
        keep[:, t, :NC] = np.arange(NC)[None] * 16 + 31 <= t * P + np.arange(P)[:, None]
    c["cmp_keep"] = keep.reshape(P, -1)
    c["pos"] = a["nsa_cmp_pos_2"][0].reshape(2, 16, P).transpose(2, 0, 1).reshape(P, -1)
    w2 = a["nsa_cmp_w2_2"][0].reshape(2, 2, P, HD)
    c["w_cmp2"] = np.concatenate([w2, w2], 3).transpose(2, 0, 1, 3).reshape(P, -1)
    c["ssd_gain"] = column_tiles(a["ssd_norm_w_2"][0])
    c["ssd_skip"] = column_tiles(np.repeat(a["ssd_d_2"][0], HD))
    return c


def prepare(a, plan=PLAN):
    units = np.concatenate([u for kind, nth in plan for u in weights_of(a, kind, nth)])
    parts = const_parts(a)
    consts = np.concatenate([parts[name] for name, _ in CONST], 1)
    rows = np.stack([a["b_b_out"][0], a["final_norm"], a["norm_gains_2"][0][1], a["norm_gains_2"][0][3],
                     a["norm_gains_2"][1][1], a["norm_gains_2"][1][3]])
    return {"units": units, "consts": consts, "rows": rows, "x_in": np.ascontiguousarray(a["x"][0])}


def kernel(**inputs):
    from concourse import bacc
    from concourse.bass_utils import run_bass_kernel_spmd

    arrays = prepare({name: np.asarray(v) for name, v in inputs.items()})
    nc = bacc.Bacc("TRN2", target_bir_lowering=False, num_devices=1)
    drams = {n: nc.dram_tensor(n, v.shape, mybir.dt.from_np(v.dtype), kind="ExternalInput").ap()
             for n, v in arrays.items()}
    out = nc.dram_tensor("out", (T, D), F32, kind="ExternalOutput").ap()
    build_program(nc, drams["units"], drams["consts"], drams["rows"], drams["x_in"], out, PLAN)
    result = run_bass_kernel_spmd(nc, [arrays], core_ids=[0])
    return result.results[0]["out"].reshape(1, T, D)
```
